# Optimizing a Trainium2 kernel written in Bass

```python
import math
import jax, jax.numpy as jnp
from jax import lax
import numpy as np

D_MODEL = 1024
BATCH = 1
SEQ = 256
DEPTH = 1
DEC_BATCH = 8
DEC_SEQ = 4
PAST_LEN = 256
PAGE_SIZE = 128

HEAD_DIM = 64
MIX_WIDTH = D_MODEL
SB_WIDTH = MIX_WIDTH // 2
NSA_WIDTH = MIX_WIDTH - SB_WIDTH
H_SB = SB_WIDTH // HEAD_DIM
H_NSA = NSA_WIDTH // HEAD_DIM
KV_GROUPS = 2
HPG = H_NSA // KV_GROUPS
COMP_BLOCK = 32
COMP_STRIDE = 16
COMP_HID = 128
SEL_BLOCK = 64
TOP_N = 8
WINDOW = 512
Q_BLOCK = 128
PEER_HEADS = 8
N_KEYS = 128
N_EXPERTS = N_KEYS * N_KEYS
PEER_TOPK = 16
D_KEY = 256
TOK_CHUNK = 256
ALPHA = (2.0 * DEPTH) ** 0.25
BETA = (8.0 * DEPTH) ** -0.25
LN_EPS = 1e-5
NEG = -1e30
FORCE = 1e4
SCALE = HEAD_DIM ** -0.5

OFF_SBKV = SB_WIDTH
OFF_QB = 3 * SB_WIDTH
OFF_NSAKV = OFF_QB + NSA_WIDTH
OFF_WIN = OFF_NSAKV + 4 * KV_GROUPS * HEAD_DIM
OFF_GATE = OFF_WIN + 2 * KV_GROUPS * HEAD_DIM
IN_COLS = OFF_GATE + 3 * H_NSA

kernel_name = 'hybrid_stickbreak_nsa_peer_step'

def layer_norm(x, g, b):
    xf = x.astype(jnp.float32)
    mu = xf.mean(-1, keepdims=True)
    var = jnp.square(xf - mu).mean(-1, keepdims=True)
    return ((xf - mu) * lax.rsqrt(var + LN_EPS) * g + b).astype(x.dtype)

def rms_norm(x, g):
    xf = x.astype(jnp.float32)
    return (xf * lax.rsqrt(jnp.square(xf).mean(-1, keepdims=True) + LN_EPS) * g).astype(x.dtype)

def masked_softmax(s, mask):
    s = jnp.where(mask, s, NEG)
    e = jnp.exp(s - s.max(-1, keepdims=True)) * mask
    tot = e.sum(-1, keepdims=True)
    return e / jnp.where(tot > 0, tot, 1.0)

def alibi_slopes():
    i = jnp.arange(1, H_NSA + 1, dtype=jnp.float32)
    return (2.0 ** (-8.0 * i / H_NSA)).reshape(KV_GROUPS, HPG)

def project(x, w_in):
    B, T, _ = x.shape
    z = x @ w_in
    q_a = z[..., :SB_WIDTH].reshape(B, T, H_SB, HEAD_DIM)
    sb_kv = z[..., OFF_SBKV:OFF_QB].reshape(B, T, 2, H_SB, HEAD_DIM)
    q_b = z[..., OFF_QB:OFF_NSAKV].reshape(B, T, H_NSA, HEAD_DIM)
    nsa_kv = z[..., OFF_NSAKV:OFF_WIN].reshape(B, T, 4, KV_GROUPS, HEAD_DIM)
    win_kv = z[..., OFF_WIN:OFF_GATE].reshape(B, T, 2, KV_GROUPS, HEAD_DIM)
    gates = jax.nn.sigmoid(z[..., OFF_GATE:]).reshape(B, T, H_NSA, 3)
    return q_a, sb_kv, q_b, nsa_kv, win_kv, gates

def stick_breaking(q, q_pos, k, v, k_pos):
    z = jnp.einsum('bthd,bshd->bhts', q, k).astype(jnp.float32) * SCALE
    mask = k_pos[None, :] < q_pos[:, None]
    log_keep = jnp.where(mask, jax.nn.log_sigmoid(-z), 0.0)
    cum = jnp.cumsum(log_keep, axis=-1)
    after = cum[..., -1:] - cum
    w = jnp.where(mask, jnp.exp(jax.nn.log_sigmoid(z) + after), 0.0)
    return jnp.einsum('bhts,bshd->bthd', w.astype(v.dtype), v)

def compress(kc, vc, cmp_pe, cmp_w1, cmp_w2):
    L = kc.shape[1]
    n_c = (L - COMP_BLOCK) // COMP_STRIDE + 1
    starts = jnp.arange(n_c) * COMP_STRIDE
    idx = starts[:, None] + jnp.arange(COMP_BLOCK)[None, :]

    def phi(t, j):
        blk = t[:, idx] + cmp_pe[j][None, None, :, None, :]
        hdn = jax.nn.gelu(jnp.einsum('bnlgd,ldh->bngh', blk, cmp_w1[j]))
        return jnp.einsum('bngh,hd->bngd', hdn, cmp_w2[j])

    ck = phi(kc, 0)
    cv = phi(vc, 1)
    c_pos = starts + COMP_BLOCK - 1
    n_sel = -(-L // SEL_BLOCK)
    sel_map = jax.nn.one_hot(starts // SEL_BLOCK, n_sel, dtype=jnp.float32)
    return ck, cv, c_pos, sel_map

def sel_prep(k, n_sel):
    pad = n_sel * SEL_BLOCK - k.shape[1]
    return jnp.pad(k, ((0, 0), (0, pad), (0, 0), (0, 0))).transpose(0, 2, 1, 3)

def gather_rows(a, idx):
    return jax.vmap(jax.vmap(lambda r, i: r[i]))(a, idx)

def nsa_attend(q, q_pos, gates, ck, cv, c_pos, sel_map, sk, sv, wk, wv, w_pos):
    B, Tq = q.shape[:2]
    qg = q.reshape(B, Tq, KV_GROUPS, HPG, HEAD_DIM)
    slopes = alibi_slopes()[None, :, :, None, None]
    qp = q_pos.astype(jnp.float32)
    s = jnp.einsum('btgrd,bngd->bgrtn', qg, ck).astype(jnp.float32) * SCALE
    s = s - slopes * (qp[:, None] - c_pos[None, :].astype(jnp.float32))
    p_c = masked_softmax(s, c_pos[None, :] <= q_pos[:, None])
    o_c = jnp.einsum('bgrtn,bngd->btgrd', p_c.astype(cv.dtype), cv)
    imp = jnp.einsum('bgrtn,nj->bgtj', p_c, sel_map)
    n_sel = sel_map.shape[1]
    blk = jnp.arange(n_sel)
    valid = blk[None, :] * SEL_BLOCK <= q_pos[:, None]
    forced = (blk[None, :] == (q_pos // SEL_BLOCK)[:, None]) | (blk[None, :] == 0)
    imp = jnp.where(forced, FORCE, jnp.where(valid, imp, -1.0))
    n_top = min(TOP_N, n_sel)
    _, idx = lax.top_k(imp, n_top)
    kpos = (idx[..., None] * SEL_BLOCK + jnp.arange(SEL_BLOCK)).reshape(B, KV_GROUPS, Tq, n_top * SEL_BLOCK)
    flat = kpos.reshape(B, KV_GROUPS, -1)
    ksel = gather_rows(sk, flat).reshape(B, KV_GROUPS, Tq, n_top * SEL_BLOCK, HEAD_DIM)
    vsel = gather_rows(sv, flat).reshape(B, KV_GROUPS, Tq, n_top * SEL_BLOCK, HEAD_DIM)
    dist_s = (q_pos[None, None, :, None] - kpos)[:, :, None]
    s = jnp.einsum('btgrd,bgtsd->bgrts', qg, ksel).astype(jnp.float32) * SCALE
    s = s - slopes * dist_s.astype(jnp.float32)
    p_s = masked_softmax(s, dist_s >= 0)
    o_s = jnp.einsum('bgrts,bgtsd->btgrd', p_s.astype(vsel.dtype), vsel)
    dist_w = q_pos[:, None] - w_pos[None, :]
    mask_w = (dist_w >= 0) & (dist_w < WINDOW) & (w_pos[None, :] >= 0)
    s = jnp.einsum('btgrd,bsgd->bgrts', qg, wk).astype(jnp.float32) * SCALE
    s = s - slopes * dist_w.astype(jnp.float32)
    p_w = masked_softmax(s, mask_w)
    o_w = jnp.einsum('bgrts,bsgd->btgrd', p_w.astype(wv.dtype), wv)
    g = gates.reshape(B, Tq, KV_GROUPS, HPG, 3)
    o = g[..., 0:1] * o_c + g[..., 1:2] * o_s + g[..., 2:3] * o_w
    return o.reshape(B, Tq, NSA_WIDTH)

def mixer_prompt(x, w_in, cmp_pe, cmp_w1, cmp_w2):
    B, T, _ = x.shape
    q_a, sb_kv, q_b, nsa_kv, win_kv, gates = project(x, w_in)
    k_a, v_a = sb_kv[:, :, 0], sb_kv[:, :, 1]
    ck, cv, c_pos, sel_map = compress(nsa_kv[:, :, 0], nsa_kv[:, :, 1], cmp_pe, cmp_w1, cmp_w2)
    n_sel = sel_map.shape[1]
    sk = sel_prep(nsa_kv[:, :, 2], n_sel)
    sv = sel_prep(nsa_kv[:, :, 3], n_sel)
    win_pad = jnp.pad(win_kv, ((0, 0), (WINDOW, 0), (0, 0), (0, 0), (0, 0)))
    k_pos = jnp.arange(T)

    def block(qb):
        q0 = qb * Q_BLOCK
        q_pos = q0 + jnp.arange(Q_BLOCK)
        sl = lambda a: lax.dynamic_slice_in_dim(a, q0, Q_BLOCK, axis=1)
        o_a = stick_breaking(sl(q_a), q_pos, k_a, v_a, k_pos).reshape(B, Q_BLOCK, SB_WIDTH)
        w = lax.dynamic_slice_in_dim(win_pad, q0, WINDOW + Q_BLOCK, axis=1)
        w_pos = q0 - WINDOW + jnp.arange(WINDOW + Q_BLOCK)
        o_b = nsa_attend(sl(q_b), q_pos, sl(gates), ck, cv, c_pos, sel_map, sk, sv,
                         w[:, :, 0], w[:, :, 1], w_pos)
        return o_a, o_b

    o_a, o_b = lax.map(block, jnp.arange(T // Q_BLOCK))
    o_a = jnp.moveaxis(o_a, 0, 1).reshape(B, T, SB_WIDTH)
    o_b = jnp.moveaxis(o_b, 0, 1).reshape(B, T, NSA_WIDTH)
    new_win = win_kv[:, T - min(WINDOW, T):]
    return o_a, o_b, sb_kv, nsa_kv, new_win

def mixer_sample(x, cache_sb, cache_nsa, cache_win, page_table, w_in, cmp_pe, cmp_w1, cmp_w2):
    B, T, _ = x.shape
    past = page_table.shape[1] * cache_sb.shape[1]
    q_a, sb_kv, q_b, nsa_kv, win_kv, gates = project(x, w_in)
    q_pos = past + jnp.arange(T)
    k_pos = jnp.arange(past + T)
    sb_all = jnp.concatenate([cache_sb[page_table].reshape(B, past, 2, H_SB, HEAD_DIM), sb_kv], axis=1)
    o_a = stick_breaking(q_a, q_pos, sb_all[:, :, 0], sb_all[:, :, 1], k_pos).reshape(B, T, SB_WIDTH)
    nsa_all = jnp.concatenate([cache_nsa[page_table].reshape(B, past, 4, KV_GROUPS, HEAD_DIM), nsa_kv], axis=1)
    ck, cv, c_pos, sel_map = compress(nsa_all[:, :, 0], nsa_all[:, :, 1], cmp_pe, cmp_w1, cmp_w2)
    n_sel = sel_map.shape[1]
    sk = sel_prep(nsa_all[:, :, 2], n_sel)
    sv = sel_prep(nsa_all[:, :, 3], n_sel)
    wb = cache_win.shape[1]
    win_all = jnp.concatenate([cache_win, win_kv], axis=1)
    w_pos = past - wb + jnp.arange(wb + T)
    o_b = nsa_attend(q_b, q_pos, gates, ck, cv, c_pos, sel_map, sk, sv,
                     win_all[:, :, 0], win_all[:, :, 1], w_pos)
    new_win = win_all[:, T:]
    return o_a, o_b, sb_kv, nsa_kv, new_win

def peer_chunk(h, w_q, sub_keys, u_tab, v_tab):
    C = h.shape[0]
    q = (h @ w_q).reshape(C, PEER_HEADS, 2, D_KEY // 2)
    s = jnp.einsum('cphd,phkd->cphk', q, sub_keys).astype(jnp.float32)
    s1, i1 = lax.top_k(s[:, :, 0], PEER_TOPK)
    s2, i2 = lax.top_k(s[:, :, 1], PEER_TOPK)
    cand = (s1[..., :, None] + s2[..., None, :]).reshape(C, PEER_HEADS, PEER_TOPK * PEER_TOPK)
    cidx = (i1[..., :, None] * N_KEYS + i2[..., None, :]).reshape(C, PEER_HEADS, PEER_TOPK * PEER_TOPK)
    top_s, top_i = lax.top_k(cand, PEER_TOPK)
    e = jnp.take_along_axis(cidx, top_i, axis=-1)
    g = jax.nn.softmax(top_s, axis=-1)
    a = jax.nn.gelu(jnp.einsum('cpkd,cd->cpk', u_tab[e], h)).astype(jnp.float32)
    return jnp.einsum('cpk,cpkd->cd', (g * a).astype(v_tab.dtype), v_tab[e])

def peer(h, w_q, sub_keys, u_tab, v_tab):
    n = h.shape[0]
    n_chunks = -(-n // TOK_CHUNK)
    hp = jnp.pad(h, ((0, n_chunks * TOK_CHUNK - n), (0, 0))).reshape(n_chunks, TOK_CHUNK, D_MODEL)
    out = lax.map(lambda hc: peer_chunk(hc, w_q, sub_keys, u_tab, v_tab), hp)
    return out.reshape(-1, D_MODEL)[:n]

def block_out(x, o_a, o_b, mix_g, w_out, ln1_g, ln1_b, w_q, sub_keys, u_tab, v_tab, ln2_g, ln2_b):
    m = jnp.concatenate([rms_norm(o_a, mix_g[:SB_WIDTH]), rms_norm(o_b, mix_g[SB_WIDTH:])], axis=-1) @ w_out
    h = layer_norm(ALPHA * x + m, ln1_g, ln1_b)
    f = peer(h.reshape(-1, D_MODEL), w_q, sub_keys, u_tab, v_tab).reshape(h.shape)
    return layer_norm(ALPHA * h + f, ln2_g, ln2_b)

def setup_inputs(seed: int = 0) -> dict:
    key = jax.random.key(seed)
    ks = jax.random.split(key, 20)
    nrm = lambda k, shape, scale: jax.random.normal(k, shape, jnp.float32) * scale
    n_pages = PAST_LEN // PAGE_SIZE
    n_used = DEC_BATCH * n_pages
    n_pool = n_used + max(1, n_used // 4)
    win_buf = min(WINDOW, PAST_LEN)
    page_table = jax.random.permutation(ks[0], n_pool)[:n_used].reshape(DEC_BATCH, n_pages).astype(jnp.int32)
    return {
        'x_prompt': nrm(ks[1], (BATCH, SEQ, D_MODEL), 1.0),
        'x_sample': nrm(ks[2], (DEC_BATCH, DEC_SEQ, D_MODEL), 1.0),
        'cache_sb_kv': nrm(ks[3], (DEPTH, n_pool, PAGE_SIZE, 2, H_SB, HEAD_DIM), 1.0),
        'cache_nsa_kv': nrm(ks[4], (DEPTH, n_pool, PAGE_SIZE, 4, KV_GROUPS, HEAD_DIM), 1.0),
        'cache_win_kv': nrm(ks[5], (DEPTH, DEC_BATCH, win_buf, 2, KV_GROUPS, HEAD_DIM), 1.0),
        'page_table': page_table,
        'w_in': nrm(ks[6], (DEPTH, D_MODEL, IN_COLS), D_MODEL ** -0.5),
        'cmp_pe': nrm(ks[7], (DEPTH, 2, COMP_BLOCK, HEAD_DIM), 0.1),
        'cmp_w1': nrm(ks[8], (DEPTH, 2, COMP_BLOCK, HEAD_DIM, COMP_HID), (COMP_BLOCK * HEAD_DIM) ** -0.5),
        'cmp_w2': nrm(ks[9], (DEPTH, 2, COMP_HID, HEAD_DIM), COMP_HID ** -0.5),
        'mix_norm_g': 1.0 + nrm(ks[10], (DEPTH, MIX_WIDTH), 0.02),
        'w_out': nrm(ks[11], (DEPTH, MIX_WIDTH, D_MODEL), BETA * MIX_WIDTH ** -0.5),
        'ln1_g': 1.0 + nrm(ks[12], (DEPTH, D_MODEL), 0.02),
        'ln1_b': nrm(ks[13], (DEPTH, D_MODEL), 0.02),
        'peer_w_q': nrm(ks[14], (DEPTH, D_MODEL, PEER_HEADS * D_KEY), D_MODEL ** -0.5),
        'peer_sub_keys': nrm(ks[15], (DEPTH, PEER_HEADS, 2, N_KEYS, D_KEY // 2), (D_KEY // 2) ** -0.5),
        'peer_u': nrm(ks[16], (DEPTH, N_EXPERTS, D_MODEL), D_MODEL ** -0.5),
        'peer_v': nrm(ks[17], (DEPTH, N_EXPERTS, D_MODEL), BETA),
        'ln2_g': 1.0 + nrm(ks[18], (DEPTH, D_MODEL), 0.02),
        'ln2_b': nrm(ks[19], (DEPTH, D_MODEL), 0.02),
    }

def reference(x_prompt, x_sample, cache_sb_kv, cache_nsa_kv, cache_win_kv, page_table,
              w_in, cmp_pe, cmp_w1, cmp_w2, mix_norm_g, w_out, ln1_g, ln1_b,
              peer_w_q, peer_sub_keys, peer_u, peer_v, ln2_g, ln2_b):
    h_p, h_s = x_prompt, x_sample
    sb_p_l, nsa_p_l, win_p_l, sb_s_l, nsa_s_l, win_s_l = [], [], [], [], [], []
    for l in range(DEPTH):
        o_a, o_b, sb_p, nsa_p, win_p = mixer_prompt(h_p, w_in[l], cmp_pe[l], cmp_w1[l], cmp_w2[l])
        h_p = block_out(h_p, o_a, o_b, mix_norm_g[l], w_out[l], ln1_g[l], ln1_b[l],
                        peer_w_q[l], peer_sub_keys[l], peer_u[l], peer_v[l], ln2_g[l], ln2_b[l])
        o_a, o_b, sb_s, nsa_s, win_s = mixer_sample(h_s, cache_sb_kv[l], cache_nsa_kv[l], cache_win_kv[l],
                                                    page_table, w_in[l], cmp_pe[l], cmp_w1[l], cmp_w2[l])
        h_s = block_out(h_s, o_a, o_b, mix_norm_g[l], w_out[l], ln1_g[l], ln1_b[l],
                        peer_w_q[l], peer_sub_keys[l], peer_u[l], peer_v[l], ln2_g[l], ln2_b[l])
        sb_p_l.append(sb_p); nsa_p_l.append(nsa_p); win_p_l.append(win_p)
        sb_s_l.append(sb_s); nsa_s_l.append(nsa_s); win_s_l.append(win_s)
    sb_kv_prompt = jnp.stack(sb_p_l)
    nsa_kv_prompt = jnp.stack(nsa_p_l)
    win_kv_prompt = jnp.stack(win_p_l)
    sb_kv_sample = jnp.stack(sb_s_l)
    nsa_kv_sample = jnp.stack(nsa_s_l)
    win_kv_sample = jnp.stack(win_s_l)
    return (h_p, h_s, sb_kv_prompt, nsa_kv_prompt, win_kv_prompt, sb_kv_sample, nsa_kv_sample, win_kv_sample)


_drawn_inputs = setup_inputs


def setup_inputs(seed=0):
    import zlib

    import numpy as np

    out = dict(_drawn_inputs(seed))
    spreads = {}
    factors = {}
    for name, (base, spread) in spreads.items():
        noise = np.random.default_rng([zlib.crc32(name.encode()), seed]).standard_normal(out[name].shape)
        drawn = base * np.exp(spread * noise) if base else spread * noise
        out[name] = __import__('jax').numpy.asarray(drawn.astype(out[name].dtype))
    for name, factor in factors.items():
        out[name] = (out[name] * factor).astype(out[name].dtype)
    return out
```

```python
from contextlib import ExitStack

import numpy as np

import concourse.bass as bass
from concourse import mybir

F32 = mybir.dt.float32
I32 = mybir.dt.int32
U32 = mybir.dt.uint32
ALU = mybir.AluOpType
ACT = mybir.ActivationFunctionType
AX = mybir.AxisListType.X

D = 1024
KD = D // 128
TP = 256
NB = 8
TS = 4
T = TP + NB * TS
TOK = [(0, 128), (128, 128), (256, 32)]
PAST = 256
PAGES = NB * 2
HD = 64
SCALE = HD ** -0.5
ALPHA = 2.0 ** 0.25
EPS = 1e-5
BIG = 1e30
NC_ = 15
NSEQ = 1 + NB
ZT = 23
KA, VA, QB, CK, SK, SV, WK, WV, GT = 4, 8, 12, 16, 18, 19, 20, 21, 22
NE = 128
TOPK = 16
ROWLEN = [TOPK // (i + 1) for i in range(TOPK)]
ROWOFF = [sum(ROWLEN[:i]) for i in range(TOPK)]
NCAND = sum(ROWLEN)
SLOPES = [2.0 ** (-(h + 1)) for h in range(8)]



def constants():
    c = {}
    s = np.arange(128)[:, None]
    t = np.arange(128)[None, :]
    c["ident"] = (s == t) * 1.0
    c["negtri"] = (s >= t) * -1.0
    c["negones"] = -np.ones((128, 128))
    c["ones"] = np.ones((128, 128))
    c["keep"] = (s < t) * 1.0
    c["block"] = np.where(s < t, 0.0, -BIG)
    q, k = s, t
    dist = lambda q, k: np.where(k <= q, -(q - k) * 1.0, -BIG)
    kk = np.arange(256)[None, :]
    c["dist"] = np.concatenate([dist(q, k), dist(q + 128, kk)], 1)
    cpos = np.arange(NC_) * 16 + 31
    bias = np.zeros((128, 8, 2, NC_))
    mask = np.zeros((128, 2, NC_))
    for tt in range(2):
        qp = np.arange(128)[:, None] + 128 * tt
        mask[:, tt] = cpos[None, :] <= qp
        for h in range(8):
            bias[:, h, tt] = np.where(cpos[None, :] <= qp, -SLOPES[h] * (qp - cpos[None, :]), -BIG)
    c["cbias"] = bias.reshape(128, -1)
    c["cmask"] = mask.reshape(128, -1)
    R = np.arange(128)
    rh, rt = (R % 32) // 4, R % 4
    tab = np.zeros((128, 2, PAST + 32))
    slope = np.array(SLOPES)[rh][:, None]
    for w in range(2):
        b = w * 4 + R // 32
        tab[:, w, :PAST] = -slope * (PAST + rt[:, None] - np.arange(PAST)[None, :])
        nb, nt = np.arange(32) // 4, np.arange(32) % 4
        ok = (nb[None, :] == b[:, None]) & (nt[None, :] <= rt[:, None])
        tab[:, w, PAST:] = np.where(ok, -slope * (rt[:, None] - nt[None, :]), -BIG)
    c["stab"] = tab.reshape(128, -1)
    c["sctab"] = -slope * (PAST + rt[:, None] - cpos[None, :])
    c["rowhead"] = (rh[:, None] == np.arange(8)[None, :]) * 1.0
    sel = np.zeros((128, 2, 128))
    for w in range(2):
        sel[(w * 4 + R // 32) * 4 + rt, w, R] = 1.0
    c["selrow"] = sel.reshape(128, -1)
    col = np.arange(256)
    cb, ct = (col % 64) // 8, col % 4
    r = np.arange(32)
    ok = (r[:, None] // 4 == cb[None, :]) & (r[:, None] % 4 < ct[None, :])
    c["keepn"] = np.concatenate([ok * 1.0, np.zeros((96, 256))])
    c["blockn"] = np.concatenate([np.where(ok, 0.0, -BIG), np.zeros((96, 256))])
    c["iota"] = np.broadcast_to(t * 1.0, (128, 128))
    off = np.array(ROWOFF, float)
    c["rowoff"] = np.broadcast_to(off, (128, 16))
    c["rowlen"] = np.broadcast_to(np.concatenate([[0.0], np.diff(off)]), (128, 16))
    order, at, parts = {}, 0, []
    for name, a in c.items():
        order[name] = (at, a.shape[1])
        parts.append(a)
        at += a.shape[1]
    return order, np.ascontiguousarray(np.concatenate(parts, 1).astype(np.float32))


CONST, CONST_ARRAY = constants()
NCONST = CONST_ARRAY.shape[1]


def trunk(nc, xT, w_in, w_gate, w_out, w_q, keysT, uT, v, w1, pe_cmp, w2, vecs, cache_sb, cache_nsa,
          cache_cmp, win_kv, win_rows, page_table, consts,
          y_out, kv_out, win_out):
    ctx = ExitStack()
    with ctx:
        base = nc.sbuf_base if isinstance(nc.sbuf_base, int) else nc.sbuf_base()
        base = (base + 63) // 64 * 64
        placed = [0]

        def at(name, shape, where, dt=F32):
            return nc.alloc_sbuf_tensor_at(name, [shape[0]] + list(shape[1:]), dt, offset=base + 4 * where)

        def bump(words):
            placed[0] += (words + 15) // 16 * 16
            return placed[0] - (words + 15) // 16 * 16

        def words(*dims):
            n = 1
            for d in dims:
                n *= d
            return n

        con = at("con", [128, NCONST], bump(NCONST))
        vec = at("vec", [128, 5, KD], bump(5 * KD))
        pt = at("pt", [1, PAGES], bump(PAGES), I32)
        xTs = at("xTs", [128, KD, T], bump(KD * T))
        at_h = bump(KD * T)
        hT = at("hT", [128, KD, T], at_h)
        vnat = at("vnat", [128, 3, 6, 128], at_h)
        ring = at("ring", [128, 4, D], bump(4 * D))
        at_a = bump(NE * T)
        act_all = at("act_all", [128, NE, T], at_a)
        o = at_a
        kvs = at("kvs", [128, PAGES, 1024], o)
        winkv = at("winkv", [128, NB, 512], o)
        o += PAGES * 1024
        nsk = at("nsk", [128, PAGES, 256], o)
        o += PAGES * 256
        at_cmp = o
        cmpT = at("cmpT", [128, 2 * NSEQ, 2, 128], o)
        o += 2 * 2 * NSEQ * 128
        zT = at("zT", [128, ZT, T], o)
        o += ZT * T
        oT = at("oT", [128, KD, T], o)
        o += KD * T
        ckT = at("ckT", [128, NSEQ, NC_], o)
        o += 144
        cv = at("cv", [NC_, NSEQ, 128], o)
        o += NSEQ * 128
        hdn = at("hdn", [128, 2, 2 * NSEQ * NC_], o)
        o += 544
        qbd_a = at("qbd_a", [128, 4, NB, 8], o)
        o += 256
        qbd_b = at("qbd_b", [128, NB, 32], o)
        o += 256
        wg = at("wg", [128, KD, 24], o)
        o += 192
        assert o <= at_a + NE * T, (o, at_a + NE * T)
        r0 = at_a + NE * T - 18432
        sT = at("sT", [128, 3, 16, 128], r0)
        qT = at("qT", [128, 16, T], r0 + 6144)
        r1 = r0 + 6144 + 16 * T
        step = at("step", [128, 8 * TOPK, TOPK], r1)
        prod = at("prod", [128, 8 * TOPK, TOPK], r1 + 2048)
        r2 = r1 + 4096
        val = at("val", [128, 8, 2, TOPK], r2)
        idx = at("idx", [128, 8, 2, TOPK], r2 + 256, U32)
        idf = at("idf", [128, 8, 2, TOPK], r2 + 512)
        dlt = at("dlt", [128, 8, 2, TOPK], r2 + 768)
        cand = at("cand", [128, 8, NCAND], r2 + 1024)
        topv = at("topv", [128, 8, TOPK], r2 + 1424)
        pos = at("pos", [128, 8, TOPK], r2 + 1552, U32)
        posf = at("posf", [128, 8 * TOPK], r2 + 1680)
        rowo = at("rowo", [128, 8 * TOPK], r2 + 1808)
        ssum = at("ssum", [128, 3, 8], r2 + 1936)
        pick = at("pick", [128, 3, 3, 8 * TOPK], r2 + 1968)
        assert r2 + 1968 + 1152 <= at_a + NE * T
        FIRST_SHARED = (r0 - at_a) // T
        at_w1 = bump(4096)
        w1s = at("w1s", [128, 2, 16, 128], at_w1)
        rest = bump(448)
        pes = at("pes", [128, 2, 16], rest)
        w2s = at("w2s", [128, 2, HD], rest + 32)
        cb = at("cb", [128, 2], rest + 160)
        gnat = at("gnat", [128, 3, 24], rest + 176)
        grow = at("grow", [128, 2, 3], rest + 256)
        gtmp = at("gtmp", [128, 2, 24], rest + 272)
        knat = at("knat", [32, 128], rest + 320)
        zb = at("zb", [128, 768], at_cmp)
        lb = at("lb", [128, 768], at_cmp + 768)
        sp_ = at("sp_", [128, 768], at_cmp + 1536)
        ab = at("ab", [128, 768], at_cmp + 2304)
        wb = at("wb", [128, 768], at_cmp + 3072)
        ptc = at("ptc", [NC_, 8, TP], at_cmp)
        sc_ = at("sc_", [128, 16, NC_], at_cmp + 2048)
        ptcs = at("ptcs", [NC_, 256], at_cmp + 2304)
        zcs = at("zcs", [NC_, 256], at_cmp + 2560)
        ssc = at("ssc", [128, 2, NC_], at_cmp + 2816)
        sm = at("sm", [128, 160], at_cmp + 2880)
        zns = at("zns", [32, 2, 256], at_cmp + 3072)
        ptns = at("ptns", [32, 2, 256], at_cmp + 3584)
        pb = at("pb", [128, 2, 2, 384], at_w1)
        ptb = at("ptb", [128, 2, 2, 384], at_w1 + 1536)
        spb = at("spb", [128, 2, 2, PAST + 32], at_w1)
        zss = at("zss", [128, 2, 512], at_w1 + 1152)
        ptss = at("ptss", [128, 2, 512], at_w1 + 2176)
        keys = at("keys", [128, 16, 128], at_w1)
        sqb = at("sqb", [128, KD, T], at_w1)
        srow = at("srow", [128, T], at_w1 + 2304)
        rrow = at("rrow", [128, T], at_w1 + 2592)
        slotT = at("slotT", [128, 3, T], at_w1)
        onehot = at("onehot", [128, 2, 4, 2, 128], at_w1 + 864)
        col = at("col", [128, 2, 4], at_w1 + 864 + 2048)
        last_word = base + 4 * placed[0]
        end = nc.sbuf_usable_end if isinstance(nc.sbuf_usable_end, int) else nc.sbuf_usable_end()
        assert last_word <= end, (last_word, end)

        ps = ctx.enter_context(nc.psum_tensor("ps", [128, 8, 512], F32))

        def k(name, rows=128):
            a, n = CONST[name]
            return con[0:rows, a:a + n]

        def sem(name):
            return ctx.enter_context(nc.semaphore(name))

        con_in, x_in, small_in, pt_in, page_in, win_in, keys_in = map(
            sem, ("con_in", "x_in", "small_in", "pt_in", "page_in", "win_in", "keys_in"))
        full = [sem(f"ring_full{r}") for r in range(4)]
        z_mm, z_sb, v_mm, v_sb, gate_sb, q_ready, cmp_ready, zero_done = map(sem, (
            "z_mm", "z_sb", "v_mm", "v_sb", "gate_sb", "q_ready", "cmp_ready", "zero_done"))
        cb_mm, ch_mm, ch_sb, ckv_mm, ckv_sb = map(sem, ("cb_mm", "ch_mm", "ch_sb", "ckv_mm", "ckv_sb"))
        sb_qk, sb_zc, sb_ln, sb_sp, sb_tri, sb_arg, sb_w, sb_pv, sb_o = map(sem, (
            "sb_qk", "sb_zc", "sb_ln", "sb_sp", "sb_tri", "sb_arg", "sb_w", "sb_pv", "sb_o"))
        ss_qk, ss_ln, ss_sp, ss_tri, ss_arg, ss_w, ss_pv, ss_o = map(sem, (
            "ss_qk", "ss_ln", "ss_sp", "ss_tri", "ss_arg", "ss_w", "ss_pv", "ss_o"))
        nc_qk, nc_s, nc_e, nc_p, nc_t, nc_pt = map(sem, ("nc_qk", "nc_s", "nc_e", "nc_p", "nc_t", "nc_pt"))
        np_qk, np_s, np_e, np_p, np_t, np_pt, np_pv, np_o = map(sem, (
            "np_qk", "np_s", "np_e", "np_p", "np_t", "np_pt", "np_pv", "np_o"))
        ns_qk, ns_z, ns_t, ns_s, ns_e, ns_p, ns_tb, ns_pt, ns_pv, ns_o = map(sem, (
            "ns_qk", "ns_z", "ns_t", "ns_s", "ns_e", "ns_p", "ns_tb", "ns_pt", "ns_pv", "ns_o"))
        rm_sq, rm_mm, rm_sd, rm_on = map(sem, ("rm_sq", "rm_mm", "rm_sd", "rm_on"))
        m_mm, m_pre = map(sem, ("m_mm", "m_pre"))
        ln_mm, ln_c, ln_sq, ln_v, ln_sd, ln_h = map(sem, ("ln_mm", "ln_c", "ln_sq", "ln_v", "ln_sd", "ln_h"))
        q_mm, q_sb, s_mm, s_sb = map(sem, ("q_mm", "q_sb", "s_mm", "s_sb"))
        rt_exp_in, rt_exp, rt_pick, rt_t, rt_slot = map(sem, ("rt_exp_in", "rt_exp", "rt_pick", "rt_t", "rt_slot"))
        u_mm, u_act, f_mm = map(sem, ("u_mm", "u_act", "f_mm"))
        oh_a, oh_b, col_sb, g_mm, g_mul = map(sem, ("oh_a", "oh_b", "col_sb", "g_mm", "g_mul"))
        dve_link, act_link, pool_link = map(sem, ("dve_link", "act_link", "pool_link"))
        out_y, out_kv, out_win = map(sem, ("out_y", "out_kv", "out_win"))

        N_IN, N_OUT, N_Q = GT, KD, 16
        AT_OUT, AT_Q = N_IN, N_IN + N_OUT
        AT_U = AT_Q + N_Q
        AT_V = AT_U + NE

        def filled(n):
            return n % 4, 16 * (n // 4 + 1)

        def used_by(n):
            for first, mine in ((AT_V, f_mm), (AT_U, u_mm), (AT_Q, q_mm), (AT_OUT, m_mm), (0, z_mm)):
                if n >= first:
                    return mine, n - first + 1

        block = ctx.enter_context(nc.Block())

        @block.sync
        def _(sp):
            sp.dma_start(xTs[:, :, :], xT).then_inc(x_in, 16)

            def load(n, src):
                if n >= 4:
                    sp.wait_ge(*used_by(n - 4))
                sp.dma_start(ring[:, n % 4, :], src).then_inc(full[n % 4], 16)

            for n in range(4):
                load(n, w_in[n])
            sp.dma_start(con[:, :], consts).then_inc(con_in, 16)
            for n in range(4, N_IN):
                load(n, w_in[n])
            for n in range(N_OUT):
                load(AT_OUT + n, w_out[n])
            for n in range(N_Q):
                load(AT_Q + n, w_q[n])
            for src, first, mine in ((uT, AT_U, u_mm), (v, AT_V, f_mm)):
                for r in range(4):
                    load(first + r, src[r])
                with sp.Fori(1, NE // 4) as i:
                    for r in range(4):
                        sp.wait_ge(mine, 4 * i + (r - 3))
                        sp.dma_start(ring[:, (first + r) % 4, :],
                                     src[bass.ds(4 * i + r, 1)].rearrange("a p c -> (a p) c")
                                     ).then_inc(full[(first + r) % 4], 16)
            sp.wait_ge(ln_h, 2 * KD)
            sp.dma_start(y_out, xTs[:, :, :]).then_inc(out_y, 16)
            sp.wait_ge(out_y, 16)
            sp.wait_ge(out_kv, 32)
            sp.wait_ge(out_win, 48)

        @block.gpsimd
        def _(pool):
            pool.dma_start(pt[:, :], page_table).then_inc(pt_in, 16)
            pool.dma_start(w1s[:, :, :, :], w1).then_inc(small_in, 16)
            pool.dma_start(pes[:, :, :], pe_cmp).then_inc(small_in, 16)
            pool.dma_start(w2s[:, :, :], w2).then_inc(small_in, 16)
            pool.dma_start(vec[:, :, :], vecs).then_inc(small_in, 16)
            pool.dma_start(wg[:, :, :], w_gate).then_inc(small_in, 16)
            nc.gpsimd.memset(qbd_a[:, :, :, :], 0.0)
            nc.gpsimd.memset(qbd_b[:, :, :], 0.0).then_inc(zero_done, 1)
            pool.wait_ge(pt_in, 16)
            for b in range(NB):
                for p in range(2):
                    n = 2 * b + p
                    page = nc.gpsimd.value_load(pt[0:1, n:n + 1], min_val=0, max_val=cache_sb.shape[0] - 1)
                    src = lambda t: t[bass.ds(page, 1)]
                    pool.dma_start(cmpT[:, 2 + 2 * b:4 + 2 * b, :, 64 * p:64 * p + 64].rearrange("p g k n -> p (g k) n"),
                                   src(cache_cmp).rearrange("a p g k n -> (a p) (g k) n")).then_inc(page_in, 16)
                    pool.dma_start(kvs[:, n, :], src(cache_sb).rearrange("a p c -> (a p) c")).then_inc(page_in, 16)
                    pool.dma_start(nsk[:, n, :], src(cache_nsa).rearrange("a p c -> (a p) c")).then_inc(page_in, 16)
            pool.dma_start(win_out[:, 0:PAST - TS, :], win_rows[:, TS:PAST, :]).then_inc(out_win, 16)
            pool.wait_ge(z_sb, 4 + ZT)
            pool.dma_start(kv_out[:, 0:8, :], zT[:, KA:KA + 8, :]).then_inc(out_kv, 16)
            pool.dma_start(kv_out[:, 8:14, :], zT[:, CK:CK + 6, :]).then_inc(out_kv, 16)
            pool.wait_ge(v_sb, 3)
            pool.dma_start(win_out[:, PAST - TS:PAST, 0:128], knat[:, :]).then_inc(out_win, 16)
            pool.dma_start(win_out[:, PAST - TS:PAST, 128:256], vnat[0:32, 2, 5, :]).then_inc(out_win, 16)
            pool.wait_ge(ss_pv, 1)
            pool.dma_start(winkv[:, :, :], win_kv).then_inc(win_in, 16)
            pool.wait_ge(ln_h, KD)
            pool.dma_start(keys[:, :, :], keysT).then_inc(keys_in, 16)
            def columns(t, g):
                nc.gpsimd.tensor_copy(col[:, g, :], slotT[:, 1, t]).then_inc(col_sb, 1)

            def onehots(g):
                for t in range(4):
                    ins = nc.gpsimd.tensor_scalar(onehot[:, g, t, 1, :], k("iota"), col[:, g, t:t + 1],
                                                  None, ALU.is_equal)
                ins.then_inc(oh_b, 1)

            pool.sem_inc(oh_b, 2)
            pool.wait_ge(rt_slot, 3)
            columns(slice(0, 4), 0)
            with pool.Fori(0, T // 8 - 1) as i:
                for g in range(2):
                    pool.wait_ge(g_mm, 2 * i + g + 1)
                    pool.wait_ge(oh_b, 2 * i + g + 2)
                    pool.wait_ge(col_sb, 2 * i + g + 1)
                    columns(bass.ds(8 * i + 4 * g + 4, 4), 1 - g)
                    onehots(g)
            pool.wait_ge(g_mm, T // 4 - 1)
            pool.wait_ge(oh_b, T // 4)
            pool.wait_ge(col_sb, T // 4 - 1)
            columns(slice(T - 4, T), 1)
            onehots(0)
            pool.wait_ge(g_mm, T // 4)
            pool.wait_ge(col_sb, T // 4)
            onehots(1)

        @block.tensor
        def _(pe):
            mm = nc.tensor.matmul
            ident = k("ident")

            pe.sem_inc(g_mm, 2)
            pe.wait_ge(x_in, 16)

            def project(r, bank, rhs, out_rows=128):
                for kd in range(KD):
                    ins = mm(ps[:, bank, 0:T], ring[:, r, kd * 128:(kd + 1) * 128], rhs[:, kd, :],
                             start=kd == 0, stop=kd == KD - 1)
                return ins

            with pe.Fori(0, 5) as i:
                for r in range(4):
                    pe.wait_ge(full[r], 16 * i + 16)
                    pe.wait_ge(z_sb, 4 * i + r + 1)
                    ins = project(r, r, xTs)
                    ins.then_inc(z_mm, 1)
            for c in range(20, N_IN):
                slot, value = filled(c)
                pe.wait_ge(full[slot], value)
                pe.wait_ge(z_sb, c + 1)
                ins = project(c % 4, c % 4, xTs)
                ins.then_inc(z_mm, 1)
            pe.wait_ge(small_in, 16 * 5)
            pe.wait_ge(z_sb, GT + 1)
            for kd in range(KD):
                ins = mm(ps[0:24, 2, 0:T], wg[:, kd, :], xTs[:, kd, :], start=kd == 0, stop=kd == KD - 1)
            ins.then_inc(z_mm, 1)

            pe.wait_ge(con_in, 16)
            pe.wait_ge(z_sb, 4 + ZT)
            for tt, (t0, n) in enumerate(TOK):
                a, b = (4, 6, 0)[tt], (5, 7, 1)[tt]
                tok = slice(t0, t0 + n)
                for j in range(4):
                    nc.tensor.transpose(ps[0:n, a, j * 128:(j + 1) * 128], zT[:, VA + j, tok], ident)
                nc.tensor.transpose(ps[0:n, b, 0:128], zT[:, SV, tok], ident)
                nc.tensor.transpose(ps[0:n, b, 128:256], zT[:, WV, tok], ident)
                if tt == 2:
                    nc.tensor.transpose(ps[0:n, b, 256:384], zT[:, WK, tok], ident)
                nc.tensor.transpose(ps[0:n, b, 384:408], zT[0:24, GT, tok], ident[0:24, 0:24]).then_inc(v_mm, 1)

            for j in range(2):
                for m in range(16):
                    ins = mm(ps[:, 2, j:j + 1], w1s[:, j, m, :], pes[:, j, m:m + 1], start=m == 0, stop=m == 15)
            ins.then_inc(cb_mm, 1)
            pe.wait_ge(cmp_ready, 1)
            pe.wait_ge(page_in, 16 * 3 * PAGES)
            for j in range(2):
                for m in range(16):
                    blocks = cmpT[:, :, j, m:m + 8 * (NC_ - 1) + 1:8]
                    ins = mm(ps[:, 3 + j, 0:2 * NSEQ * NC_], w1s[:, j, m, :], blocks, start=m == 0, stop=m == 15)
                ins.then_inc(ch_mm, 1)
                if j == 0:
                    pe.wait_ge(v_sb, 1)
            pe.wait_ge(ch_sb, 1)
            pe.wait_ge(v_sb, 3)
            hd = hdn[:, :, :].rearrange("p j (s g n) -> p j s g n", g=2, n=NC_)
            for g in range(2):
                ins = mm(ps[g * HD:(g + 1) * HD, 5, 0:NSEQ * NC_], w2s[:, 0, :], hd[:, 0, :, g, :],
                         start=True, stop=True)
            ins.then_inc(ckv_mm, 1)
            pe.wait_ge(ch_sb, 2)
            for s in range(NSEQ):
                for g in range(2):
                    c = (s % 4) * 128 + g * HD
                    ins = mm(ps[0:NC_, (6, 7, 0)[s // 4], c:c + HD], hd[:, 1, s, g, :], w2s[:, 1, :],
                             start=True, stop=True)
            ins.then_inc(ckv_mm, 1)

            pe.wait_ge(q_ready, 1)
            pe.wait_ge(ckv_sb, 2)

            def sb_scores(h):
                if h >= 2:
                    pe.wait_ge(sb_zc, h - 1)
                hp, half = h // 2, slice((h % 2) * HD, (h % 2 + 1) * HD)
                b = 1 + h % 2
                mm(ps[:, b, 0:256], zT[half, KA + hp, 0:128], zT[half, hp, 0:256], start=True, stop=True)
                mm(ps[:, b, 256:384], zT[half, KA + hp, 128:256], zT[half, hp, 128:256],
                   start=True, stop=True).then_inc(sb_qk, 1)

            def sb_sums(h):
                pe.wait_ge(sb_sp, h + 1)
                if h >= 2:
                    pe.wait_ge(sb_arg, h - 1)
                b, x = 3 + h % 2, (h % 2) * 384
                mm(ps[:, b, 0:256], k("negtri"), sp_[:, x:x + 256], start=True, stop=False)
                mm(ps[:, b, 128:256], k("negones"), sp_[:, x + 256:x + 384], start=False, stop=False)
                mm(ps[:, b, 0:128], ident, k("block"), start=False, stop=True)
                mm(ps[:, b, 256:384], k("negtri"), sp_[:, x + 256:x + 384], start=True, stop=False)
                mm(ps[:, b, 256:384], ident, k("block"), start=False, stop=True).then_inc(sb_tri, 1)

            def sb_values(h):
                pe.wait_ge(sb_w, h + 1)
                hp, x = h // 2, (h % 2) * 384
                if h % 2 == 0 and hp >= 2:
                    pe.wait_ge(sb_o, hp - 1)
                half = slice((h % 2) * HD, (h % 2 + 1) * HD)
                b = 5 + hp % 2
                mm(ps[half, b, 0:256], vnat[:, 0, hp, half], wb[:, x:x + 256], start=True, stop=False)
                mm(ps[half, b, 128:256], vnat[:, 1, hp, half], wb[:, x + 256:x + 384],
                   start=False, stop=True).then_inc(sb_pv, 1)

            sb_scores(0)
            sb_scores(1)
            sb_sums(0)
            for h in range(8):
                if h + 2 < 8:
                    sb_scores(h + 2)
                if h + 1 < 8:
                    sb_sums(h + 1)
                sb_values(h)

            pe.wait_ge(sb_zc, 8)
            for p in range(2):
                for b in range(NB):
                    for hp in range(4):
                        c = p * 256 + hp * 64 + b * 8
                        mm(ps[:, 1, c:c + 8], kvs[:, 2 * b + p, hp * 128:(hp + 1) * 128], qbd_a[:, hp, b, :],
                           start=True, stop=True)
            for hp in range(4):
                ins = mm(ps[0:32, 2, hp * 64:(hp + 1) * 64], zT[:, KA + hp, TP:T],
                         qbd_a[:, hp, :, :], start=True, stop=True)
            ins.then_inc(ss_qk, 1)
            pe.wait_ge(ss_sp, 1)
            pe.wait_ge(sb_arg, 8)
            mm(ps[:, 3, 0:512], k("negtri"), sp_[:, 0:512], start=True, stop=False)
            mm(ps[:, 3, 0:256], k("negones"), sp_[:, 256:512], start=False, stop=False)
            mm(ps[:, 3, 0:256], k("negones", 32), sp_[0:32, 512:768], start=False, stop=False)
            mm(ps[:, 3, 256:512], k("negones", 32), sp_[0:32, 512:768], start=False, stop=True)
            mm(ps[0:32, 4, 0:256], k("negtri", 32)[:, 0:32], sp_[0:32, 512:768], start=True, stop=False)
            mm(ps[0:32, 4, 0:256], ident[0:32, 0:32], k("blockn", 32), start=False, stop=True).then_inc(ss_tri, 1)
            pe.wait_ge(ss_w, 1)
            for hp in range(4):
                mm(ps[:, 7, hp * 64:(hp + 1) * 64], vnat[0:32, 2, hp, :], wb[0:32, 512 + hp * 64:576 + hp * 64],
                   start=True, stop=False)
                for b in range(NB):
                    for p in range(2):
                        c = hp * 64 + b * 8
                        ins = mm(ps[:, 7, c:c + 8], kvs[:, 2 * b + p, 512 + hp * 128:640 + hp * 128],
                                 wb[:, p * 256 + c:p * 256 + c + 8], start=False, stop=(b == NB - 1 and p == 1))
            ins.then_inc(ss_pv, 1)

            pe.wait_ge(sb_o, 4)
            pe.wait_ge(ss_o, 1)
            for h in range(8):
                r, g = h % 4, slice((h // 4) * HD, (h // 4 + 1) * HD)
                for tt in range(2):
                    c = (2 * r + tt) * 16
                    ins = mm(ps[:, 6 + h // 4, c:c + NC_], zT[g, QB + r, tt * 128:(tt + 1) * 128], ckT[g, 0, :],
                             start=True, stop=True)
            ins.then_inc(nc_qk, 1)
            pe.wait_ge(nc_p, 1)
            for h in range(8):
                for tt in range(2):
                    ins = nc.tensor.transpose(ps[0:NC_, h // 2, (h % 2) * 256 + tt * 128:(h % 2) * 256 + (tt + 1) * 128],
                                              sc_[:, 2 * h + tt, :], ident)
            ins.then_inc(nc_t, 1)

            HEADS = [(n // 2, n % 2) for n in range(8)]

            def np_scores(n):
                r, g = HEADS[n]
                half = slice(g * HD, (g + 1) * HD)
                if n < 2:
                    pe.wait_ge(nc_pt, 1)
                else:
                    pe.wait_ge(np_s, n - 1)
                for br, kt in enumerate((SK, WK)):
                    b = 2 * (n % 2) + br
                    mm(ps[:, b, 0:128], zT[half, QB + r, 0:128], zT[half, kt, 0:128], start=True, stop=True)
                    ins = mm(ps[:, b, 128:384], zT[half, QB + r, 128:256], zT[half, kt, 0:256],
                             start=True, stop=True)
                ins.then_inc(np_qk, 1)

            def np_turn(n):
                pe.wait_ge(np_p, n + 1)
                if n >= 1:
                    pe.wait_ge(np_pt, n)
                for br in range(2):
                    for c in range(3):
                        ins = nc.tensor.transpose(ps[:, 4 + br, c * 128:(c + 1) * 128],
                                                  pb[:, n % 2, br, c * 128:(c + 1) * 128], ident)
                ins.then_inc(np_t, 1)

            def np_values(n):
                r, g = HEADS[n]
                half = slice(g * HD, (g + 1) * HD)
                h = g * 4 + r
                b = 6 + r % 2
                pe.wait_ge(np_pt, n + 1)
                if g == 0 and r >= 2:
                    pe.wait_ge(np_o, r - 1)
                mm(ps[half, b, 0:256], cv[:, 0, half], ptc[:, h, :], start=True, stop=False)
                for br in range(2):
                    mm(ps[half, b, 0:256], vnat[:, 0, 4 + br, half], ptb[:, n % 2, br, 0:256], start=False, stop=False)
                    ins = mm(ps[half, b, 128:256], vnat[:, 1, 4 + br, half], ptb[:, n % 2, br, 256:384],
                             start=False, stop=br == 1)
                ins.then_inc(np_pv, 1)

            np_scores(0)
            np_scores(1)
            for n in range(9):
                if n < 8:
                    np_turn(n)
                if n + 2 < 8:
                    np_scores(n + 2)
                if n >= 1:
                    np_values(n - 1)

            pe.wait_ge(win_in, 16)
            pe.wait_ge(np_s, 8)
            for b in range(NB):
                for p in range(2):
                    c = p * 256 + b * 32
                    mm(ps[:, 0, c:c + 32], nsk[:, 2 * b + p, 0:128], qbd_b[:, b, :], start=True, stop=True)
                    mm(ps[:, 1, c:c + 32], winkv[:, b, p * 128:(p + 1) * 128], qbd_b[:, b, :], start=True, stop=True)
                mm(ps[0:NC_, 3, b * 32:(b + 1) * 32], ckT[:, 1 + b, :], qbd_b[:, b, :], start=True, stop=True)
            for br, kt in enumerate((SK, WK)):
                ins = mm(ps[0:32, 2, br * 256:(br + 1) * 256], zT[:, kt, TP:T], qbd_b[:, :, :], start=True, stop=True)
            ins.then_inc(ns_qk, 1)
            pe.wait_ge(ns_z, 1)
            pe.wait_ge(np_o, 4)
            for br in range(2):
                for w in range(2):
                    b = 4 + 2 * br + w
                    for p in range(2):
                        nc.tensor.transpose(ps[:, b, p * 128:(p + 1) * 128],
                                            zss[:, br, p * 256 + w * 128:p * 256 + (w + 1) * 128], ident)
                    nc.tensor.transpose(ps[:, b, 256:288], zns[:, br, w * 128:(w + 1) * 128], ident[0:32, 0:32])
            for w in range(2):
                nc.tensor.transpose(ps[:, 0, w * 16:w * 16 + NC_], zcs[:, w * 128:(w + 1) * 128], ident[0:NC_, 0:NC_])
                ins = mm(ps[:, 1, w * 24:(w + 1) * 24], k("selrow", 32)[:, w * 128:(w + 1) * 128], gnat[0:32, 2, :],
                         start=True, stop=True)
            ins.then_inc(ns_t, 1)
            pe.wait_ge(ns_p, 1)
            for w in range(2):
                for br in range(2):
                    for p in range(2):
                        nc.tensor.transpose(ps[:, 2 + br, p * 256 + w * 128:p * 256 + (w + 1) * 128],
                                            spb[:, br, w, p * 128:(p + 1) * 128], ident)
                    nc.tensor.transpose(ps[0:32, 0, br * 256 + w * 128:br * 256 + (w + 1) * 128],
                                        spb[:, br, w, 256:288], ident)
                ins = nc.tensor.transpose(ps[0:NC_, 1, w * 128:(w + 1) * 128], ssc[:, w, :], ident)
            ins.then_inc(ns_tb, 1)
            pe.wait_ge(ns_pt, 1)
            for br in range(2):
                mm(ps[:, 4, 0:256], vnat[0:32, 2, 4 + br, :], ptns[:, br, :], start=br == 0, stop=False)
            for b in range(NB):
                c = slice(b * 32, (b + 1) * 32)
                for p in range(2):
                    pc = slice(p * 256 + b * 32, p * 256 + (b + 1) * 32)
                    mm(ps[:, 4, c], nsk[:, 2 * b + p, 128:256], ptss[:, 0, pc], start=False, stop=False)
                    mm(ps[:, 4, c], winkv[:, b, 256 + p * 128:384 + p * 128], ptss[:, 1, pc], start=False, stop=False)
                ins = mm(ps[:, 4, c], cv[:, 1 + b, :], ptcs[:, b * 32:(b + 1) * 32], start=False, stop=b == NB - 1)
            ins.then_inc(ns_pv, 1)

            pe.wait_ge(rm_sq, 1)
            for m in range(2):
                for j in range(4):
                    ins = mm(ps[:, m, 0:T], k("ones"), sqb[:, 4 * m + j, :], start=j == 0, stop=j == 3)
            ins.then_inc(rm_mm, 1)
            pe.wait_ge(rm_on, KD)
            for c in range(KD):
                slot, value = filled(AT_OUT + c)
                pe.wait_ge(full[slot], value)
                if c >= 4:
                    pe.wait_ge(m_pre, c - 3)
                ins = project(slot, 4 + c % 4, oT)
                ins.then_inc(m_mm, 1)

            def norm_sums(n):
                for c in range(KD):
                    pe.wait_ge(m_pre, KD * n + c + 1)
                    ins = mm(ps[:, 0, 0:T], k("ones"), xTs[:, c, :], start=c == 0, stop=c == KD - 1)
                ins.then_inc(ln_mm, 1)
                pe.wait_ge(ln_sq, n + 1)
                for c in range(KD):
                    ins = mm(ps[:, 1, 0:T], k("ones"), sqb[:, c, :], start=c == 0, stop=c == KD - 1)
                ins.then_inc(ln_v, 1)

            norm_sums(0)

            pe.wait_ge(ln_h, KD)
            with pe.Fori(0, 4) as i:
                for r in range(4):
                    slot, value = filled(AT_Q + r)
                    pe.wait_ge(full[slot], 16 * i + value)
                    pe.wait_ge(q_sb, 4 * i + r + 1)
                    ins = project(slot, r, hT)
                    ins.then_inc(q_mm, 1)
            pe.wait_ge(keys_in, 16)
            pe.wait_ge(q_sb, 4 + 16)
            for tt, (t0, n) in enumerate(TOK):
                if tt:
                    pe.wait_ge(s_sb, tt)
                for c in range(16):
                    ins = mm(ps[0:n, 4 + c // 4, (c % 4) * 128:(c % 4 + 1) * 128], qT[:, c, t0:t0 + n],
                             keys[:, c, :], start=True, stop=True)
                ins.then_inc(s_mm, 1)

            def experts_up(first, last):
                with pe.Fori(first, last) as i:
                    for r in range(4):
                        slot, value = filled(AT_U + r)
                        pe.wait_ge(full[slot], 16 * i + value)
                        pe.wait_ge(u_act, 4 * i + r + 1)
                        ins = project(slot, r, hT)
                        ins.then_inc(u_mm, 1)

            experts_up(0, 16)
            pe.wait_ge(rt_pick, 3)
            pe.wait_ge(s_sb, 3)
            for c in range(3):
                for tt, (t0, n) in enumerate(TOK):
                    ins = nc.tensor.transpose(ps[:, 4 + c, t0:t0 + n], pick[0:n, tt, c, :], ident[0:n, 0:n])
                ins.then_inc(rt_t, 1)
            experts_up(16, 32)

            pe.wait_ge(rt_slot, 3)
            with pe.Fori(0, T // 8) as i:
                for g in range(2):
                    pe.wait_ge(oh_a, 2 * i + g + 1)
                    pe.wait_ge(oh_b, 2 * i + g + 3)
                    pe.wait_ge(g_mul, 2 * i + g + 1)
                    for t in range(4):
                        ins = mm(ps[:, 4 + g, t * 128:(t + 1) * 128], onehot[:, g, t, 0, :],
                                 onehot[:, g, t, 1, :], start=True, stop=True)
                    ins.then_inc(g_mm, 1)

            pe.wait_ge(g_mul, 2 + T // 4)
            pe.wait_ge(u_act, 4 + NE)

            def experts_down(i, r, row, value, start, stop):
                pe.wait_ge(full[(AT_V + r) % 4], value)
                for c in range(KD):
                    ins = mm(ps[:, c, 0:T], ring[:, (AT_V + r) % 4, c * 128:(c + 1) * 128], row,
                             start=start, stop=stop)
                ins.then_inc(f_mm, 1)

            for r in range(4):
                experts_down(0, r, act_all[:, r, :], filled(AT_V + r)[1], r == 0, False)
            with pe.Fori(1, NE // 4 - 1) as i:
                for r in range(4):
                    experts_down(i, r, act_all[:, bass.ds(4 * i + r, 1), :].rearrange("p a t -> p (a t)"),
                                 16 * i + filled(AT_V + r)[1], False, False)
            for r in range(4):
                j = NE - 4 + r
                experts_down(0, r, act_all[:, j, :], filled(AT_V + j)[1], False, r == 3)
            norm_sums(1)

        @block.scalar
        def _(act):
            A = nc.scalar.activation
            done = [0]

            def link(ins):
                done[0] += 1
                ins.then_inc(act_link, 1)
                act.wait_ge(act_link, done[0])

            act.sem_inc(z_sb, 4)
            with act.Fori(0, 5) as i:
                for r in range(4):
                    act.wait_ge(z_mm, 4 * i + r + 1)
                    nc.scalar.copy(zT[:, bass.ds(4 * i + r, 1), :], ps[:, r:r + 1, 0:T]).then_inc(z_sb, 1)
            for c in range(20, GT):
                act.wait_ge(z_mm, c + 1)
                nc.scalar.copy(zT[:, c, :], ps[:, c % 4, 0:T]).then_inc(z_sb, 1)
            act.wait_ge(z_mm, ZT)
            nc.scalar.copy(zT[0:24, GT, :], ps[0:24, 2, 0:T]).then_inc(z_sb, 1)

            for tt, (t0, n) in enumerate(TOK):
                a, b = (4, 6, 0)[tt], (5, 7, 1)[tt]
                act.wait_ge(v_mm, tt + 1)
                nc.scalar.copy(vnat[0:n, tt, 0:4, :], ps[0:n, a, :].rearrange("p (a b) -> p a b", b=128))
                nc.scalar.copy(vnat[0:n, tt, 4:6, :], ps[0:n, b, 0:256].rearrange("p (a b) -> p a b", b=128))
                if tt == 2:
                    nc.scalar.copy(knat[:, :], ps[0:n, b, 256:384])
                A(gnat[0:n, tt, :], ps[0:n, b, 384:408], ACT.Exp, scale=-1.0).then_inc(v_sb, 1)
            act.wait_ge(cb_mm, 1)
            link(nc.scalar.copy(cb[:, :], ps[:, 2, 0:2]))
            for j in range(2):
                act.wait_ge(ch_mm, j + 1)
                A(hdn[:, j, :], ps[:, 3 + j, 0:2 * NSEQ * NC_], ACT.Gelu_apprx_tanh,
                  bias=cb[:, j:j + 1]).then_inc(ch_sb, 1)
            act.wait_ge(ckv_mm, 1)
            nc.scalar.copy(ckT[:, :, :], ps[:, 5, 0:NSEQ * NC_].rearrange("p (s n) -> p s n", n=NC_)).then_inc(ckv_sb, 1)
            act.wait_ge(ckv_mm, 2)
            for m in range(3):
                w = min(4, NSEQ - 4 * m)
                ins = nc.scalar.copy(cv[:, 4 * m:4 * m + w, :],
                                     ps[0:NC_, (6, 7, 0)[m], 0:w * 128].rearrange("p (s n) -> p s n", n=128))
            ins.then_inc(ckv_sb, 1)

            def sb_soft(h):
                x = slice((h % 2) * 384, (h % 2) * 384 + 384)
                act.wait_ge(sb_qk, h + 1)
                if h >= 2:
                    act.wait_ge(sb_arg, h - 1)
                nc.scalar.copy(zb[:, x], ps[:, 1 + h % 2, 0:384])
                ins = A(lb[:, x], ps[:, 1 + h % 2, 0:384], ACT.Abs)
                ins.then_inc(sb_zc, 1)
                act.wait_ge(sb_zc, h + 1)
                link(A(lb[:, x], lb[:, x], ACT.Exp, scale=-1.0))
                A(lb[:, x], lb[:, x], ACT.Ln, bias=1.0).then_inc(sb_ln, 1)

            def sb_exp(h):
                x = slice((h % 2) * 384, (h % 2) * 384 + 384)
                act.wait_ge(sb_arg, h + 1)
                if h >= 2:
                    act.wait_ge(sb_pv, h - 1)
                A(wb[:, x], ab[:, x], ACT.Exp).then_inc(sb_w, 1)

            sb_soft(0)
            for h in range(8):
                if h + 1 < 8:
                    sb_soft(h + 1)
                sb_exp(h)

            act.wait_ge(ss_qk, 1)
            act.wait_ge(sb_arg, 8)
            parts = ((slice(0, 128), slice(0, 512), 1), (slice(0, 32), slice(512, 768), 2))
            for rows, c, b in parts:
                w = c.stop - c.start
                nc.scalar.copy(zb[rows, c], ps[rows, b, 0:w])
                link(A(lb[rows, c], ps[rows, b, 0:w], ACT.Abs))
            for rows, c, b in parts:
                link(A(lb[rows, c], lb[rows, c], ACT.Exp, scale=-1.0))
            for rows, c, b in parts:
                ins = A(lb[rows, c], lb[rows, c], ACT.Ln, bias=1.0)
            ins.then_inc(ss_ln, 1)
            act.wait_ge(ss_arg, 1)
            act.wait_ge(sb_pv, 8)
            for rows, c, b in parts:
                ins = A(wb[rows, c], ab[rows, c], ACT.Exp)
            ins.then_inc(ss_w, 1)

            act.wait_ge(nc_s, 1)
            A(sc_[:, :, :], sc_[:, :, :], ACT.Exp).then_inc(nc_e, 1)
            act.wait_ge(nc_t, 1)
            act.wait_ge(ss_pv, 1)
            for m in range(4):
                ins = nc.scalar.copy(ptc[:, 2 * m:2 * m + 2, :], ps[0:NC_, m, :].rearrange("p (h t) -> p h t", t=256))
            ins.then_inc(nc_pt, 1)

            def np_exp(n):
                act.wait_ge(np_s, n + 1)
                x = (n % 2) * 16
                for br in range(2):
                    for tt, c in enumerate((slice(0, 128), slice(128, 384))):
                        y = x + 2 * br + tt
                        ins = A(pb[:, n % 2, br, c], pb[:, n % 2, br, c], ACT.Exp, bias=sm[:, y:y + 1],
                                accum_out=sm[:, y + 4:y + 5])
                ins.then_inc(np_e, 1)

            np_exp(0)
            for n in range(8):
                if n + 1 < 8:
                    np_exp(n + 1)
                act.wait_ge(np_t, n + 1)
                if n >= 2:
                    act.wait_ge(np_pv, n - 1)
                nc.scalar.copy(ptb[:, n % 2, :, :], ps[:, 4:6, 0:384]).then_inc(np_pt, 1)

            act.wait_ge(ns_qk, 1)
            nc.scalar.copy(zss[:, :, :], ps[:, 0:2, :])
            nc.scalar.copy(zns[:, :, :], ps[0:32, 2, :].rearrange("p (a b) -> p a b", b=256))
            nc.scalar.copy(zcs[:, :], ps[0:NC_, 3, 0:256]).then_inc(ns_z, 1)
            act.wait_ge(ns_s, 1)
            for w in range(2):
                for br in range(2):
                    y = 64 + 2 * br + w
                    A(spb[:, br, w, :], spb[:, br, w, :], ACT.Exp, bias=sm[:, y:y + 1], accum_out=sm[:, y + 8:y + 9])
                y = 64 + 4 + w
                ins = A(ssc[:, w, :], ssc[:, w, :], ACT.Exp, bias=sm[:, y:y + 1], accum_out=sm[:, y + 8:y + 9])
            ins.then_inc(ns_e, 1)
            act.wait_ge(ns_tb, 1)
            nc.scalar.copy(ptss[:, :, :], ps[:, 2:4, :])
            nc.scalar.copy(ptns[:, :, :], ps[0:32, 0, :].rearrange("p (a b) -> p a b", b=256))
            nc.scalar.copy(ptcs[:, :], ps[0:NC_, 1, 0:256]).then_inc(ns_pt, 1)

            act.wait_ge(ns_o, 1)
            A(sqb[:, :, :], oT[:, :, :], ACT.Square).then_inc(rm_sq, 1)
            act.wait_ge(rm_mm, 1)
            act.wait_ge(rm_sd, 1)
            A(srow[:, :], srow[:, :], ACT.Sqrt)
            A(rrow[:, :], rrow[:, :], ACT.Sqrt).then_inc(rm_sd, 1)

            def norm_act(n):
                act.wait_ge(ln_c, n + 1)
                A(sqb[:, :, :], xTs[:, :, :], ACT.Square).then_inc(ln_sq, 1)
                act.wait_ge(ln_sd, 2 * n + 1)
                A(srow[:, :], srow[:, :], ACT.Sqrt).then_inc(ln_sd, 1)

            norm_act(0)

            act.sem_inc(q_sb, 4)
            with act.Fori(0, 4) as i:
                for r in range(4):
                    act.wait_ge(q_mm, 4 * i + r + 1)
                    nc.scalar.copy(qT[:, bass.ds(4 * i + r, 1), :], ps[:, r:r + 1, 0:T]).then_inc(q_sb, 1)
            for tt, (t0, n) in enumerate(TOK):
                act.wait_ge(s_mm, tt + 1)
                nc.scalar.copy(sT[0:n, tt, :, :].rearrange("p (a b) c -> p a (b c)", b=4),
                               ps[0:n, 4:8, :]).then_inc(s_sb, 1)

            act.wait_ge(out_kv, 32)
            act.wait_ge(out_win, 48)
            act.sem_inc(u_act, 4)

            def gelus(first, last):
                with act.Fori(first, last) as i:
                    for r in range(4):
                        act.wait_ge(u_mm, 4 * i + r + 1)
                        A(act_all[:, bass.ds(4 * i + r, 1), :], ps[:, r:r + 1, 0:T],
                          ACT.Gelu_apprx_tanh).then_inc(u_act, 1)

            gelus(0, 14)
            act.wait_ge(rt_exp_in, 3)
            for tt, (t0, n) in enumerate(TOK):
                A(pick[0:n, tt, 2, :], pick[0:n, tt, 2, :], ACT.Exp).then_inc(rt_exp, 1)
            gelus(14, 16)
            for c in range(3):
                act.wait_ge(rt_t, c + 1)
                nc.scalar.copy(slotT[:, c, :], ps[:, 4 + c, 0:T]).then_inc(rt_slot, 1)
            gelus(16, 32)
            norm_act(1)

        @block.vector
        def _(dve):
            V = nc.vector
            done = [0]

            def link(ins):
                done[0] += 1
                ins.then_inc(dve_link, 1)
                dve.wait_ge(dve_link, done[0])

            dve.wait_ge(z_sb, 4 + ZT)
            for g in range(2):
                for par in range(2):
                    for j in range(2):
                        ins = V.tensor_copy(cmpT[par * HD:(par + 1) * HD, g, j, :],
                                            zT[g * HD:(g + 1) * HD, CK + j, par:TP:2])
            ins.then_inc(cmp_ready, 1)
            link(V.tensor_scalar(zT[:, 0:4, :], zT[:, 0:4, :], SCALE, None, ALU.mult))
            link(V.tensor_scalar(zT[:, QB:QB + 4, :], zT[:, QB:QB + 4, :], SCALE, None, ALU.mult))
            dve.wait_ge(zero_done, 1)
            for g in range(2):
                half = slice(g * HD, (g + 1) * HD)
                V.tensor_copy(qbd_a[half, :, :, g * 4:(g + 1) * 4],
                              zT[half, 0:4, TP:T].rearrange("p h (b t) -> p h b t", t=TS))
                ins = V.tensor_copy(qbd_b[half, :, g * 16:(g + 1) * 16].rearrange("p b (r t) -> p b r t", t=TS),
                                    zT[half, QB:QB + 4, TP:T].rearrange("p r (b t) -> p b r t", t=TS))
            ins.then_inc(q_ready, 1)
            dve.wait_ge(v_sb, 3)
            for rows, tt in ((slice(0, 128), slice(0, 2)), (slice(0, 32), slice(2, 3))):
                link(V.tensor_scalar(gnat[rows, tt, :], gnat[rows, tt, :], 1.0, None, ALU.add))
                link(V.reciprocal(gnat[rows, tt, :], gnat[rows, tt, :]))

            def sb_plus(h):
                x = (h % 2) * 384
                dve.wait_ge(sb_ln, h + 1)
                if h >= 2:
                    dve.wait_ge(sb_tri, h - 1)
                link(V.scalar_tensor_tensor(sp_[:, x:x + 384], zb[:, x:x + 384], 0.0, lb[:, x:x + 384],
                                            ALU.max, ALU.add))
                V.tensor_tensor(sp_[:, x:x + 128], sp_[:, x:x + 128], k("keep"), ALU.mult)
                V.tensor_tensor(sp_[:, x + 256:x + 384], sp_[:, x + 256:x + 384], k("keep"),
                                ALU.mult).then_inc(sb_sp, 1)

            def sb_out(hp):
                dve.wait_ge(sb_pv, 2 * hp + 2)
                V.tensor_copy(oT[:, hp, 0:256], ps[:, 5 + hp % 2, 0:256]).then_inc(sb_o, 1)

            sb_plus(0)
            for h in range(8):
                if h + 1 < 8:
                    sb_plus(h + 1)
                x = (h % 2) * 384
                dve.wait_ge(sb_tri, h + 1)
                if h >= 2:
                    dve.wait_ge(sb_w, h - 1)
                V.tensor_tensor(ab[:, x:x + 384], zb[:, x:x + 384], ps[:, 3 + h % 2, 0:384],
                                ALU.add).then_inc(sb_arg, 1)
                if h in (3, 5, 7):
                    sb_out((h - 3) // 2)
            sb_out(3)

            dve.wait_ge(ss_ln, 1)
            dve.wait_ge(sb_tri, 8)
            V.scalar_tensor_tensor(sp_[:, 0:512], zb[:, 0:512], 0.0, lb[:, 0:512], ALU.max, ALU.add)
            link(V.scalar_tensor_tensor(sp_[0:32, 512:768], zb[0:32, 512:768], 0.0, lb[0:32, 512:768],
                                        ALU.max, ALU.add))
            V.tensor_tensor(sp_[0:32, 512:768], sp_[0:32, 512:768], k("keepn", 32), ALU.mult).then_inc(ss_sp, 1)
            dve.wait_ge(ss_tri, 1)
            dve.wait_ge(sb_w, 8)
            V.tensor_tensor(ab[:, 0:512], zb[:, 0:512], ps[:, 3, 0:512], ALU.add)
            V.tensor_tensor(ab[0:32, 512:768], zb[0:32, 512:768], ps[0:32, 4, 0:256], ALU.add).then_inc(ss_arg, 1)
            dve.wait_ge(ss_pv, 1)
            for g in range(2):
                half = slice(g * HD, (g + 1) * HD)
                ins = V.tensor_copy(oT[half, 0:4, TP:T].rearrange("p h (b t) -> p h b t", t=TS),
                                    ps[half, 7, 0:256].rearrange("p (h b g t) -> p h b g t", h=4, b=NB, g=2)[:, :, :, g, :])
            ins.then_inc(ss_o, 1)

            dve.wait_ge(nc_qk, 1)
            for g in range(2):
                ins = V.tensor_tensor(sc_[:, 8 * g:8 * g + 8, :],
                                      ps[:, 6 + g, 0:128].rearrange("p (a b) -> p a b", b=16)[:, :, 0:NC_],
                                      k("cbias").rearrange("p (a b) -> p a b", b=NC_)[:, 8 * g:8 * g + 8, :], ALU.add)
            link(ins)
            mx, tot = sm[:, 96:112], sm[:, 112:128]
            wide = lambda a: a.unsqueeze(2).to_broadcast([128, 16, NC_])
            link(V.tensor_reduce(mx, sc_[:, :, :], AX, ALU.max))
            V.tensor_tensor(sc_[:, :, :], sc_[:, :, :], wide(mx), ALU.subtract).then_inc(nc_s, 1)
            dve.wait_ge(nc_e, 1)
            v4 = sc_[:, :, :].rearrange("p (h w) n -> p h w n", w=2)
            cm = k("cmask").rearrange("p (w n) -> p w n", n=NC_).unsqueeze(1).to_broadcast([128, 8, 2, NC_])
            link(V.tensor_tensor(v4, v4, cm, ALU.mult))
            link(V.tensor_reduce(tot, sc_[:, :, :], AX, ALU.add))
            link(V.tensor_scalar(tot, tot, 1.0, None, ALU.max))
            link(V.reciprocal(tot, tot))
            gate = gnat[:, 0:2, :].rearrange("p w (h b) -> p h w b", b=3)
            link(V.tensor_tensor(mx.rearrange("p (h w) -> p h w", w=2), tot.rearrange("p (h w) -> p h w", w=2),
                                 gate[:, :, :, 0], ALU.mult))
            V.tensor_tensor(sc_[:, :, :], sc_[:, :, :], wide(mx), ALU.mult).then_inc(nc_p, 1)

            HEADS = [(n // 2, n % 2) for n in range(8)]

            def np_bias(n):
                r, g = HEADS[n]
                dve.wait_ge(np_qk, n + 1)
                if n >= 2:
                    dve.wait_ge(np_t, n - 1)
                else:
                    dve.wait_ge(ckv_sb, 2)
                b = 2 * (n % 2)
                x = (n % 2) * 16
                link(V.scalar_tensor_tensor(pb[:, n % 2, :, :], k("dist").unsqueeze(1).to_broadcast([128, 2, 384]),
                                            SLOPES[g * 4 + r], ps[:, b:b + 2, 0:384], ALU.mult, ALU.add))
                m = sm[:, x:x + 4].rearrange("p (b w) -> p b w", w=2)
                V.tensor_reduce(m[:, :, 0:1], pb[:, n % 2, :, 0:128], AX, ALU.max, negate=True)
                V.tensor_reduce(m[:, :, 1:2], pb[:, n % 2, :, 128:384], AX, ALU.max, negate=True).then_inc(np_s, 1)

            def np_scale(n):
                r, g = HEADS[n]
                h = g * 4 + r
                x = (n % 2) * 16
                dve.wait_ge(np_e, n + 1)
                link(V.reciprocal(sm[:, x + 4:x + 8], sm[:, x + 4:x + 8]))
                link(V.tensor_tensor(sm[:, x + 8:x + 12].rearrange("p (b w) -> p b w", w=2),
                                     sm[:, x + 4:x + 8].rearrange("p (b w) -> p b w", w=2),
                                     gnat[:, 0:2, 3 * h + 1:3 * h + 3].rearrange("p w b -> p b w"), ALU.mult))
                for br in range(2):
                    for tt, c in enumerate((slice(0, 128), slice(128, 384))):
                        y = x + 8 + 2 * br + tt
                        ins = V.tensor_scalar(pb[:, n % 2, br, c], pb[:, n % 2, br, c], sm[:, y:y + 1], None, ALU.mult)
                ins.then_inc(np_p, 1)

            def np_out(r):
                dve.wait_ge(np_pv, 2 * r + 2)
                V.tensor_copy(oT[:, 4 + r, 0:256], ps[:, 6 + r % 2, 0:256]).then_inc(np_o, 1)

            np_bias(0)
            for n in range(8):
                if n + 1 < 8:
                    np_bias(n + 1)
                np_scale(n)
                if n in (3, 5, 7):
                    np_out((n - 3) // 2)
            np_out(3)

            dve.wait_ge(ns_t, 1)
            tab = k("stab").rearrange("p (w s) -> p w s", w=2)
            for br in range(2):
                V.tensor_tensor(spb[:, br, :, :], ps[:, 4 + 2 * br:6 + 2 * br, 0:PAST + 32], tab, ALU.add)
            V.tensor_tensor(ssc[:, :, :], ps[:, 0, 0:32].rearrange("p (w n) -> p w n", n=16)[:, :, 0:NC_],
                            k("sctab").unsqueeze(1).to_broadcast([128, 2, NC_]), ALU.add)
            g3 = gtmp[:, :, :].rearrange("p w (h b) -> p w h b", b=3)
            link(V.tensor_tensor(g3, ps[:, 1, 0:48].rearrange("p (w h b) -> p w h b", h=8, b=3),
                                 k("rowhead").unsqueeze(1).unsqueeze(3).to_broadcast([128, 2, 8, 3]), ALU.mult))
            V.tensor_reduce(sm[:, 64:68].rearrange("p (b w) -> p b w", w=2), spb[:, :, :, :], AX, ALU.max, negate=True)
            V.tensor_reduce(grow[:, :, :], gtmp[:, :, :].rearrange("p w (h b) -> p w b h", b=3), AX, ALU.add)
            link(V.tensor_reduce(sm[:, 68:70], ssc[:, :, :], AX, ALU.max, negate=True))
            V.tensor_copy(sm[:, 88:90], sm[:, 68:70]).then_inc(ns_s, 1)
            dve.wait_ge(ns_e, 1)
            link(V.reciprocal(sm[:, 72:78], sm[:, 72:78]))
            V.tensor_tensor(sm[:, 80:84].rearrange("p (b w) -> p b w", w=2),
                            sm[:, 72:76].rearrange("p (b w) -> p b w", w=2),
                            grow[:, :, 1:3].rearrange("p w b -> p b w"), ALU.mult)
            link(V.tensor_tensor(sm[:, 84:86], sm[:, 76:78], grow[:, :, 0], ALU.mult))
            for w in range(2):
                for br in range(2):
                    y = 80 + 2 * br + w
                    V.tensor_scalar(spb[:, br, w, :], spb[:, br, w, :], sm[:, y:y + 1], None, ALU.mult)
                ins = V.tensor_scalar(ssc[:, w, :], ssc[:, w, :], sm[:, 84 + w:85 + w], None, ALU.mult)
            ins.then_inc(ns_p, 1)
            dve.wait_ge(ns_pv, 1)
            for g in range(2):
                half = slice(g * HD, (g + 1) * HD)
                ins = V.tensor_copy(oT[half, 4:8, TP:T].rearrange("p r (b t) -> p b r t", t=TS),
                                    ps[half, 4, 0:256].rearrange("p (b g r t) -> p b g r t", g=2, r=4, t=TS)[:, :, g, :, :])
            ins.then_inc(ns_o, 1)

            dve.wait_ge(rm_mm, 1)
            dve.wait_ge(small_in, 16 * 5)
            V.tensor_scalar(srow[:, :], ps[:, 0, 0:T], 1.0 / 512, EPS, ALU.mult, ALU.add)
            V.tensor_scalar(rrow[:, :], ps[:, 1, 0:T], 1.0 / 512, EPS, ALU.mult, ALU.add).then_inc(rm_sd, 1)
            dve.wait_ge(rm_sd, 2)
            V.reciprocal(srow[:, :], srow[:, :])
            link(V.reciprocal(rrow[:, :], rrow[:, :]))
            for c in range(KD):
                V.scalar_tensor_tensor(oT[:, c, :], oT[:, c, :], vec[:, 0, c:c + 1], (srow, rrow)[c // 4][:, :],
                                       ALU.mult, ALU.mult).then_inc(rm_on, 1)

            def norm(n, out, g, b):
                wide = lambda a: a.unsqueeze(1).to_broadcast([128, KD, T])
                dve.wait_ge(ln_mm, n + 1)
                link(V.tensor_scalar(srow[:, :], ps[:, 0, 0:T], 1.0 / D, None, ALU.mult))
                V.tensor_tensor(xTs[:, :, :], xTs[:, :, :], wide(srow[:, :]), ALU.subtract).then_inc(ln_c, 1)
                dve.wait_ge(ln_v, n + 1)
                V.tensor_scalar(srow[:, :], ps[:, 1, 0:T], 1.0 / D, EPS, ALU.mult, ALU.add).then_inc(ln_sd, 1)
                dve.wait_ge(ln_sd, 2 * n + 2)
                link(V.reciprocal(rrow[:, :], srow[:, :]))
                link(V.tensor_tensor(xTs[:, :, :], xTs[:, :, :], wide(rrow[:, :]), ALU.mult))
                for c in range(KD):
                    V.tensor_scalar(out[:, c, :], xTs[:, c, :], vec[:, g, c:c + 1], vec[:, b, c:c + 1],
                                    ALU.mult, ALU.add).then_inc(ln_h, 1)

            for c in range(KD):
                dve.wait_ge(m_mm, c + 1)
                V.scalar_tensor_tensor(xTs[:, c, :], xTs[:, c, :], ALPHA, ps[:, 4 + c % 4, 0:T],
                                       ALU.mult, ALU.add).then_inc(m_pre, 1)
            norm(0, hT, 1, 2)

            for tt, (t0, n) in enumerate(TOK):
                R = slice(0, n)
                dve.wait_ge(s_sb, tt + 1)

                def top16(values, out, where):
                    link(V.max(out[:, 0:8], values))
                    V.max_index(where[:, 0:8], out[:, 0:8], values)
                    link(V.match_replace(values, out[:, 0:8], values, -3.0e38))
                    link(V.max(out[:, 8:16], values))
                    link(V.max_index(where[:, 8:16], out[:, 8:16], values))

                for c in range(16):
                    top16(sT[R, tt, c, :], val[R, c // 2, c % 2, :], idx[R, c // 2, c % 2, :])
                link(V.tensor_copy(idf[R, :, :, :], idx[R, :, :, :]))
                s1, s2 = val[R, :, 0, :], val[R, :, 1, :]
                for i in range(5):
                    w = ROWLEN[i]
                    V.tensor_tensor(cand[R, :, ROWOFF[i]:ROWOFF[i] + w], s2[:, :, 0:w],
                                    s1[:, :, i:i + 1].to_broadcast([n, 8, w]), ALU.add)
                V.tensor_tensor(cand[R, :, ROWOFF[5]:ROWOFF[8]].rearrange("p h (i j) -> p h i j", j=2),
                                s1[:, :, 5:8].unsqueeze(3).to_broadcast([n, 8, 3, 2]),
                                s2[:, :, 0:2].unsqueeze(2).to_broadcast([n, 8, 3, 2]), ALU.add)
                link(V.tensor_tensor(cand[R, :, ROWOFF[8]:NCAND], s1[:, :, 8:16],
                                     s2[:, :, 0:1].to_broadcast([n, 8, 8]), ALU.add))
                for h in range(8):
                    top16(cand[R, h, :], topv[R, h, :], pos[R, h, :])
                V.tensor_tensor(pick[R, tt, 2, :].rearrange("p (h k) -> p h k", k=TOPK), topv[R, :, :],
                                topv[R, :, 0:1].to_broadcast([n, 8, TOPK]), ALU.subtract).then_inc(rt_exp_in, 1)
                link(V.tensor_copy(posf[R, :], pos[R, :, :].rearrange("p h k -> p (h k)")))
                V.tensor_copy(dlt[R, :, :, 0:1], idf[R, :, :, 0:1])
                link(V.tensor_tensor(dlt[R, :, :, 1:TOPK], idf[R, :, :, 1:TOPK], idf[R, :, :, 0:TOPK - 1], ALU.subtract))
                many = [n, 8 * TOPK, TOPK]
                link(V.tensor_tensor(step[R, :, :], posf[R, :].unsqueeze(2).to_broadcast(many),
                                     k("rowoff")[R, :].unsqueeze(1).to_broadcast(many), ALU.is_ge))

                def pick_from(out, steps):
                    link(V.tensor_tensor(prod[R, :, :].rearrange("p (h k) i -> p h k i", k=TOPK),
                                         step[R, :, :].rearrange("p (h k) i -> p h k i", k=TOPK), steps, ALU.mult))
                    link(V.tensor_reduce(out, prod[R, :, :], AX, ALU.add))

                four = [n, 8, TOPK, TOPK]
                pick_from(pick[R, tt, 0, :], dlt[R, :, 0, :].unsqueeze(2).to_broadcast(four))
                pick_from(rowo[R, :], k("rowlen")[R, :].unsqueeze(1).unsqueeze(1).to_broadcast(four))
                link(V.tensor_tensor(posf[R, :], posf[R, :], rowo[R, :], ALU.subtract))
                link(V.tensor_tensor(step[R, :, :], posf[R, :].unsqueeze(2).to_broadcast(many),
                                     k("iota")[R, 0:TOPK].unsqueeze(1).to_broadcast(many), ALU.is_ge))
                pick_from(pick[R, tt, 1, :], dlt[R, :, 1, :].unsqueeze(2).to_broadcast(four))
            for tt, (t0, n) in enumerate(TOK):
                R = slice(0, n)
                e = pick[R, tt, 2, :].rearrange("p (h k) -> p h k", k=TOPK)
                dve.wait_ge(rt_exp, tt + 1)
                link(V.tensor_reduce(ssum[R, tt, :], e, AX, ALU.add))
                link(V.reciprocal(ssum[R, tt, :], ssum[R, tt, :]))
                V.tensor_tensor(e, e, ssum[R, tt, :].unsqueeze(2).to_broadcast([n, 8, TOPK]), ALU.mult).then_inc(rt_pick, 1)

            dve.wait_ge(rt_slot, 3)
            GROUPS = T // 4

            def onehots(t, g):
                for a in range(4):
                    ins = V.tensor_scalar(onehot[:, g, a, 0, :], k("iota"), slotT[:, 0, t(a)], slotT[:, 2, t(a)],
                                          ALU.is_equal, ALU.mult)
                ins.then_inc(oh_a, 1)

            def weigh(tok, g):
                a = act_all[:, :, tok].rearrange("p j t -> p t j")
                V.tensor_tensor(a, a, ps[:, 4 + g, :].rearrange("p (t j) -> p t j", j=128),
                                ALU.mult).then_inc(g_mul, 1)

            dve.sem_inc(g_mul, 2)
            dve.wait_ge(u_act, 4 + NE)
            onehots(lambda a: slice(a, a + 1), 0)
            with dve.Fori(0, GROUPS // 2 - 1) as i:
                for g in range(2):
                    dve.wait_ge(g_mm, 2 * i + g + 2)
                    onehots(lambda a: bass.ds(8 * i + 4 * g + 4 + a, 1), 1 - g)
                    dve.wait_ge(g_mm, 2 * i + g + 3)
                    weigh(bass.ds(8 * i + 4 * g, 4), g)
            dve.wait_ge(g_mm, GROUPS)
            onehots(lambda a: slice(T - 4 + a, T - 3 + a), 1)
            dve.wait_ge(g_mm, GROUPS + 1)
            weigh(slice(T - 8, T - 4), 0)
            dve.wait_ge(g_mm, GROUPS + 2)
            weigh(slice(T - 4, T), 1)

            dve.wait_ge(f_mm, NE)
            for c in range(KD):
                V.scalar_tensor_tensor(xTs[:, c, :], hT[:, c, :], ALPHA, ps[:, c, 0:T],
                                       ALU.mult, ALU.add).then_inc(m_pre, 1)
            norm(1, xTs, 3, 4)




def lay_out(x_prompt, x_sample, cache_sb_kv, cache_nsa_kv, cache_win_kv, page_table, w_in, cmp_pe, cmp_w1,
            cmp_w2, mix_norm_g, w_out, ln1_g, ln1_b, peer_w_q, peer_sub_keys, peer_u, peer_v, ln2_g, ln2_b):
    f = np.ascontiguousarray
    np_ = lambda a: np.asarray(a)
    x = np.concatenate([np_(x_prompt).reshape(-1, D), np_(x_sample).reshape(-1, D)])
    feat = lambda a: a.reshape(a.shape[0], KD, 128).transpose(2, 1, 0)

    def tiles(w):
        return w.reshape(KD, 128, -1, 128).transpose(2, 1, 0, 3).reshape(w.shape[1] // 128, 128, D)

    swap = lambda a, ax: a.reshape(a.shape[:ax] + (2, 4, HD) + a.shape[ax + 1:]).swapaxes(ax, ax + 1).reshape(a.shape)
    w = np_(w_in)[0]
    qb, kb = QB * 128, CK * 128
    w = np.concatenate([w[:, :qb], swap(w[:, qb:kb], 1), w[:, kb:]], 1)
    wo = np_(w_out)[0]
    wo = np.concatenate([wo[:512], swap(wo[512:], 0)])
    mg = np_(mix_norm_g)[0]
    mg = np.concatenate([mg[:512], swap(mg[512:], 0)])
    vecs = np.stack([a.reshape(KD, 128).T for a in (mg, np_(ln1_g)[0], np_(ln1_b)[0], np_(ln2_g)[0], np_(ln2_b)[0])], 1)
    sb = np_(cache_sb_kv)[0]
    pages = sb.shape[0]
    kT = sb[:, :, 0].reshape(pages, 128, 4, 128).transpose(0, 3, 2, 1).reshape(pages, 128, 512)
    cache_sb = np.concatenate([kT, sb[:, :, 1].reshape(pages, 128, 512)], 2)
    ns = np_(cache_nsa_kv)[0]
    cache_nsa = np.concatenate([ns[:, :, 2].reshape(pages, 128, 128).transpose(0, 2, 1),
                                ns[:, :, 3].reshape(pages, 128, 128)], 2)
    cache_cmp = ns[:, :, 0:2].reshape(pages, 64, 2, 2, 2, HD).transpose(0, 2, 5, 4, 3, 1).reshape(pages, 128, 2, 2, 64)
    win = np_(cache_win_kv)[0].reshape(NB, PAST, 2, 128)
    win_kT = win[:, :, 0].transpose(2, 0, 1)
    win_v = win[:, :, 1].reshape(NB, 2, 128, 128).transpose(2, 0, 1, 3).reshape(128, NB, 256)
    return {
        "xT": f(feat(x)), "w_in": f(tiles(w[:, :GT * 128])),
        "w_gate": f(w[:, GT * 128:].reshape(KD, 128, 24).transpose(1, 0, 2)),
        "w_out": f(tiles(wo)), "w_q": f(tiles(np_(peer_w_q)[0])),
        "keysT": f(np_(peer_sub_keys)[0].reshape(16, 128, 128).transpose(2, 0, 1)),
        "uT": f(np_(peer_u)[0].reshape(128, 128, KD, 128).transpose(1, 3, 2, 0).reshape(128, 128, D)),
        "v": f(np_(peer_v)[0].reshape(128, 128, D).transpose(1, 0, 2)),
        "w1": f(np_(cmp_w1)[0].reshape(2, 16, 128, 128).transpose(2, 0, 1, 3)),
        "pe_cmp": f(np_(cmp_pe)[0].reshape(2, 16, 128).transpose(2, 0, 1)),
        "w2": f(np_(cmp_w2)[0].transpose(1, 0, 2)),
        "vecs": f(vecs), "cache_sb": f(cache_sb), "cache_nsa": f(cache_nsa), "cache_cmp": f(cache_cmp),
        "win_kv": f(np.concatenate([win_kT, win_v], 2)),
        "win_rows": f(win.reshape(NB, PAST, 256)), "page_table": f(np_(page_table).reshape(1, PAGES)),
        "consts": CONST_ARRAY,
    }


OUTPUTS = [((128, KD, T), "float32"), ((128, 14, T), "float32"), ((NB, PAST, 256), "float32")]


def take_out(y, kv, win):
    rows = lambda a: a.transpose(2, 1, 0).reshape(T, -1)
    y, kv = rows(y), rows(kv)
    sb, nsa, wn = kv[:, :1024], kv[:, 1024:1536], kv[:, 1536:]
    c = np.ascontiguousarray
    return (c(y[:TP].reshape(1, TP, D)), c(y[TP:].reshape(NB, TS, D)),
            c(sb[:TP].reshape(1, 1, TP, 2, 8, HD)), c(nsa[:TP].reshape(1, 1, TP, 4, 2, HD)),
            c(wn[:TP].reshape(1, 1, TP, 2, 2, HD)),
            c(sb[TP:].reshape(1, NB, TS, 2, 8, HD)), c(nsa[TP:].reshape(1, NB, TS, 4, 2, HD)),
            c(win.reshape(1, NB, PAST, 2, 2, HD)))


def kernel(**inputs):
    import concourse.bacc as bacc
    from concourse.bass_utils import run_bass_kernel_spmd

    arrays = lay_out(**inputs)
    nc = bacc.Bacc("TRN2", target_bir_lowering=False, num_devices=1)
    args = [nc.dram_tensor(f"in_{n}_dram", a.shape, mybir.dt.from_np(a.dtype), kind="ExternalInput").ap()
            for n, a in arrays.items()]
    outs = [nc.dram_tensor(f"out_{i}_dram", s, mybir.dt.from_np(np.dtype(d)), kind="ExternalOutput").ap()
            for i, (s, d) in enumerate(OUTPUTS)]
    trunk(nc, *args, *outs)
    got = run_bass_kernel_spmd(nc, [{f"in_{n}_dram": a for n, a in arrays.items()}], core_ids=[0]).results[0]
    return take_out(*(np.asarray(got[f"out_{i}_dram"]) for i in range(len(OUTPUTS))))
```

```python
from contextlib import ExitStack

import numpy as np

import concourse.bass as bass
from concourse import mybir

F32 = mybir.dt.float32
F32R = mybir.dt.float32r
I32 = mybir.dt.int32
U32 = mybir.dt.uint32
ALU = mybir.AluOpType
ACT = mybir.ActivationFunctionType
AX = mybir.AxisListType.X

D = 1024
KD = D // 128
TP = 256
NB = 8
TS = 4
T = TP + NB * TS
TOK = [(0, 128), (128, 128), (256, 32)]
PAST = 256
PAGES = NB * 2
HD = 64
SCALE = HD ** -0.5
ALPHA = 2.0 ** 0.25
EPS = 1e-5
BIG = 1e30
NC_ = 15
NSEQ = 1 + NB
ZT = 23
KA, VA, QB, CK, SK, SV, WK, WV, GT = 4, 8, 12, 16, 18, 19, 20, 21, 22
NE = 128
TOPK = 16
ROWLEN = [TOPK // (i + 1) for i in range(TOPK)]
ROWOFF = [sum(ROWLEN[:i]) for i in range(TOPK)]
NCAND = sum(ROWLEN)
SLOPES = [2.0 ** (-(h + 1)) for h in range(8)]



def constants():
    c = {}
    s = np.arange(128)[:, None]
    t = np.arange(128)[None, :]
    c["ident"] = (s == t) * 1.0
    c["negtri"] = (s >= t) * -1.0
    c["negones"] = -np.ones((128, 128))
    c["ones"] = np.ones((128, 128))
    c["keep"] = (s < t) * 1.0
    c["block"] = np.where(s < t, 0.0, -BIG)
    q, k = s, t
    dist = lambda q, k: np.where(k <= q, -(q - k) * 1.0, -BIG)
    kk = np.arange(256)[None, :]
    c["dist"] = np.concatenate([dist(q, k), dist(q + 128, kk)], 1)
    cpos = np.arange(NC_) * 16 + 31
    bias = np.zeros((128, 8, 2, NC_))
    mask = np.zeros((128, 2, NC_))
    for tt in range(2):
        qp = np.arange(128)[:, None] + 128 * tt
        mask[:, tt] = cpos[None, :] <= qp
        for h in range(8):
            bias[:, h, tt] = np.where(cpos[None, :] <= qp, -SLOPES[h] * (qp - cpos[None, :]), -BIG)
    c["cbias"] = bias.reshape(128, -1)
    c["cmask"] = mask.reshape(128, -1)
    R = np.arange(128)
    rh, rt = (R % 32) // 4, R % 4
    tab = np.zeros((128, 2, PAST + 32))
    slope = np.array(SLOPES)[rh][:, None]
    for w in range(2):
        b = w * 4 + R // 32
        tab[:, w, :PAST] = -slope * (PAST + rt[:, None] - np.arange(PAST)[None, :])
        nb, nt = np.arange(32) // 4, np.arange(32) % 4
        ok = (nb[None, :] == b[:, None]) & (nt[None, :] <= rt[:, None])
        tab[:, w, PAST:] = np.where(ok, -slope * (rt[:, None] - nt[None, :]), -BIG)
    c["stab"] = tab.reshape(128, -1)
    c["sctab"] = -slope * (PAST + rt[:, None] - cpos[None, :])
    c["rowhead"] = (rh[:, None] == np.arange(8)[None, :]) * 1.0
    sel = np.zeros((128, 2, 128))
    for w in range(2):
        sel[(w * 4 + R // 32) * 4 + rt, w, R] = 1.0
    c["selrow"] = sel.reshape(128, -1)
    col = np.arange(256)
    cb, ct = (col % 64) // 8, col % 4
    r = np.arange(32)
    ok = (r[:, None] // 4 == cb[None, :]) & (r[:, None] % 4 < ct[None, :])
    c["keepn"] = np.concatenate([ok * 1.0, np.zeros((96, 256))])
    c["blockn"] = np.concatenate([np.where(ok, 0.0, -BIG), np.zeros((96, 256))])
    c["iota"] = np.broadcast_to(t * 1.0, (128, 128))
    off = np.array(ROWOFF, float)
    c["rowoff"] = np.broadcast_to(off, (128, 16))
    c["rowlen"] = np.broadcast_to(np.concatenate([[0.0], np.diff(off)]), (128, 16))
    order, at, parts = {}, 0, []
    last = ["ident", "ones", "iota", "rowoff", "rowlen"]
    for name, a in sorted(c.items(), key=lambda x: x[0] not in last):
        order[name] = (at, a.shape[1])
        parts.append(a)
        at += a.shape[1]
    return order, np.ascontiguousarray(np.concatenate(parts, 1).astype(np.float32))


CONST, CONST_ARRAY = constants()
NCONST = CONST_ARRAY.shape[1]
NLIVE = sum(CONST[n][1] for n in ("ident", "ones", "iota", "rowoff", "rowlen"))


def trunk(nc, xT, w_in, w_gate, w_out, w_q, keysT, uT, v, w1, pe_cmp, w2, vecs, cache_sb, cache_nsa,
          cache_cmp, win_kv, win_rows, page_table, consts,
          y_out, kv_out, win_out):
    ctx = ExitStack()
    with ctx:
        base = nc.sbuf_base if isinstance(nc.sbuf_base, int) else nc.sbuf_base()
        base = (base + 63) // 64 * 64
        placed = [0]

        def at(name, shape, where, dt=F32):
            return nc.alloc_sbuf_tensor_at(name, [shape[0]] + list(shape[1:]), dt, offset=base + 4 * where)

        def bump(words):
            placed[0] += (words + 15) // 16 * 16
            return placed[0] - (words + 15) // 16 * 16

        def words(*dims):
            n = 1
            for d in dims:
                n *= d
            return n

        at_con = bump(NCONST)
        con = at("con", [128, NCONST], at_con)
        vec = at("vec", [128, 5, KD], bump(5 * KD))
        pt = at("pt", [1, PAGES], bump(PAGES), I32)
        ring = at("ring", [128, 4, D], bump(4 * D))
        at_x = bump(KD * T)
        at_h = bump(KD * T)
        at_a = bump(NE * T)
        at_w1 = bump(4096)
        rest = bump(256)
        end = nc.sbuf_usable_end if isinstance(nc.sbuf_usable_end, int) else nc.sbuf_usable_end()
        assert base + 4 * placed[0] <= end, (base + 4 * placed[0], end)

        xTs = at("xTs", [128, KD, T], at_x)
        vnat = at("vnat", [128, 3, 6, 128], at_h)
        o = at_a
        kvs = at("kvs", [128, PAGES, 1024], o)
        winkv = kvs[:, 0:NB, 0:512]
        zss = ptss = kvs[:, NB:NB + 2, 0:512]
        o += PAGES * 1024
        nsk = at("nsk", [128, PAGES, 256], o)
        o += PAGES * 256
        at_cmp = o
        cmpT = at("cmpT", [128, 2 * NSEQ, 2, 128], o)
        o += 2 * 2 * NSEQ * 128
        zT = at("zT", [128, ZT, T], o)
        spb = at("spb", [128, 2, 2, PAST + 32], o + VA * T)
        o += ZT * T
        oT = at("oT", [128, KD, T], o)
        o += KD * T
        ckT = at("ckT", [128, NSEQ, NC_], o)
        o += 144
        cv = at("cv", [NC_, NSEQ, 128], o)
        o += NSEQ * 128
        hdn = at("hdn", [128, 2, 2 * NSEQ * NC_], o)
        o += 544
        qbd_a = at("qbd_a", [128, 4, NB, 8], o)
        o += 256
        qbd_b = at("qbd_b", [128, NB, 32], o)
        o += 256
        wg = at("wg", [128, KD, 24], o)
        o += 192
        knat = at("knat", [32, 128], o)
        o += 128
        grow = at("grow", [128, 2, 3], o)
        gtmp = at("gtmp", [128, 2, 24], o + 16)
        o += 64
        assert o <= at_a + NE * T, (o, at_a + NE * T)
        w1s = at("w1s", [128, 2, 16, 128], at_w1)
        pes = at("pes", [128, 2, 16], rest)
        w2s = at("w2s", [128, 2, HD], rest + 32)
        cb = at("cb", [128, 2], rest + 160)
        gnat = at("gnat", [128, 3, 24], rest + 176)
        zb = at("zb", [128, 768], at_cmp)
        lb = at("lb", [128, 768], at_cmp + 768)
        sp_ = at("sp_", [128, 768], at_cmp + 1536)
        ab = at("ab", [128, 768], at_cmp + 2304)
        wb = at("wb", [128, 768], at_cmp + 3072)
        ptc = at("ptc", [NC_, 8, TP], at_cmp)
        sc_ = at("sc_", [128, 16, NC_], at_cmp + 3840)
        zns = at("zns", [32, 2, 256], at_w1 + 3072)
        ptns = at("ptns", [32, 2, 256], at_w1 + 3072)
        zcs = at("zcs", [NC_, 256], at_w1 + 3584)
        ptcs = at("ptcs", [NC_, 256], at_w1 + 3584)
        ssc = at("ssc", [128, 2, NC_], at_w1 + 3840)
        sm = at("sm", [128, 160], at_w1 + 3872)
        pb = at("pb", [128, 2, 2, 384], at_w1)
        ptb = at("ptb", [128, 2, 2, 384], at_w1 + 1536)
        sqb = at("sqb", [128, KD, T], at_w1)
        srow = at("srow", [128, T], at_w1 + 2304)
        rrow = at("rrow", [128, T], at_w1 + 2592)

        h_hi = at("h_hi", [128, KD, T], at_h, F32R)
        h_lo = at("h_lo", [128, KD, T], at_con + NLIVE, F32R)
        assert NLIVE + KD * T <= NCONST
        far = at_a + NE * T - 4 * D
        w_hi = [at(f"w_hi{s}", [128, D], (at_w1 + s * D, far + (s - 2) * D)[s // 2], F32R) for s in range(4)]
        w_lo = [at(f"w_lo{s}", [128, D], (at_w1 + (2 + s) * D, far + s * D)[s // 2], F32R) for s in range(4)]
        keys = at("keys", [128, 16, 128], at_a)
        sT = at("sT", [128, 3, 16, 128], at_a + 2048)
        r0 = at_a + 2048 + 6144
        qT = at("qT", [128, 16, T], r0)
        r1 = r0 + 16 * T
        step = at("step", [128, 8 * TOPK, TOPK], r1)
        prod = at("prod", [128, 8 * TOPK, TOPK], r1 + 2048)
        r2 = r1 + 4096
        val = at("val", [128, 8, 2, TOPK], r2)
        idx = at("idx", [128, 8, 2, TOPK], r2 + 256, U32)
        idf = at("idf", [128, 8, 2, TOPK], r2 + 512)
        dlt = at("dlt", [128, 8, 2, TOPK], r2 + 768)
        cand = at("cand", [128, 8, NCAND], r2 + 1024)
        topv = at("topv", [128, 8, TOPK], r2 + 1424)
        pos = at("pos", [128, 8, TOPK], r2 + 1552, U32)
        posf = at("posf", [128, 8 * TOPK], r2 + 1680)
        rowo = at("rowo", [128, 8 * TOPK], r2 + 1808)
        ssum = at("ssum", [128, 3, 8], r2 + 1936)
        pick = at("pick", [128, 3, 3, 8 * TOPK], r2 + 1968)
        gates = at("gates", [128, NE, T], at_a)
        u_out = at("u_out", [128, 2, T], at_x)
        slotT = at("slotT", [128, 3, T], at_x + 2 * T)
        one_a = at("one_a", [128, 2, 2, 128], at_x + 5 * T)
        one_b = [at("one_b0", [128, 2, 128], at_x + 5 * T + 512), at("one_b1", [128, 2, 128], rest)]
        assert at_x + 5 * T + 768 <= at_h
        a_in = at("a_in", [128, 4, T], at_x)
        y_hi = at("y_hi", [128, 2, T], at_x + 4 * T, F32R)
        y_lo = at("y_lo", [128, 2, T], at_x + 6 * T, F32R)
        assert at_x + 8 * T <= at_h
        yT = at("yT", [128, KD, T], at_a)
        a_dram = nc.dram_tensor("activations", [NE, 128, T], F32, kind="Internal").ap()

        ps = ctx.enter_context(nc.psum_tensor("ps", [128, 8, 512], F32))

        def k(name, rows=128):
            a, n = CONST[name]
            return con[0:rows, a:a + n]

        def sem(name):
            return ctx.enter_context(nc.semaphore(name))

        con_in, x_in, small_in, pt_in, page_in, win_in, keys_in = map(
            sem, ("con_in", "x_in", "small_in", "pt_in", "page_in", "win_in", "keys_in"))
        full = [sem(f"ring_full{r}") for r in range(4)]
        z_mm, z_sb, v_mm, v_sb, gate_sb, q_ready, cmp_ready, zero_done = map(sem, (
            "z_mm", "z_sb", "v_mm", "v_sb", "gate_sb", "q_ready", "cmp_ready", "zero_done"))
        cb_mm, ch_mm, ch_sb, ckv_mm, ckv_sb = map(sem, ("cb_mm", "ch_mm", "ch_sb", "ckv_mm", "ckv_sb"))
        sb_qk, sb_zc, sb_ln, sb_sp, sb_tri, sb_arg, sb_w, sb_pv, sb_o = map(sem, (
            "sb_qk", "sb_zc", "sb_ln", "sb_sp", "sb_tri", "sb_arg", "sb_w", "sb_pv", "sb_o"))
        ss_half, ss_qk, ss_ln, ss_sp, ss_tri, ss_arg, ss_w, ss_pv, ss_o = map(sem, (
            "ss_half", "ss_qk", "ss_ln", "ss_sp", "ss_tri", "ss_arg", "ss_w", "ss_pv", "ss_o"))
        nc_qk, nc_s, nc_e, nc_p, nc_t, nc_pt = map(sem, ("nc_qk", "nc_s", "nc_e", "nc_p", "nc_t", "nc_pt"))
        np_qk, np_s, np_e, np_p, np_t, np_pt, np_pv, np_o = map(sem, (
            "np_qk", "np_s", "np_e", "np_p", "np_t", "np_pt", "np_pv", "np_o"))
        ns_qk, ns_z, ns_t, ns_s, ns_e, ns_p, ns_tb, ns_pt, ns_pv, ns_o = map(sem, (
            "ns_qk", "ns_z", "ns_t", "ns_s", "ns_e", "ns_p", "ns_tb", "ns_pt", "ns_pv", "ns_o"))
        rm_sq, rm_mm, rm_sd, rm_on = map(sem, ("rm_sq", "rm_mm", "rm_sd", "rm_on"))
        m_mm, m_pre = map(sem, ("m_mm", "m_pre"))
        ln_mm, ln_c, ln_sq, ln_v, ln_sd, ln_g, ln_h = map(sem, (
            "ln_mm", "ln_c", "ln_sq", "ln_v", "ln_sd", "ln_g", "ln_h"))
        h_h, h_l, q_sb, s_mm, s_sb = map(sem, ("h_h", "h_l", "q_sb", "s_mm", "s_sb"))
        part_hi, part_lo, w_mm = map(sem, ("part_hi", "part_lo", "w_mm"))
        rt_exp_in, rt_exp, rt_pick, rt_t, rt_slot = map(sem, ("rt_exp_in", "rt_exp", "rt_pick", "rt_t", "rt_slot"))
        u_act, one_ready, g_mm, g_sb = map(sem, ("u_act", "one_ready", "g_mm", "g_sb"))
        spill = [sem(f"spill{r}") for r in range(2)]
        a_full = [sem(f"a_full{r}") for r in range(4)]
        y_mul, y_h, y_l = map(sem, ("y_mul", "y_h", "y_l"))
        dve_link, act_link = map(sem, ("dve_link", "act_link"))
        out_y, out_kv, out_win = map(sem, ("out_y", "out_kv", "out_win"))

        N_IN, N_OUT, N_Q = GT, KD, 16
        AT_OUT, AT_Q = N_IN, N_IN + N_OUT
        AT_U = AT_Q + N_Q
        AT_V = AT_U + NE

        def filled(n):
            return n % 4, 16 * (n // 4 + 1)

        M_U, M_V = N_Q, N_Q + NE
        U_ALONE = NE - T // 8

        def freed_by(n):
            for first, mine, per in ((AT_Q, part_lo, 2), (AT_OUT, m_mm, 1), (0, z_mm, 1)):
                if n >= first:
                    return mine, per * (n - first + 1)

        block = ctx.enter_context(nc.Block())

        @block.sync
        def _(sp):
            sp.dma_start(xTs[:, :, :], xT).then_inc(x_in, 16)

            def load(n, src):
                if n >= 4:
                    sp.wait_ge(*freed_by(n - 4))
                sp.dma_start(ring[:, n % 4, :], src).then_inc(full[n % 4], 16)

            for n in range(4):
                load(n, w_in[n])
            sp.dma_start(con[:, :], consts).then_inc(con_in, 16)
            for n in range(4, N_IN):
                load(n, w_in[n])
            for n in range(N_OUT):
                load(AT_OUT + n, w_out[n])
            for n in range(N_Q):
                load(AT_Q + n, w_q[n])

            tile = lambda t, i, r: t[bass.ds(4 * i + r, 1)].rearrange("a p c -> (a p) c")

            def store(r, act_done, dst):
                sp.wait_ge(u_act, act_done)
                sp.dma_start(dst, u_out[:, r % 2, :]).then_inc(spill[r % 2], 16)

            for n in range(8):
                load(AT_U + n, uT[n])
                if n >= 6:
                    store(n, 4 + n - 5, a_dram[n - 6])
            with sp.Fori(2, NE // 4) as i:
                for r in range(4):
                    sp.wait_ge(part_lo, 8 * i + 2 * (M_U + r - 3))
                    sp.dma_start(ring[:, (AT_U + r) % 4, :], tile(uT, i, r)).then_inc(full[(AT_U + r) % 4], 16)
                    store(r, 4 * i + r - 1, tile(a_dram, i - 2 + r // 2, (r + 2) % 4))
            for n in range(NE, NE + 6):
                if n < NE + 4:
                    load(AT_U + n, v[n - NE])
                store(n, 4 + n - 5, a_dram[n - 6])
            for r in range(2):
                sp.wait_ge(spill[r], 16 * NE // 2)
            sp.wait_ge(g_mm, 2 + T // 2)
            for r in range(4):
                sp.dma_start(a_in[:, r, :], a_dram[r]).then_inc(a_full[r], 16)
            with sp.Fori(1, NE // 4) as i:
                for r in range(4):
                    sp.wait_ge(part_lo, 8 * i + 2 * (M_V + r - 3))
                    sp.dma_start(ring[:, (AT_V + r) % 4, :], tile(v, i, r)).then_inc(full[(AT_V + r) % 4], 16)
                    sp.wait_ge(y_l, 4 * i + r - 3)
                    sp.dma_start(a_in[:, r, :], tile(a_dram, i, r)).then_inc(a_full[r], 16)
            for c in range(0, KD, 2):
                sp.wait_ge(ln_h, c + 2)
                sp.dma_start(y_out[:, c:c + 2, :], sqb[:, c:c + 2, :]).then_inc(out_y, 16)
            sp.wait_ge(out_y, 16 * KD // 2)
            sp.wait_ge(out_kv, 32)
            sp.wait_ge(out_win, 48)

        @block.gpsimd
        def _(pool):
            pool.dma_start(pt[:, :], page_table).then_inc(pt_in, 16)
            pool.dma_start(w1s[:, :, :, :], w1).then_inc(small_in, 16)
            pool.dma_start(pes[:, :, :], pe_cmp).then_inc(small_in, 16)
            pool.dma_start(w2s[:, :, :], w2).then_inc(small_in, 16)
            pool.dma_start(vec[:, :, :], vecs).then_inc(small_in, 16)
            pool.dma_start(wg[:, :, :], w_gate).then_inc(small_in, 16)
            nc.gpsimd.memset(qbd_a[:, :, :, :], 0.0)
            nc.gpsimd.memset(qbd_b[:, :, :], 0.0).then_inc(zero_done, 1)
            pool.wait_ge(pt_in, 16)
            for b in range(NB):
                for p in range(2):
                    n = 2 * b + p
                    page = nc.gpsimd.value_load(pt[0:1, n:n + 1], min_val=0, max_val=cache_sb.shape[0] - 1)
                    src = lambda t: t[bass.ds(page, 1)]
                    pool.dma_start(cmpT[:, 2 + 2 * b:4 + 2 * b, :, 64 * p:64 * p + 64].rearrange("p g k n -> p (g k) n"),
                                   src(cache_cmp).rearrange("a p g k n -> (a p) (g k) n")).then_inc(page_in, 16)
                    pool.dma_start(kvs[:, n, :], src(cache_sb).rearrange("a p c -> (a p) c")).then_inc(page_in, 16)
                    pool.dma_start(nsk[:, n, :], src(cache_nsa).rearrange("a p c -> (a p) c")).then_inc(page_in, 16)
            pool.dma_start(win_out[:, 0:PAST - TS, :], win_rows[:, TS:PAST, :]).then_inc(out_win, 16)
            pool.wait_ge(z_sb, 4 + ZT)
            pool.dma_start(kv_out[:, 0:8, :], zT[:, KA:KA + 8, :]).then_inc(out_kv, 16)
            pool.dma_start(kv_out[:, 8:14, :], zT[:, CK:CK + 6, :]).then_inc(out_kv, 16)
            pool.wait_ge(v_sb, 3)
            pool.dma_start(win_out[:, PAST - TS:PAST, 0:128], knat[:, :]).then_inc(out_win, 16)
            pool.dma_start(win_out[:, PAST - TS:PAST, 128:256], vnat[0:32, 2, 5, :]).then_inc(out_win, 16)
            pool.wait_ge(ss_half, 1)
            pool.dma_start(winkv, win_kv).then_inc(win_in, 16)
            pool.wait_ge(h_l, KD)
            pool.dma_start(keys[:, :, :], keysT).then_inc(keys_in, 16)
        @block.tensor
        def _(pe):
            mm = nc.tensor.matmul
            ident = k("ident")

            pe.sem_inc(g_mm, 2)
            pe.wait_ge(x_in, 16)

            def project(r, bank, rhs, out_rows=128):
                for kd in range(KD):
                    ins = mm(ps[:, bank, 0:T], ring[:, r, kd * 128:(kd + 1) * 128], rhs[:, kd, :],
                             start=kd == 0, stop=kd == KD - 1)
                return ins

            with pe.Fori(0, 5) as i:
                for r in range(4):
                    pe.wait_ge(full[r], 16 * i + 16)
                    pe.wait_ge(z_sb, 4 * i + r + 1)
                    ins = project(r, r, xTs)
                    ins.then_inc(z_mm, 1)
            for c in range(20, N_IN):
                slot, value = filled(c)
                pe.wait_ge(full[slot], value)
                pe.wait_ge(z_sb, c + 1)
                ins = project(c % 4, c % 4, xTs)
                ins.then_inc(z_mm, 1)
            pe.wait_ge(small_in, 16 * 5)
            pe.wait_ge(z_sb, GT + 1)
            for kd in range(KD):
                ins = mm(ps[0:24, 2, 0:T], wg[:, kd, :], xTs[:, kd, :], start=kd == 0, stop=kd == KD - 1)
            ins.then_inc(z_mm, 1)

            pe.wait_ge(con_in, 16)
            pe.wait_ge(z_sb, 4 + ZT)
            for tt, (t0, n) in enumerate(TOK):
                a, b = (4, 6, 0)[tt], (5, 7, 1)[tt]
                tok = slice(t0, t0 + n)
                for j in range(4):
                    nc.tensor.transpose(ps[0:n, a, j * 128:(j + 1) * 128], zT[:, VA + j, tok], ident)
                nc.tensor.transpose(ps[0:n, b, 0:128], zT[:, SV, tok], ident)
                nc.tensor.transpose(ps[0:n, b, 128:256], zT[:, WV, tok], ident)
                if tt == 2:
                    nc.tensor.transpose(ps[0:n, b, 256:384], zT[:, WK, tok], ident)
                nc.tensor.transpose(ps[0:n, b, 384:408], zT[0:24, GT, tok], ident[0:24, 0:24]).then_inc(v_mm, 1)

            for j in range(2):
                for m in range(16):
                    ins = mm(ps[:, 2, j:j + 1], w1s[:, j, m, :], pes[:, j, m:m + 1], start=m == 0, stop=m == 15)
            ins.then_inc(cb_mm, 1)
            pe.wait_ge(cmp_ready, 1)
            pe.wait_ge(page_in, 16 * 3 * PAGES)
            for j in range(2):
                for m in range(16):
                    blocks = cmpT[:, :, j, m:m + 8 * (NC_ - 1) + 1:8]
                    ins = mm(ps[:, 3 + j, 0:2 * NSEQ * NC_], w1s[:, j, m, :], blocks, start=m == 0, stop=m == 15)
                ins.then_inc(ch_mm, 1)
                if j == 0:
                    pe.wait_ge(v_sb, 1)
            pe.wait_ge(ch_sb, 1)
            pe.wait_ge(v_sb, 3)
            hd = hdn[:, :, :].rearrange("p j (s g n) -> p j s g n", g=2, n=NC_)
            for g in range(2):
                ins = mm(ps[g * HD:(g + 1) * HD, 5, 0:NSEQ * NC_], w2s[:, 0, :], hd[:, 0, :, g, :],
                         start=True, stop=True)
            ins.then_inc(ckv_mm, 1)
            pe.wait_ge(ch_sb, 2)
            for s in range(NSEQ):
                for g in range(2):
                    c = (s % 4) * 128 + g * HD
                    ins = mm(ps[0:NC_, (6, 7, 0)[s // 4], c:c + HD], hd[:, 1, s, g, :], w2s[:, 1, :],
                             start=True, stop=True)
            ins.then_inc(ckv_mm, 1)

            pe.wait_ge(q_ready, 1)
            pe.wait_ge(ckv_sb, 2)

            def sb_scores(h):
                if h >= 2:
                    pe.wait_ge(sb_zc, h - 1)
                hp, half = h // 2, slice((h % 2) * HD, (h % 2 + 1) * HD)
                b = 1 + h % 2
                mm(ps[:, b, 0:256], zT[half, KA + hp, 0:128], zT[half, hp, 0:256], start=True, stop=True)
                mm(ps[:, b, 256:384], zT[half, KA + hp, 128:256], zT[half, hp, 128:256],
                   start=True, stop=True).then_inc(sb_qk, 1)

            def sb_sums(h):
                pe.wait_ge(sb_sp, h + 1)
                if h >= 2:
                    pe.wait_ge(sb_arg, h - 1)
                b, x = 3 + h % 2, (h % 2) * 384
                mm(ps[:, b, 0:256], k("negtri"), sp_[:, x:x + 256], start=True, stop=False)
                mm(ps[:, b, 128:256], k("negones"), sp_[:, x + 256:x + 384], start=False, stop=False)
                mm(ps[:, b, 0:128], ident, k("block"), start=False, stop=True)
                mm(ps[:, b, 256:384], k("negtri"), sp_[:, x + 256:x + 384], start=True, stop=False)
                mm(ps[:, b, 256:384], ident, k("block"), start=False, stop=True).then_inc(sb_tri, 1)

            def sb_values(h):
                pe.wait_ge(sb_w, h + 1)
                hp, x = h // 2, (h % 2) * 384
                if h % 2 == 0 and hp >= 2:
                    pe.wait_ge(sb_o, hp - 1)
                half = slice((h % 2) * HD, (h % 2 + 1) * HD)
                b = 5 + hp % 2
                mm(ps[half, b, 0:256], vnat[:, 0, hp, half], wb[:, x:x + 256], start=True, stop=False)
                mm(ps[half, b, 128:256], vnat[:, 1, hp, half], wb[:, x + 256:x + 384],
                   start=False, stop=True).then_inc(sb_pv, 1)

            sb_scores(0)
            sb_scores(1)
            sb_sums(0)
            for h in range(8):
                if h + 2 < 8:
                    sb_scores(h + 2)
                for p in range(2):
                    for hp in range(4):
                        c = p * 256 + hp * 64 + h * 8
                        ins = mm(ps[:, 0, c:c + 8], kvs[:, 2 * h + p, hp * 128:(hp + 1) * 128], qbd_a[:, hp, h, :],
                           start=True, stop=True)
                if h == 3:
                    ins.then_inc(ss_half, 1)
                if h + 1 < 8:
                    sb_sums(h + 1)
                sb_values(h)
            for hp in range(4):
                ins = mm(ps[0:32, 7, hp * 64:(hp + 1) * 64], zT[:, KA + hp, TP:T],
                         qbd_a[:, hp, :, :], start=True, stop=True)
            ins.then_inc(ss_qk, 1)

            pe.wait_ge(sb_o, 4)
            for h in range(8):
                r, g = h % 4, slice((h // 4) * HD, (h // 4 + 1) * HD)
                for tt in range(2):
                    c = (2 * r + tt) * 16
                    ins = mm(ps[:, 5 + h // 4, c:c + NC_], zT[g, QB + r, tt * 128:(tt + 1) * 128], ckT[g, 0, :],
                             start=True, stop=True)
            ins.then_inc(nc_qk, 1)

            pe.wait_ge(sb_zc, 8)
            pe.wait_ge(win_in, 16)

            def ns_scores(b):
                for p in range(2):
                    c = p * 256 + b * 32
                    mm(ps[:, 1, c:c + 32], nsk[:, 2 * b + p, 0:128], qbd_b[:, b, :], start=True, stop=True)
                    mm(ps[:, 2, c:c + 32], winkv[:, b, p * 128:(p + 1) * 128], qbd_b[:, b, :], start=True, stop=True)

            for b in range(5):
                ns_scores(b)
            pe.wait_ge(ss_sp, 1)
            pe.wait_ge(sb_arg, 8)
            mm(ps[:, 3, 0:512], k("negtri"), sp_[:, 0:512], start=True, stop=False)
            mm(ps[:, 3, 0:256], k("negones"), sp_[:, 256:512], start=False, stop=False)
            mm(ps[:, 3, 0:256], k("negones", 32), sp_[0:32, 512:768], start=False, stop=False)
            mm(ps[:, 3, 256:512], k("negones", 32), sp_[0:32, 512:768], start=False, stop=True)
            mm(ps[0:32, 4, 0:256], k("negtri", 32)[:, 0:32], sp_[0:32, 512:768], start=True, stop=False)
            mm(ps[0:32, 4, 0:256], ident[0:32, 0:32], k("blockn", 32), start=False, stop=True).then_inc(ss_tri, 1)
            for b in range(5, NB):
                ns_scores(b)
            for b in range(NB):
                mm(ps[0:NC_, 0, b * 32:(b + 1) * 32], ckT[:, 1 + b, :], qbd_b[:, b, :], start=True, stop=True)
            for br, kt in enumerate((SK, WK)):
                ins = mm(ps[0:32, 7, br * 256:(br + 1) * 256], zT[:, kt, TP:T], qbd_b[:, :, :], start=True, stop=True)
            ins.then_inc(ns_qk, 1)

            pe.wait_ge(nc_p, 1)
            pe.wait_ge(ss_arg, 1)
            for h in range(8):
                for tt in range(2):
                    ins = nc.tensor.transpose(ps[0:NC_, 3 + h // 2, (h % 2) * 256 + tt * 128:(h % 2) * 256 + (tt + 1) * 128],
                                              sc_[:, 2 * h + tt, :], ident)
            ins.then_inc(nc_t, 1)

            pe.wait_ge(ns_z, 1)
            for w in range(2):
                nc.tensor.transpose(ps[:, 2, w * 16:w * 16 + NC_], zcs[:, w * 128:(w + 1) * 128], ident[0:NC_, 0:NC_])
            pe.wait_ge(nc_pt, 1)
            for w in range(2):
                mm(ps[:, 3, w * 24:(w + 1) * 24], k("selrow", 32)[:, w * 128:(w + 1) * 128], gnat[0:32, 2, :],
                   start=True, stop=True)
            for br in range(2):
                for w in range(2):
                    b = 4 + 2 * br + w
                    for p in range(2):
                        nc.tensor.transpose(ps[:, b, p * 128:(p + 1) * 128],
                                            zss[:, br, p * 256 + w * 128:p * 256 + (w + 1) * 128], ident)
                    ins = nc.tensor.transpose(ps[:, b, 256:288], zns[:, br, w * 128:(w + 1) * 128], ident[0:32, 0:32])
            ins.then_inc(ns_t, 1)

            HEADS = [(n // 2, n % 2) for n in range(8)]

            def np_scores(n):
                r, g = HEADS[n]
                half = slice(g * HD, (g + 1) * HD)
                if n >= 2:
                    pe.wait_ge(np_s, n - 1)
                elif n == 1:
                    pe.wait_ge(ns_s, 1)
                for br, kt in enumerate((SK, WK)):
                    b = 2 * (n % 2) + br
                    mm(ps[:, b, 0:128], zT[half, QB + r, 0:128], zT[half, kt, 0:128], start=True, stop=True)
                    ins = mm(ps[:, b, 128:384], zT[half, QB + r, 128:256], zT[half, kt, 0:256],
                             start=True, stop=True)
                ins.then_inc(np_qk, 1)

            def np_turn(n):
                pe.wait_ge(np_p, n + 1)
                if n >= 1:
                    pe.wait_ge(np_pt, n)
                else:
                    pe.wait_ge(ns_s, 1)
                for br in range(2):
                    for c in range(3):
                        ins = nc.tensor.transpose(ps[:, 4 + br, c * 128:(c + 1) * 128],
                                                  pb[:, n % 2, br, c * 128:(c + 1) * 128], ident)
                ins.then_inc(np_t, 1)

            def np_values(n):
                r, g = HEADS[n]
                half = slice(g * HD, (g + 1) * HD)
                h = g * 4 + r
                b = 6
                pe.wait_ge(np_pt, n + 1)
                if g == 0 and r >= 1:
                    pe.wait_ge(np_o, r)
                mm(ps[half, b, 0:256], cv[:, 0, half], ptc[:, h, :], start=True, stop=False)
                for br in range(2):
                    mm(ps[half, b, 0:256], vnat[:, 0, 4 + br, half], ptb[:, n % 2, br, 0:256], start=False, stop=False)
                    ins = mm(ps[half, b, 128:256], vnat[:, 1, 4 + br, half], ptb[:, n % 2, br, 256:384],
                             start=False, stop=br == 1)
                ins.then_inc(np_pv, 1)

            def ss_values(n):
                hp = n // 2
                if n % 2 == 0:
                    mm(ps[:, 7, hp * 64:(hp + 1) * 64], vnat[0:32, 2, hp, :], wb[0:32, 512 + hp * 64:576 + hp * 64],
                       start=True, stop=False)
                for b in range(n % 2 * 4, n % 2 * 4 + 4):
                    for p in range(2):
                        c = hp * 64 + b * 8
                        ins = mm(ps[:, 7, c:c + 8], kvs[:, 2 * b + p, 512 + hp * 128:640 + hp * 128],
                                 wb[:, p * 256 + c:p * 256 + c + 8], start=False, stop=(b == NB - 1 and p == 1))
                if n == 7:
                    ins.then_inc(ss_pv, 1)

            np_scores(0)
            np_scores(1)
            pe.wait_ge(ss_w, 1)
            for n in range(9):
                if n < 8:
                    np_turn(n)
                if n + 2 < 8:
                    np_scores(n + 2)
                if n < 8:
                    ss_values(n)
                if n >= 1:
                    np_values(n - 1)

            pe.wait_ge(ns_p, 1)
            pe.wait_ge(np_s, 8)
            for w in range(2):
                for br in range(2):
                    for p in range(2):
                        nc.tensor.transpose(ps[:, 2 + br, p * 256 + w * 128:p * 256 + (w + 1) * 128],
                                            spb[:, br, w, p * 128:(p + 1) * 128], ident)
                    nc.tensor.transpose(ps[0:32, 0, br * 256 + w * 128:br * 256 + (w + 1) * 128],
                                        spb[:, br, w, 256:288], ident)
                ins = nc.tensor.transpose(ps[0:NC_, 1, w * 128:(w + 1) * 128], ssc[:, w, :], ident)
            ins.then_inc(ns_tb, 1)
            pe.wait_ge(ns_pt, 1)
            pe.wait_ge(np_pt, 8)
            for br in range(2):
                mm(ps[:, 4, 0:256], vnat[0:32, 2, 4 + br, :], ptns[:, br, :], start=br == 0, stop=False)
            for b in range(NB):
                c = slice(b * 32, (b + 1) * 32)
                for p in range(2):
                    pc = slice(p * 256 + b * 32, p * 256 + (b + 1) * 32)
                    mm(ps[:, 4, c], nsk[:, 2 * b + p, 128:256], ptss[:, 0, pc], start=False, stop=False)
                    mm(ps[:, 4, c], winkv[:, b, 256 + p * 128:384 + p * 128], ptss[:, 1, pc], start=False, stop=False)
                ins = mm(ps[:, 4, c], cv[:, 1 + b, :], ptcs[:, b * 32:(b + 1) * 32], start=False, stop=b == NB - 1)
            ins.then_inc(ns_pv, 1)

            pe.wait_ge(rm_sq, 1)
            for m in range(2):
                for j in range(4):
                    ins = mm(ps[:, m, 0:T], k("ones"), sqb[:, 4 * m + j, :], start=j == 0, stop=j == 3)
            ins.then_inc(rm_mm, 1)
            pe.wait_ge(rm_on, KD)
            for c in range(KD):
                slot, value = filled(AT_OUT + c)
                pe.wait_ge(full[slot], value)
                if c >= 4:
                    pe.wait_ge(m_pre, c - 3)
                ins = project(slot, 4 + c % 4, oT)
                ins.then_inc(m_mm, 1)

            def norm_sums(n, x):
                for c in range(KD):
                    pe.wait_ge(m_pre, KD * n + c + 1)
                    ins = mm(ps[:, 0, 0:T], k("ones"), x[:, c, :], start=c == 0, stop=c == KD - 1)
                ins.then_inc(ln_mm, 1)
                for c in range(KD):
                    pe.wait_ge(ln_sq, KD * n + c + 1)
                    ins = mm(ps[:, 1, 0:T], k("ones"), sqb[:, c, :], start=c == 0, stop=c == KD - 1)
                ins.then_inc(ln_v, 1)

            norm_sums(0, xTs)

            def parts(slot, x_hi, x_lo, c, bank, start, stop):
                block_ = slice(c * 128, (c + 1) * 128)
                hi, lo = w_hi[slot][:, block_], w_lo[slot][:, block_]
                mm(ps[:, bank, 0:T], hi, x_hi, start=start, stop=False)
                mm(ps[:, bank, 0:T], hi, x_lo, start=False, stop=False)
                return mm(ps[:, bank, 0:T], lo, x_hi, start=False, stop=stop)

            def project_parts(slot, bank, lows, between=lambda kd: None):
                for kd in range(KD):
                    if kd % 4 == 0:
                        pe.wait_ge(part_lo, lows[kd // 4])
                    ins = parts(slot, h_hi[:, kd, :], h_lo[:, kd, :], kd, bank, kd == 0, kd == KD - 1)
                    if kd % 4 == 3:
                        ins.then_inc(w_mm, 1)
                    between(kd)

            def halves(i, m):
                return 8 * i + (2 * m + 1), 8 * i + (2 * m + 2)

            pe.wait_ge(h_l, KD)
            with pe.Fori(0, N_Q // 4) as i:
                for r in range(4):
                    pe.wait_ge(q_sb, 4 * i + r + 1)
                    project_parts(r, r, halves(i, r))
            pe.wait_ge(keys_in, 16)
            pe.wait_ge(q_sb, 4 + 16)
            for tt, (t0, n) in enumerate(TOK):
                if tt:
                    pe.wait_ge(s_sb, tt)
                for c in range(16):
                    ins = mm(ps[0:n, 4 + c // 4, (c % 4) * 128:(c % 4 + 1) * 128], qT[:, c, t0:t0 + n],
                             keys[:, c, :], start=True, stop=True)
                ins.then_inc(s_mm, 1)
                if tt < 2:
                    for r in (2 * tt, 2 * tt + 1):
                        pe.wait_ge(u_act, r + 1)
                        project_parts(r, r, halves(0, M_U + r))

            def experts_up(first, last):
                with pe.Fori(first, last) as i:
                    for r in range(4):
                        pe.wait_ge(u_act, 4 * i + r + 1)
                        project_parts(r, r, halves(i, M_U + r))

            experts_up(1, U_ALONE // 4 - 1)
            pe.wait_ge(rt_pick, 3)
            pe.wait_ge(s_sb, 3)
            for c in range(3):
                for tt, (t0, n) in enumerate(TOK):
                    ins = nc.tensor.transpose(ps[:, 4 + c, t0:t0 + n], pick[0:n, tt, c, :], ident[0:n, 0:n])
                ins.then_inc(rt_t, 1)
            experts_up(U_ALONE // 4 - 1, U_ALONE // 4)

            pe.wait_ge(rt_slot, 3)
            with pe.Fori(0, T // 32) as i:
                for r in range(4):
                    def pair(kd):
                        if kd % 2 == 0:
                            return
                        q = kd // 2
                        pe.wait_ge(one_ready, 16 * i + (4 * r + q + 1))
                        if q % 2 == 0:
                            pe.wait_ge(g_sb, 8 * i + (2 * r + q // 2 + 1))
                        for t in range(2):
                            c = (q % 2) * 256 + t * 128
                            ins = mm(ps[:, 4 + (2 * r + q // 2) % 4, c:c + 128], one_a[:, q % 2, t, :],
                                     one_b[q % 2][:, t, :], start=True, stop=True)
                        ins.then_inc(g_mm, 1)

                    pe.wait_ge(u_act, 4 * i + (U_ALONE + r + 1))
                    project_parts(r % 2, r, halves(i, M_U + U_ALONE + r), pair)

            pe.wait_ge(g_sb, 4 + T // 4)
            pe.wait_ge(u_act, 4 + NE)

            def experts_down(r, lows, ready, start, stop):
                pe.wait_ge(y_l, ready)
                for c in range(KD):
                    if c % 4 == 0:
                        pe.wait_ge(part_lo, lows[c // 4])
                    ins = parts(r % 2, y_hi[:, r % 2, :], y_lo[:, r % 2, :], c, c, start, stop)
                    if c % 4 == 3:
                        ins.then_inc(w_mm, 1)

            for r in range(4):
                experts_down(r, halves(0, M_V + r), r + 1, r == 0, False)
            with pe.Fori(1, NE // 4 - 1) as i:
                for r in range(4):
                    experts_down(r, halves(i, M_V + r), 4 * i + r + 1, False, False)
            for r in range(4):
                experts_down(r, halves(0, M_V + NE - 4 + r), NE - 3 + r, False, r == 3)
            norm_sums(1, yT)

        @block.scalar
        def _(act):
            A = nc.scalar.activation
            done = [0]

            def link(ins):
                done[0] += 1
                ins.then_inc(act_link, 1)
                act.wait_ge(act_link, done[0])

            act.sem_inc(z_sb, 4)
            with act.Fori(0, 5) as i:
                for r in range(4):
                    act.wait_ge(z_mm, 4 * i + r + 1)
                    nc.scalar.copy(zT[:, bass.ds(4 * i + r, 1), :], ps[:, r:r + 1, 0:T]).then_inc(z_sb, 1)
            for c in range(20, GT):
                act.wait_ge(z_mm, c + 1)
                nc.scalar.copy(zT[:, c, :], ps[:, c % 4, 0:T]).then_inc(z_sb, 1)
            act.wait_ge(z_mm, ZT)
            nc.scalar.copy(zT[0:24, GT, :], ps[0:24, 2, 0:T]).then_inc(z_sb, 1)

            for tt, (t0, n) in enumerate(TOK):
                a, b = (4, 6, 0)[tt], (5, 7, 1)[tt]
                act.wait_ge(v_mm, tt + 1)
                nc.scalar.copy(vnat[0:n, tt, 0:4, :], ps[0:n, a, :].rearrange("p (a b) -> p a b", b=128))
                nc.scalar.copy(vnat[0:n, tt, 4:6, :], ps[0:n, b, 0:256].rearrange("p (a b) -> p a b", b=128))
                if tt == 2:
                    nc.scalar.copy(knat[:, :], ps[0:n, b, 256:384])
                A(gnat[0:n, tt, :], ps[0:n, b, 384:408], ACT.Exp, scale=-1.0).then_inc(v_sb, 1)
            act.wait_ge(cb_mm, 1)
            link(nc.scalar.copy(cb[:, :], ps[:, 2, 0:2]))
            for j in range(2):
                act.wait_ge(ch_mm, j + 1)
                A(hdn[:, j, :], ps[:, 3 + j, 0:2 * NSEQ * NC_], ACT.Gelu_apprx_tanh,
                  bias=cb[:, j:j + 1]).then_inc(ch_sb, 1)
            act.wait_ge(ckv_mm, 1)
            nc.scalar.copy(ckT[:, :, :], ps[:, 5, 0:NSEQ * NC_].rearrange("p (s n) -> p s n", n=NC_)).then_inc(ckv_sb, 1)
            act.wait_ge(ckv_mm, 2)
            for m in range(3):
                w = min(4, NSEQ - 4 * m)
                ins = nc.scalar.copy(cv[:, 4 * m:4 * m + w, :],
                                     ps[0:NC_, (6, 7, 0)[m], 0:w * 128].rearrange("p (s n) -> p s n", n=128))
            ins.then_inc(ckv_sb, 1)

            def sb_soft(h):
                x = slice((h % 2) * 384, (h % 2) * 384 + 384)
                act.wait_ge(sb_qk, h + 1)
                if h >= 2:
                    act.wait_ge(sb_arg, h - 1)
                nc.scalar.copy(zb[:, x], ps[:, 1 + h % 2, 0:384])
                ins = A(lb[:, x], ps[:, 1 + h % 2, 0:384], ACT.Abs)
                ins.then_inc(sb_zc, 1)
                act.wait_ge(sb_zc, h + 1)
                link(A(lb[:, x], lb[:, x], ACT.Exp, scale=-1.0))
                A(lb[:, x], lb[:, x], ACT.Ln, bias=1.0).then_inc(sb_ln, 1)

            def sb_exp(h):
                x = slice((h % 2) * 384, (h % 2) * 384 + 384)
                act.wait_ge(sb_arg, h + 1)
                if h >= 2:
                    act.wait_ge(sb_pv, h - 1)
                A(wb[:, x], ab[:, x], ACT.Exp).then_inc(sb_w, 1)

            sb_soft(0)
            for h in range(8):
                if h + 1 < 8:
                    sb_soft(h + 1)
                sb_exp(h)

            act.wait_ge(ss_qk, 1)
            act.wait_ge(sb_arg, 8)
            parts = ((slice(0, 128), slice(0, 512), 0), (slice(0, 32), slice(512, 768), 7))
            for rows, c, b in parts:
                w = c.stop - c.start
                nc.scalar.copy(zb[rows, c], ps[rows, b, 0:w])
                link(A(lb[rows, c], ps[rows, b, 0:w], ACT.Abs))
            for rows, c, b in parts:
                link(A(lb[rows, c], lb[rows, c], ACT.Exp, scale=-1.0))
            for rows, c, b in parts:
                ins = A(lb[rows, c], lb[rows, c], ACT.Ln, bias=1.0)
            ins.then_inc(ss_ln, 1)
            act.wait_ge(nc_s, 1)
            A(sc_[:, :, :], sc_[:, :, :], ACT.Exp).then_inc(nc_e, 1)
            act.wait_ge(ss_arg, 1)
            act.wait_ge(sb_pv, 8)
            for rows, c, b in parts:
                ins = A(wb[rows, c], ab[rows, c], ACT.Exp)
            ins.then_inc(ss_w, 1)
            act.wait_ge(ns_qk, 1)
            nc.scalar.copy(zss[:, :, :], ps[:, 1:3, :])
            nc.scalar.copy(zns[:, :, :], ps[0:32, 7, :].rearrange("p (a b) -> p a b", b=256))
            nc.scalar.copy(zcs[:, :], ps[0:NC_, 0, 0:256]).then_inc(ns_z, 1)
            act.wait_ge(nc_t, 1)
            for m in range(4):
                ins = nc.scalar.copy(ptc[:, 2 * m:2 * m + 2, :], ps[0:NC_, 3 + m, :].rearrange("p (h t) -> p h t", t=256))
            ins.then_inc(nc_pt, 1)

            def np_exp(n):
                act.wait_ge(np_s, n + 1)
                x = (n % 2) * 16
                for br in range(2):
                    for tt, c in enumerate((slice(0, 128), slice(128, 384))):
                        y = x + 2 * br + tt
                        ins = A(pb[:, n % 2, br, c], pb[:, n % 2, br, c], ACT.Exp, bias=sm[:, y:y + 1],
                                accum_out=sm[:, y + 4:y + 5])
                ins.then_inc(np_e, 1)

            np_exp(0)
            for n in range(8):
                if n + 1 < 8:
                    np_exp(n + 1)
                if n == 1:
                    act.wait_ge(ns_s, 1)
                    for w in range(2):
                        for br in range(2):
                            y = 64 + 2 * br + w
                            A(spb[:, br, w, :], spb[:, br, w, :], ACT.Exp, bias=sm[:, y:y + 1], accum_out=sm[:, y + 8:y + 9])
                        y = 64 + 4 + w
                        ins = A(ssc[:, w, :], ssc[:, w, :], ACT.Exp, bias=sm[:, y:y + 1], accum_out=sm[:, y + 8:y + 9])
                    ins.then_inc(ns_e, 1)
                act.wait_ge(np_t, n + 1)
                if n >= 2:
                    act.wait_ge(np_pv, n - 1)
                nc.scalar.copy(ptb[:, n % 2, :, :], ps[:, 4:6, 0:384]).then_inc(np_pt, 1)

            act.wait_ge(ns_tb, 1)
            nc.scalar.copy(ptss[:, :, :], ps[:, 2:4, :])
            nc.scalar.copy(ptns[:, :, :], ps[0:32, 0, :].rearrange("p (a b) -> p a b", b=256))
            nc.scalar.copy(ptcs[:, :], ps[0:NC_, 1, 0:256]).then_inc(ns_pt, 1)

            act.wait_ge(ns_o, 1)
            act.wait_ge(ss_o, 1)
            act.wait_ge(np_o, 4)
            A(sqb[:, :, :], oT[:, :, :], ACT.Square).then_inc(rm_sq, 1)
            act.wait_ge(rm_mm, 1)
            act.wait_ge(rm_sd, 1)
            A(srow[:, :], srow[:, :], ACT.Sqrt)
            A(rrow[:, :], rrow[:, :], ACT.Sqrt).then_inc(rm_sd, 1)

            def norm_act(n, x, b, out, done):
                for c in range(KD):
                    act.wait_ge(ln_c, KD * n + c + 1)
                    A(sqb[:, c, :], x[:, c, :], ACT.Square).then_inc(ln_sq, 1)
                act.wait_ge(ln_sd, 2 * n + 1)
                A(srow[:, :], srow[:, :], ACT.Sqrt).then_inc(ln_sd, 1)
                for c in range(KD):
                    act.wait_ge(ln_g, KD * n + c + 1)
                    A(out[:, c, :], x[:, c, :], ACT.Identity, bias=vec[:, b, c:c + 1]).then_inc(done, 1)

            act.wait_ge(out_win, 48)
            act.wait_ge(out_kv, 32)
            norm_act(0, xTs, 2, h_hi, h_h)

            def high(ring_slot, arrived, slot, half=None, used=None):
                act.wait_ge(full[ring_slot], arrived)
                if used is not None:
                    act.wait_ge(w_mm, used)
                x = slice(0, D) if half is None else slice(half * D // 2, (half + 1) * D // 2)
                nc.scalar.copy(w_hi[slot][:, x], ring[:, ring_slot, x]).then_inc(part_hi, 2 if half is None else 1)

            act.sem_inc(q_sb, 4)
            for m in range(3):
                high(*filled(AT_Q + m), m)
            for m in range(N_Q):
                high(*filled(AT_Q + m + 3), (m + 3) % 4, used=2 * m if m else None)
                act.wait_ge(w_mm, 2 * (m + 1))
                nc.scalar.copy(qT[:, m, :], ps[:, m % 4, 0:T]).then_inc(q_sb, 1)
            act.sem_inc(u_act, 4)
            act.sem_inc(g_sb, 4)

            def gelu(i, r, first=0):
                act.wait_ge(w_mm, 8 * i + 2 * (M_U + first + r + 1))
                if first + r >= 2:
                    act.wait_ge(spill[r % 2], 32 * i + 16 * ((first + r) // 2))
                A(u_out[:, r % 2, :], ps[:, r, 0:T], ACT.Gelu_apprx_tanh).then_inc(u_act, 1)

            def high_then_gelu(i, r, first=0):
                slot, value = filled(AT_U + first + r + 3)
                high(slot, 16 * i + value, (r + 3) % 4, used=8 * i + 2 * (M_U + first + r))
                gelu(i, r, first)

            for tt, (t0, n) in enumerate(TOK):
                act.wait_ge(s_mm, tt + 1)
                nc.scalar.copy(sT[0:n, tt, :, :].rearrange("p (a b) c -> p a (b c)", b=4),
                               ps[0:n, 4:8, :]).then_inc(s_sb, 1)
                if tt < 2:
                    high_then_gelu(0, 2 * tt)
                    high_then_gelu(0, 2 * tt + 1)
            with act.Fori(0, U_ALONE // 4 - 3) as i:
                for r in range(4):
                    high_then_gelu(i, r, 4)
            act.wait_ge(rt_exp_in, 3)
            for tt, (t0, n) in enumerate(TOK):
                A(pick[0:n, tt, 2, :], pick[0:n, tt, 2, :], ACT.Exp).then_inc(rt_exp, 1)
            for r in range(8):
                if r == 4:
                    for c in range(3):
                        act.wait_ge(rt_t, c + 1)
                        nc.scalar.copy(slotT[:, c, :], ps[:, 4 + c, 0:T]).then_inc(rt_slot, 1)
                if r < 7:
                    high_then_gelu(0, r % 4, U_ALONE - 8 + r // 4 * 4)
                else:
                    gelu(0, 3, U_ALONE - 4)

            with act.Fori(0, T // 32) as i:
                for r in range(4):
                    slot, value = filled(AT_U + U_ALONE + r + 2)
                    for half in range(2):
                        if half:
                            gelu(i, r, U_ALONE)
                        high(slot, 16 * i + value, r % 2, half, 8 * i + (2 * (M_U + U_ALONE + r) + half + 1))
                        act.wait_ge(g_mm, 16 * i + (2 + 4 * r + 2 * half + 2))
                        nc.scalar.copy(gates[:, :, bass.ds(32 * i + (8 * r + 4 * half), 4)],
                                       ps[:, 4 + (2 * r + half) % 4, :].rearrange("p (t j) -> p j t", j=128)
                                       ).then_inc(g_sb, 1)

            def high_y(r, ready, used=None):
                act.wait_ge(y_mul, ready)
                if used is not None:
                    act.wait_ge(w_mm, used)
                nc.scalar.copy(y_hi[:, r % 2, :], a_in[:, r % 4, :]).then_inc(y_h, 1)

            def highs_down(i, j):
                slot, value = filled(AT_V + j)
                used = 8 * i + 2 * (M_V + j - 2)
                high(slot, 16 * i + value, j % 2, 0, used + 1)
                high_y(j, 4 * i + j + 1, used + 2)
                high(slot, 16 * i + value, j % 2, 1, used + 2)

            high_y(0, 1)
            high_y(1, 2)
            for j in range(2, 4):
                highs_down(0, j)
            with act.Fori(0, NE // 4 - 1) as i:
                for j in range(4, 8):
                    highs_down(i, j)
            norm_act(1, yT, 4, sqb, ln_h)

        @block.vector
        def _(dve):
            V = nc.vector
            done = [0]

            def link(ins):
                done[0] += 1
                ins.then_inc(dve_link, 1)
                dve.wait_ge(dve_link, done[0])

            dve.wait_ge(z_sb, 4 + ZT)
            for g in range(2):
                for par in range(2):
                    for j in range(2):
                        ins = V.tensor_copy(cmpT[par * HD:(par + 1) * HD, g, j, :],
                                            zT[g * HD:(g + 1) * HD, CK + j, par:TP:2])
            ins.then_inc(cmp_ready, 1)
            link(V.tensor_scalar(zT[:, 0:4, :], zT[:, 0:4, :], SCALE, None, ALU.mult))
            link(V.tensor_scalar(zT[:, QB:QB + 4, :], zT[:, QB:QB + 4, :], SCALE, None, ALU.mult))
            dve.wait_ge(zero_done, 1)
            for g in range(2):
                half = slice(g * HD, (g + 1) * HD)
                V.tensor_copy(qbd_a[half, :, :, g * 4:(g + 1) * 4],
                              zT[half, 0:4, TP:T].rearrange("p h (b t) -> p h b t", t=TS))
                ins = V.tensor_copy(qbd_b[half, :, g * 16:(g + 1) * 16].rearrange("p b (r t) -> p b r t", t=TS),
                                    zT[half, QB:QB + 4, TP:T].rearrange("p r (b t) -> p b r t", t=TS))
            ins.then_inc(q_ready, 1)
            dve.wait_ge(v_sb, 3)
            for rows, tt in ((slice(0, 128), slice(0, 2)), (slice(0, 32), slice(2, 3))):
                link(V.tensor_scalar(gnat[rows, tt, :], gnat[rows, tt, :], 1.0, None, ALU.add))
                link(V.reciprocal(gnat[rows, tt, :], gnat[rows, tt, :]))

            def sb_plus(h):
                x = (h % 2) * 384
                dve.wait_ge(sb_ln, h + 1)
                if h >= 2:
                    dve.wait_ge(sb_tri, h - 1)
                link(V.scalar_tensor_tensor(sp_[:, x:x + 384], zb[:, x:x + 384], 0.0, lb[:, x:x + 384],
                                            ALU.max, ALU.add))
                V.tensor_tensor(sp_[:, x:x + 128], sp_[:, x:x + 128], k("keep"), ALU.mult)
                V.tensor_tensor(sp_[:, x + 256:x + 384], sp_[:, x + 256:x + 384], k("keep"),
                                ALU.mult).then_inc(sb_sp, 1)

            def sb_out(hp):
                dve.wait_ge(sb_pv, 2 * hp + 2)
                V.tensor_copy(oT[:, hp, 0:256], ps[:, 5 + hp % 2, 0:256]).then_inc(sb_o, 1)

            sb_plus(0)
            for h in range(8):
                if h + 1 < 8:
                    sb_plus(h + 1)
                x = (h % 2) * 384
                dve.wait_ge(sb_tri, h + 1)
                if h >= 2:
                    dve.wait_ge(sb_w, h - 1)
                V.tensor_tensor(ab[:, x:x + 384], zb[:, x:x + 384], ps[:, 3 + h % 2, 0:384],
                                ALU.add).then_inc(sb_arg, 1)
                if h in (3, 5, 7):
                    sb_out((h - 3) // 2)
            sb_out(3)

            dve.wait_ge(ss_ln, 1)
            dve.wait_ge(sb_tri, 8)
            V.scalar_tensor_tensor(sp_[:, 0:512], zb[:, 0:512], 0.0, lb[:, 0:512], ALU.max, ALU.add)
            link(V.scalar_tensor_tensor(sp_[0:32, 512:768], zb[0:32, 512:768], 0.0, lb[0:32, 512:768],
                                        ALU.max, ALU.add))
            V.tensor_tensor(sp_[0:32, 512:768], sp_[0:32, 512:768], k("keepn", 32), ALU.mult).then_inc(ss_sp, 1)
            dve.wait_ge(nc_qk, 1)
            for g in range(2):
                ins = V.tensor_tensor(sc_[:, 8 * g:8 * g + 8, :],
                                      ps[:, 5 + g, 0:128].rearrange("p (a b) -> p a b", b=16)[:, :, 0:NC_],
                                      k("cbias").rearrange("p (a b) -> p a b", b=NC_)[:, 8 * g:8 * g + 8, :], ALU.add)
            link(ins)
            mx, tot = sm[:, 96:112], sm[:, 112:128]
            wide = lambda a: a.unsqueeze(2).to_broadcast([128, 16, NC_])
            link(V.tensor_reduce(mx, sc_[:, :, :], AX, ALU.max))
            V.tensor_tensor(sc_[:, :, :], sc_[:, :, :], wide(mx), ALU.subtract).then_inc(nc_s, 1)
            dve.wait_ge(ss_tri, 1)
            dve.wait_ge(sb_w, 8)
            V.tensor_tensor(ab[:, 0:512], zb[:, 0:512], ps[:, 3, 0:512], ALU.add)
            V.tensor_tensor(ab[0:32, 512:768], zb[0:32, 512:768], ps[0:32, 4, 0:256], ALU.add).then_inc(ss_arg, 1)
            dve.wait_ge(nc_e, 1)
            v4 = sc_[:, :, :].rearrange("p (h w) n -> p h w n", w=2)
            cm = k("cmask").rearrange("p (w n) -> p w n", n=NC_).unsqueeze(1).to_broadcast([128, 8, 2, NC_])
            link(V.tensor_tensor(v4, v4, cm, ALU.mult))
            link(V.tensor_reduce(tot, sc_[:, :, :], AX, ALU.add))
            link(V.tensor_scalar(tot, tot, 1.0, None, ALU.max))
            link(V.reciprocal(tot, tot))
            gate = gnat[:, 0:2, :].rearrange("p w (h b) -> p h w b", b=3)
            link(V.tensor_tensor(mx.rearrange("p (h w) -> p h w", w=2), tot.rearrange("p (h w) -> p h w", w=2),
                                 gate[:, :, :, 0], ALU.mult))
            V.tensor_tensor(sc_[:, :, :], sc_[:, :, :], wide(mx), ALU.mult).then_inc(nc_p, 1)

            dve.wait_ge(ns_t, 1)
            dve.wait_ge(out_kv, 32)
            tab = k("stab").rearrange("p (w s) -> p w s", w=2)
            for br in range(2):
                V.tensor_tensor(spb[:, br, :, :], ps[:, 4 + 2 * br:6 + 2 * br, 0:PAST + 32], tab, ALU.add)
            V.tensor_tensor(ssc[:, :, :], ps[:, 2, 0:32].rearrange("p (w n) -> p w n", n=16)[:, :, 0:NC_],
                            k("sctab").unsqueeze(1).to_broadcast([128, 2, NC_]), ALU.add)
            g3 = gtmp[:, :, :].rearrange("p w (h b) -> p w h b", b=3)
            link(V.tensor_tensor(g3, ps[:, 3, 0:48].rearrange("p (w h b) -> p w h b", h=8, b=3),
                                 k("rowhead").unsqueeze(1).unsqueeze(3).to_broadcast([128, 2, 8, 3]), ALU.mult))
            V.tensor_reduce(sm[:, 64:68].rearrange("p (b w) -> p b w", w=2), spb[:, :, :, :], AX, ALU.max, negate=True)
            V.tensor_reduce(grow[:, :, :], gtmp[:, :, :].rearrange("p w (h b) -> p w b h", b=3), AX, ALU.add)
            link(V.tensor_reduce(sm[:, 68:70], ssc[:, :, :], AX, ALU.max, negate=True))
            V.tensor_copy(sm[:, 88:90], sm[:, 68:70]).then_inc(ns_s, 1)
            HEADS = [(n // 2, n % 2) for n in range(8)]

            def np_bias(n):
                r, g = HEADS[n]
                dve.wait_ge(np_qk, n + 1)
                if n >= 2:
                    dve.wait_ge(np_t, n - 1)
                else:
                    dve.wait_ge(ckv_sb, 2)
                b = 2 * (n % 2)
                x = (n % 2) * 16
                link(V.scalar_tensor_tensor(pb[:, n % 2, :, :], k("dist").unsqueeze(1).to_broadcast([128, 2, 384]),
                                            SLOPES[g * 4 + r], ps[:, b:b + 2, 0:384], ALU.mult, ALU.add))
                m = sm[:, x:x + 4].rearrange("p (b w) -> p b w", w=2)
                V.tensor_reduce(m[:, :, 0:1], pb[:, n % 2, :, 0:128], AX, ALU.max, negate=True)
                V.tensor_reduce(m[:, :, 1:2], pb[:, n % 2, :, 128:384], AX, ALU.max, negate=True).then_inc(np_s, 1)

            def np_scale(n):
                r, g = HEADS[n]
                h = g * 4 + r
                x = (n % 2) * 16
                dve.wait_ge(np_e, n + 1)
                link(V.reciprocal(sm[:, x + 4:x + 8], sm[:, x + 4:x + 8]))
                link(V.tensor_tensor(sm[:, x + 8:x + 12].rearrange("p (b w) -> p b w", w=2),
                                     sm[:, x + 4:x + 8].rearrange("p (b w) -> p b w", w=2),
                                     gnat[:, 0:2, 3 * h + 1:3 * h + 3].rearrange("p w b -> p b w"), ALU.mult))
                for br in range(2):
                    for tt, c in enumerate((slice(0, 128), slice(128, 384))):
                        y = x + 8 + 2 * br + tt
                        ins = V.tensor_scalar(pb[:, n % 2, br, c], pb[:, n % 2, br, c], sm[:, y:y + 1], None, ALU.mult)
                ins.then_inc(np_p, 1)

            def np_out(r):
                dve.wait_ge(np_pv, 2 * r + 2)
                V.tensor_copy(oT[:, 4 + r, 0:256], ps[:, 6, 0:256]).then_inc(np_o, 1)

            def ns_scale():
                dve.wait_ge(ns_e, 1)
                link(V.reciprocal(sm[:, 72:78], sm[:, 72:78]))
                V.tensor_tensor(sm[:, 80:84].rearrange("p (b w) -> p b w", w=2),
                                sm[:, 72:76].rearrange("p (b w) -> p b w", w=2),
                                grow[:, :, 1:3].rearrange("p w b -> p b w"), ALU.mult)
                link(V.tensor_tensor(sm[:, 84:86], sm[:, 76:78], grow[:, :, 0], ALU.mult))
                for w in range(2):
                    for br in range(2):
                        y = 80 + 2 * br + w
                        V.tensor_scalar(spb[:, br, w, :], spb[:, br, w, :], sm[:, y:y + 1], None, ALU.mult)
                    ins = V.tensor_scalar(ssc[:, w, :], ssc[:, w, :], sm[:, 84 + w:85 + w], None, ALU.mult)
                ins.then_inc(ns_p, 1)

            np_bias(0)
            for n in range(8):
                if n + 1 < 8:
                    np_bias(n + 1)
                np_scale(n)
                if n == 1:
                    ns_scale()
                if n in (3, 5, 7):
                    np_out((n - 3) // 2)
            np_out(3)

            dve.wait_ge(ss_pv, 1)
            for g in range(2):
                half = slice(g * HD, (g + 1) * HD)
                ins = V.tensor_copy(oT[half, 0:4, TP:T].rearrange("p h (b t) -> p h b t", t=TS),
                                    ps[half, 7, 0:256].rearrange("p (h b g t) -> p h b g t", h=4, b=NB, g=2)[:, :, :, g, :])
            ins.then_inc(ss_o, 1)
            dve.wait_ge(ns_pv, 1)
            for g in range(2):
                half = slice(g * HD, (g + 1) * HD)
                ins = V.tensor_copy(oT[half, 4:8, TP:T].rearrange("p r (b t) -> p b r t", t=TS),
                                    ps[half, 4, 0:256].rearrange("p (b g r t) -> p b g r t", g=2, r=4, t=TS)[:, :, g, :, :])
            ins.then_inc(ns_o, 1)

            dve.wait_ge(rm_mm, 1)
            dve.wait_ge(small_in, 16 * 5)
            V.tensor_scalar(srow[:, :], ps[:, 0, 0:T], 1.0 / 512, EPS, ALU.mult, ALU.add)
            V.tensor_scalar(rrow[:, :], ps[:, 1, 0:T], 1.0 / 512, EPS, ALU.mult, ALU.add).then_inc(rm_sd, 1)
            dve.wait_ge(rm_sd, 2)
            V.reciprocal(srow[:, :], srow[:, :])
            link(V.reciprocal(rrow[:, :], rrow[:, :]))
            for c in range(KD):
                V.scalar_tensor_tensor(oT[:, c, :], oT[:, c, :], vec[:, 0, c:c + 1], (srow, rrow)[c // 4][:, :],
                                       ALU.mult, ALU.mult).then_inc(rm_on, 1)

            def norm(n, x, g):
                dve.wait_ge(ln_mm, n + 1)
                link(V.tensor_scalar(srow[:, :], ps[:, 0, 0:T], 1.0 / D, None, ALU.mult))
                for c in range(KD):
                    V.tensor_tensor(x[:, c, :], x[:, c, :], srow[:, :], ALU.subtract).then_inc(ln_c, 1)
                dve.wait_ge(ln_v, n + 1)
                V.tensor_scalar(srow[:, :], ps[:, 1, 0:T], 1.0 / D, EPS, ALU.mult, ALU.add).then_inc(ln_sd, 1)
                dve.wait_ge(ln_sd, 2 * n + 2)
                link(V.reciprocal(rrow[:, :], srow[:, :]))
                for c in range(KD):
                    V.scalar_tensor_tensor(x[:, c, :], x[:, c, :], vec[:, g, c:c + 1], rrow[:, :],
                                           ALU.mult, ALU.mult).then_inc(ln_g, 1)

            for c in range(KD):
                dve.wait_ge(m_mm, c + 1)
                V.scalar_tensor_tensor(xTs[:, c, :], xTs[:, c, :], ALPHA, ps[:, 4 + c % 4, 0:T],
                                       ALU.mult, ALU.add).then_inc(m_pre, 1)
            norm(0, xTs, 1)
            for c in range(KD):
                dve.wait_ge(h_h, c + 1)
                V.scalar_tensor_tensor(h_lo[:, c, :], xTs[:, c, :], vec[:, 2, c:c + 1], h_hi[:, c, :].bitcast(F32),
                                       ALU.add, ALU.subtract).then_inc(h_l, 1)

            def low(highs, ring_slot, slot, half=None):
                dve.wait_ge(part_hi, highs)
                x = slice(0, D) if half is None else slice(half * D // 2, (half + 1) * D // 2)
                V.tensor_tensor(w_lo[slot][:, x], ring[:, ring_slot, x], w_hi[slot][:, x].bitcast(F32),
                                ALU.subtract).then_inc(part_lo, 2 if half is None else 1)

            lows = [0]

            def low_next():
                m = lows[0]
                low(2 * (m + 1), (AT_Q + m) % 4, m % 4)
                lows[0] = m + 1

            for m in range(N_Q + 3):
                low_next()

            for tt, (t0, n) in enumerate(TOK):
                R = slice(0, n)
                dve.wait_ge(s_sb, tt + 1)

                def top16(values, out, where):
                    link(V.max(out[:, 0:8], values))
                    V.max_index(where[:, 0:8], out[:, 0:8], values)
                    link(V.match_replace(values, out[:, 0:8], values, -3.0e38))
                    link(V.max(out[:, 8:16], values))
                    link(V.max_index(where[:, 8:16], out[:, 8:16], values))

                for c in range(16):
                    top16(sT[R, tt, c, :], val[R, c // 2, c % 2, :], idx[R, c // 2, c % 2, :])
                    low_next()
                link(V.tensor_copy(idf[R, :, :, :], idx[R, :, :, :]))
                s1, s2 = val[R, :, 0, :], val[R, :, 1, :]
                for i in range(5):
                    w = ROWLEN[i]
                    V.tensor_tensor(cand[R, :, ROWOFF[i]:ROWOFF[i] + w], s2[:, :, 0:w],
                                    s1[:, :, i:i + 1].to_broadcast([n, 8, w]), ALU.add)
                V.tensor_tensor(cand[R, :, ROWOFF[5]:ROWOFF[8]].rearrange("p h (i j) -> p h i j", j=2),
                                s1[:, :, 5:8].unsqueeze(3).to_broadcast([n, 8, 3, 2]),
                                s2[:, :, 0:2].unsqueeze(2).to_broadcast([n, 8, 3, 2]), ALU.add)
                link(V.tensor_tensor(cand[R, :, ROWOFF[8]:NCAND], s1[:, :, 8:16],
                                     s2[:, :, 0:1].to_broadcast([n, 8, 8]), ALU.add))
                for h in range(8):
                    top16(cand[R, h, :], topv[R, h, :], pos[R, h, :])
                    low_next()
                V.tensor_tensor(pick[R, tt, 2, :].rearrange("p (h k) -> p h k", k=TOPK), topv[R, :, :],
                                topv[R, :, 0:1].to_broadcast([n, 8, TOPK]), ALU.subtract).then_inc(rt_exp_in, 1)
                link(V.tensor_copy(posf[R, :], pos[R, :, :].rearrange("p h k -> p (h k)")))
                V.tensor_copy(dlt[R, :, :, 0:1], idf[R, :, :, 0:1])
                link(V.tensor_tensor(dlt[R, :, :, 1:TOPK], idf[R, :, :, 1:TOPK], idf[R, :, :, 0:TOPK - 1], ALU.subtract))
                many = [n, 8 * TOPK, TOPK]
                link(V.tensor_tensor(step[R, :, :], posf[R, :].unsqueeze(2).to_broadcast(many),
                                     k("rowoff")[R, :].unsqueeze(1).to_broadcast(many), ALU.is_ge))

                def pick_from(out, steps):
                    link(V.tensor_tensor(prod[R, :, :].rearrange("p (h k) i -> p h k i", k=TOPK),
                                         step[R, :, :].rearrange("p (h k) i -> p h k i", k=TOPK), steps, ALU.mult))
                    link(V.tensor_reduce(out, prod[R, :, :], AX, ALU.add))

                four = [n, 8, TOPK, TOPK]
                low_next()
                pick_from(pick[R, tt, 0, :], dlt[R, :, 0, :].unsqueeze(2).to_broadcast(four))
                low_next()
                pick_from(rowo[R, :], k("rowlen")[R, :].unsqueeze(1).unsqueeze(1).to_broadcast(four))
                link(V.tensor_tensor(posf[R, :], posf[R, :], rowo[R, :], ALU.subtract))
                link(V.tensor_tensor(step[R, :, :], posf[R, :].unsqueeze(2).to_broadcast(many),
                                     k("iota")[R, 0:TOPK].unsqueeze(1).to_broadcast(many), ALU.is_ge))
                low_next()
                pick_from(pick[R, tt, 1, :], dlt[R, :, 1, :].unsqueeze(2).to_broadcast(four))
            while lows[0] < M_U + U_ALONE - 4:
                low_next()
            assert lows[0] == M_U + U_ALONE - 4
            for tt, (t0, n) in enumerate(TOK):
                R = slice(0, n)
                e = pick[R, tt, 2, :].rearrange("p (h k) -> p h k", k=TOPK)
                dve.wait_ge(rt_exp, tt + 1)
                link(V.tensor_reduce(ssum[R, tt, :], e, AX, ALU.add))
                link(V.reciprocal(ssum[R, tt, :], ssum[R, tt, :]))
                V.tensor_tensor(e, e, ssum[R, tt, :].unsqueeze(2).to_broadcast([n, 8, TOPK]), ALU.mult).then_inc(rt_pick, 1)
            for r in range(4):
                low_next()

            def low_half(i, m, half):
                low(8 * i + (2 * m + half + 1), (AT_Q + m) % 4, m % 2, half)

            m0 = M_U + U_ALONE
            low_half(0, m0, 0)
            low_half(0, m0, 1)
            low_half(0, m0 + 1, 0)
            dve.wait_ge(rt_slot, 3)
            with dve.Fori(0, T // 32) as i:
                for r in range(4):
                    for q in range(4):
                        t0 = 8 * r + 2 * q
                        dve.wait_ge(g_mm, 16 * i + (4 * r + q + 1))
                        for t in range(2):
                            at_t = bass.ds(32 * i + (t0 + t), 1)
                            V.tensor_scalar(one_a[:, q % 2, t, :], k("iota"), slotT[:, 0, at_t], slotT[:, 2, at_t],
                                            ALU.is_equal, ALU.mult)
                        V.tensor_tensor(one_b[q % 2][:, :, :], k("iota").unsqueeze(1).to_broadcast([128, 2, 128]),
                                        slotT[:, 1, bass.ds(32 * i + t0, 2)].unsqueeze(2).to_broadcast([128, 2, 128]),
                                        ALU.is_equal).then_inc(one_ready, 1)
                        if q == 1:
                            low_half(i, m0 + r + 1, 1)
                        if q == 3:
                            low_half(i, m0 + r + 2, 0)

            def weigh(r, j, arrived):
                dve.wait_ge(a_full[r], arrived)
                V.tensor_tensor(a_in[:, r, :].unsqueeze(1), a_in[:, r, :].unsqueeze(1), gates[:, j, :],
                                ALU.mult).then_inc(y_mul, 1)

            def low_y(r, ready):
                dve.wait_ge(y_h, ready)
                V.tensor_tensor(y_lo[:, r % 2, :], a_in[:, r % 4, :], y_hi[:, r % 2, :].bitcast(F32),
                                ALU.subtract).then_inc(y_l, 1)

            def lows_down(i, j, weigh_next=True):
                low_half(i, M_V + j, 0)
                if weigh_next:
                    weigh((j + 1) % 4, bass.ds(4 * i + j + 1, 1), 16 * i + 16 * ((j + 1) // 4 + 1))
                low_y(j, 4 * i + j + 1)
                low_half(i, M_V + j, 1)

            dve.wait_ge(g_sb, 4 + T // 4)
            for j in range(2):
                weigh(j, slice(j, j + 1), 16)
            low_half(0, M_V + 1, 1)
            low_y(0, 1)
            low_y(1, 2)
            weigh(2, slice(2, 3), 16)
            lows_down(0, 2)
            lows_down(0, 3)
            with dve.Fori(1, NE // 4 - 1) as i:
                for r in range(4):
                    lows_down(i, r)
            for r in range(4):
                lows_down(0, NE - 4 + r, r < 3)

            V.tensor_tensor(yT[:, :, :], h_hi[:, :, :].bitcast(F32), h_lo[:, :, :].bitcast(F32), ALU.add
                            ).then_inc(y_mul, 1)
            dve.wait_ge(y_mul, NE + 1)
            for c in range(KD):
                dve.wait_ge(w_mm, 2 * (M_V + NE) - 1 + c // 4)
                V.scalar_tensor_tensor(yT[:, c, :], yT[:, c, :], ALPHA, ps[:, c, 0:T],
                                       ALU.mult, ALU.add).then_inc(m_pre, 1)
            norm(1, yT, 3)




def lay_out(x_prompt, x_sample, cache_sb_kv, cache_nsa_kv, cache_win_kv, page_table, w_in, cmp_pe, cmp_w1,
            cmp_w2, mix_norm_g, w_out, ln1_g, ln1_b, peer_w_q, peer_sub_keys, peer_u, peer_v, ln2_g, ln2_b):
    f = np.ascontiguousarray
    np_ = lambda a: np.asarray(a)
    x = np.concatenate([np_(x_prompt).reshape(-1, D), np_(x_sample).reshape(-1, D)])
    feat = lambda a: a.reshape(a.shape[0], KD, 128).transpose(2, 1, 0)

    def tiles(w):
        return w.reshape(KD, 128, -1, 128).transpose(2, 1, 0, 3).reshape(w.shape[1] // 128, 128, D)

    swap = lambda a, ax: a.reshape(a.shape[:ax] + (2, 4, HD) + a.shape[ax + 1:]).swapaxes(ax, ax + 1).reshape(a.shape)
    w = np_(w_in)[0]
    qb, kb = QB * 128, CK * 128
    w = np.concatenate([w[:, :qb], swap(w[:, qb:kb], 1), w[:, kb:]], 1)
    wo = np_(w_out)[0]
    wo = np.concatenate([wo[:512], swap(wo[512:], 0)])
    mg = np_(mix_norm_g)[0]
    mg = np.concatenate([mg[:512], swap(mg[512:], 0)])
    vecs = np.stack([a.reshape(KD, 128).T for a in (mg, np_(ln1_g)[0], np_(ln1_b)[0], np_(ln2_g)[0], np_(ln2_b)[0])], 1)
    sb = np_(cache_sb_kv)[0]
    pages = sb.shape[0]
    kT = sb[:, :, 0].reshape(pages, 128, 4, 128).transpose(0, 3, 2, 1).reshape(pages, 128, 512)
    cache_sb = np.concatenate([kT, sb[:, :, 1].reshape(pages, 128, 512)], 2)
    ns = np_(cache_nsa_kv)[0]
    cache_nsa = np.concatenate([ns[:, :, 2].reshape(pages, 128, 128).transpose(0, 2, 1),
                                ns[:, :, 3].reshape(pages, 128, 128)], 2)
    cache_cmp = ns[:, :, 0:2].reshape(pages, 64, 2, 2, 2, HD).transpose(0, 2, 5, 4, 3, 1).reshape(pages, 128, 2, 2, 64)
    win = np_(cache_win_kv)[0].reshape(NB, PAST, 2, 128)
    win_kT = win[:, :, 0].transpose(2, 0, 1)
    win_v = win[:, :, 1].reshape(NB, 2, 128, 128).transpose(2, 0, 1, 3).reshape(128, NB, 256)
    return {
        "xT": f(feat(x)), "w_in": f(tiles(w[:, :GT * 128])),
        "w_gate": f(w[:, GT * 128:].reshape(KD, 128, 24).transpose(1, 0, 2)),
        "w_out": f(tiles(wo)), "w_q": f(tiles(np_(peer_w_q)[0])),
        "keysT": f(np_(peer_sub_keys)[0].reshape(16, 128, 128).transpose(2, 0, 1)),
        "uT": f(np_(peer_u)[0].reshape(128, 128, KD, 128).transpose(1, 3, 2, 0).reshape(128, 128, D)),
        "v": f(np_(peer_v)[0].reshape(128, 128, D).transpose(1, 0, 2)),
        "w1": f(np_(cmp_w1)[0].reshape(2, 16, 128, 128).transpose(2, 0, 1, 3)),
        "pe_cmp": f(np_(cmp_pe)[0].reshape(2, 16, 128).transpose(2, 0, 1)),
        "w2": f(np_(cmp_w2)[0].transpose(1, 0, 2)),
        "vecs": f(vecs), "cache_sb": f(cache_sb), "cache_nsa": f(cache_nsa), "cache_cmp": f(cache_cmp),
        "win_kv": f(np.concatenate([win_kT, win_v], 2)),
        "win_rows": f(win.reshape(NB, PAST, 256)), "page_table": f(np_(page_table).reshape(1, PAGES)),
        "consts": CONST_ARRAY,
    }


OUTPUTS = [((128, KD, T), "float32"), ((128, 14, T), "float32"), ((NB, PAST, 256), "float32")]


def take_out(y, kv, win):
    rows = lambda a: a.transpose(2, 1, 0).reshape(T, -1)
    y, kv = rows(y), rows(kv)
    sb, nsa, wn = kv[:, :1024], kv[:, 1024:1536], kv[:, 1536:]
    c = np.ascontiguousarray
    return (c(y[:TP].reshape(1, TP, D)), c(y[TP:].reshape(NB, TS, D)),
            c(sb[:TP].reshape(1, 1, TP, 2, 8, HD)), c(nsa[:TP].reshape(1, 1, TP, 4, 2, HD)),
            c(wn[:TP].reshape(1, 1, TP, 2, 2, HD)),
            c(sb[TP:].reshape(1, NB, TS, 2, 8, HD)), c(nsa[TP:].reshape(1, NB, TS, 4, 2, HD)),
            c(win.reshape(1, NB, PAST, 2, 2, HD)))


def kernel(**inputs):
    import concourse.bacc as bacc
    from concourse.bass_utils import run_bass_kernel_spmd

    arrays = lay_out(**inputs)
    nc = bacc.Bacc("TRN2", target_bir_lowering=False, num_devices=1)
    args = [nc.dram_tensor(f"in_{n}_dram", a.shape, mybir.dt.from_np(a.dtype), kind="ExternalInput").ap()
            for n, a in arrays.items()]
    outs = [nc.dram_tensor(f"out_{i}_dram", s, mybir.dt.from_np(np.dtype(d)), kind="ExternalOutput").ap()
            for i, (s, d) in enumerate(OUTPUTS)]
    trunk(nc, *args, *outs)
    got = run_bass_kernel_spmd(nc, [{f"in_{n}_dram": a for n, a in arrays.items()}], core_ids=[0]).results[0]
    return take_out(*(np.asarray(got[f"out_{i}_dram"]) for i in range(len(OUTPUTS))))
```

```python
from contextlib import ExitStack

import numpy as np

import concourse.bass as bass
from concourse import mybir

F32 = mybir.dt.float32
F32R = mybir.dt.float32r
BF16 = mybir.dt.bfloat16
I32 = mybir.dt.int32
U32 = mybir.dt.uint32
ALU = mybir.AluOpType
ACT = mybir.ActivationFunctionType
AX = mybir.AxisListType.X

D = 1024
KD = D // 128
TP = 256
NB = 8
TS = 4
T = TP + NB * TS
TOK = [(0, 128), (128, 128), (256, 32)]
PAST = 256
PAGES = NB * 2
HD = 64
SCALE = HD ** -0.5
ALPHA = 2.0 ** 0.25
EPS = 1e-5
BIG = 1e30
NC_ = 15
NSEQ = 1 + NB
ZT = 23
KA, VA, QB, CK, SK, SV, WK, WV, GT = 4, 8, 12, 16, 18, 19, 20, 21, 22
NE = 128
TOPK = 16
ROWLEN = [TOPK // (i + 1) for i in range(TOPK)]
ROWOFF = [sum(ROWLEN[:i]) for i in range(TOPK)]
NCAND = sum(ROWLEN)
PACE, PACE_Q = 1.5, 2.0
SLOPES = [2.0 ** (-(h + 1)) for h in range(8)]



def constants():
    c = {}
    s = np.arange(128)[:, None]
    t = np.arange(128)[None, :]
    c["ident"] = (s == t) * 1.0
    c["negtri"] = (s >= t) * -1.0
    c["negones"] = -np.ones((128, 128))
    c["ones"] = np.ones((128, 128))
    c["keep"] = (s < t) * 1.0
    c["block"] = np.where(s < t, 0.0, -BIG)
    q, k = s, t
    dist = lambda q, k: np.where(k <= q, -(q - k) * 1.0, -BIG)
    kk = np.arange(256)[None, :]
    c["dist"] = np.concatenate([dist(q, k), dist(q + 128, kk)], 1)
    cpos = np.arange(NC_) * 16 + 31
    bias = np.zeros((128, 8, 2, NC_))
    mask = np.zeros((128, 2, NC_))
    for tt in range(2):
        qp = np.arange(128)[:, None] + 128 * tt
        mask[:, tt] = cpos[None, :] <= qp
        for h in range(8):
            bias[:, h, tt] = np.where(cpos[None, :] <= qp, -SLOPES[h] * (qp - cpos[None, :]), -BIG)
    c["cbias"] = bias.reshape(128, -1)
    c["cmask"] = mask.reshape(128, -1)
    R = np.arange(128)
    rh, rt = (R % 32) // 4, R % 4
    tab = np.zeros((128, 2, PAST + 32))
    slope = np.array(SLOPES)[rh][:, None]
    for w in range(2):
        b = w * 4 + R // 32
        tab[:, w, :PAST] = -slope * (PAST + rt[:, None] - np.arange(PAST)[None, :])
        nb, nt = np.arange(32) // 4, np.arange(32) % 4
        ok = (nb[None, :] == b[:, None]) & (nt[None, :] <= rt[:, None])
        tab[:, w, PAST:] = np.where(ok, -slope * (rt[:, None] - nt[None, :]), -BIG)
    c["stab"] = tab.reshape(128, -1)
    c["sctab"] = -slope * (PAST + rt[:, None] - cpos[None, :])
    c["rowhead"] = (rh[:, None] == np.arange(8)[None, :]) * 1.0
    sel = np.zeros((128, 2, 128))
    for w in range(2):
        sel[(w * 4 + R // 32) * 4 + rt, w, R] = 1.0
    c["selrow"] = sel.reshape(128, -1)
    col = np.arange(256)
    cb, ct = (col % 64) // 8, col % 4
    r = np.arange(32)
    ok = (r[:, None] // 4 == cb[None, :]) & (r[:, None] % 4 < ct[None, :])
    c["keepn"] = np.concatenate([ok * 1.0, np.zeros((96, 256))])
    c["blockn"] = np.concatenate([np.where(ok, 0.0, -BIG), np.zeros((96, 256))])
    c["iota"] = np.broadcast_to(t * 1.0, (128, 128))
    off = np.array(ROWOFF, float)
    c["rowoff"] = np.broadcast_to(off, (128, 16))
    c["rowlen"] = np.broadcast_to(np.concatenate([[0.0], np.diff(off)]), (128, 16))
    order, at, parts = {}, 0, []
    last = ["ident", "ones", "iota", "rowoff", "rowlen"]
    for name, a in sorted(c.items(), key=lambda x: x[0] not in last):
        order[name] = (at, a.shape[1])
        parts.append(a)
        at += a.shape[1]
    return order, np.ascontiguousarray(np.concatenate(parts, 1).astype(np.float32))


CONST, CONST_ARRAY = constants()
NCONST = CONST_ARRAY.shape[1]
NLIVE = sum(CONST[n][1] for n in ("ident", "ones", "iota", "rowoff", "rowlen"))


def trunk(nc, xT, w_in, w_gate, w_out, w_q, keysT, uT, v, w1, pe_cmp, w2, vecs, cache_sb, cache_nsa,
          cache_cmp, win_kv, win_rows, page_table, consts,
          y_out, kv_out, win_out):
    ctx = ExitStack()
    with ctx:
        base = nc.sbuf_base if isinstance(nc.sbuf_base, int) else nc.sbuf_base()
        base = (base + 63) // 64 * 64
        placed = [0]

        def at(name, shape, where, dt=F32):
            return nc.alloc_sbuf_tensor_at(name, [shape[0]] + list(shape[1:]), dt, offset=base + 4 * where)

        def bump(words):
            placed[0] += (words + 15) // 16 * 16
            return placed[0] - (words + 15) // 16 * 16

        def words(*dims):
            n = 1
            for d in dims:
                n *= d
            return n

        at_con = bump(NCONST)
        con = at("con", [128, NCONST], at_con)
        vec = at("vec", [128, 5, KD], bump(5 * KD))
        pt = at("pt", [1, PAGES], bump(PAGES), I32)
        at_ring = bump(4 * D)
        ring = at("ring", [128, 4, D], at_ring)
        at_x = bump(KD * T)
        at_h = bump(KD * T)
        at_a = bump(NE * T)
        at_w1 = bump(4096)
        rest = bump(256)
        end = nc.sbuf_usable_end if isinstance(nc.sbuf_usable_end, int) else nc.sbuf_usable_end()
        assert base + 4 * placed[0] <= end, (base + 4 * placed[0], end)

        xTs = at("xTs", [128, KD, T], at_x)
        vnat = at("vnat", [128, 3, 6, 128], at_h)
        o = at_a
        kvs = at("kvs", [128, PAGES, 1024], o)
        winkv = kvs[:, 0:NB, 0:512]
        x_hi = at("x_hi", [128, KD, T], o, F32R)
        x_lo = at("x_lo", [128, KD, T], o + KD * T, F32R)
        at_e = o + PAGES * 512
        sqb = kvs[:, 0:KD, 512:512 + T]
        o += PAGES * 1024
        nsk = at("nsk", [128, PAGES, 256], o)
        o += PAGES * 256
        at_cmp = o
        cmpT = at("cmpT", [128, 2 * NSEQ + 1, 2, 128], o)
        o_hi = at("o_hi", [128, KD, T], o, F32R)
        o_lo = at("o_lo", [128, KD, T], o + KD * T, F32R)
        pes = cmpT[:, 2 * NSEQ, :, :]
        o += 2 * (2 * NSEQ + 1) * 128
        zT = at("zT", [128, ZT, T], o)
        spb = at("spb", [128, 2, 2, PAST + 32], o + VA * T)
        srow = at("srow", [128, T], o)
        rrow = at("rrow", [128, T], o + T)
        o += ZT * T
        oT = at("oT", [128, KD, T], o)
        hdn = at("hdn", [128, 2, 2 * NSEQ * NC_], o)
        o += KD * T
        ckT = at("ckT", [128, NSEQ, NC_], o)
        o += 144
        cv = at("cv", [NC_, NSEQ, 128], o)
        o += NSEQ * 128
        qbd_a = at("qbd_a", [128, 4, NB, 8], o)
        o += 256
        qbd_b = at("qbd_b", [128, NB, 32], o)
        o += 256
        wg = at("wg", [128, KD, 24], o)
        o += 192
        knat = at("knat", [32, 128], o)
        o += 128
        grow = at("grow", [128, 2, 3], o)
        gtmp = at("gtmp", [128, 2, 24], o + 16)
        o += 64
        assert o <= at_a + NE * T, (o, at_a + NE * T)
        w1s = at("w1s", [128, 2, 16, 128], at_w1)
        w2s = at("w2s", [128, 2, HD], rest + 32)
        cb = at("cb", [128, 2], rest + 160)
        gnat = at("gnat", [128, 3, 24], rest + 176)
        zb = at("zb", [128, 768], at_ring)
        lb = at("lb", [128, 768], at_ring + 768)
        sp_ = at("sp_", [128, 768], at_ring + 1536)
        ab = at("ab", [128, 768], at_ring + 2304)
        wb = at("wb", [128, 768], at_cmp + 3072)
        ptc = at("ptc", [NC_, 8, TP], at_cmp)
        sc_ = at("sc_", [128, 16, NC_], at_cmp + 3840)
        ptns = at("ptns", [32, 2, 256], at_w1 + 3072)
        ptcs = at("ptcs", [NC_, 256], at_w1 + 3584)
        ssc = at("ssc", [128, 2, NC_], at_w1 + 3840)
        sm = at("sm", [128, 160], at_w1 + 3872)
        pb = at("pb", [128, 2, 2, 384], at_w1)
        ptb = at("ptb", [128, 2, 2, 384], at_w1 + 1536)
        ptss = at("ptss", [128, 2, 512], at_w1)
        os_ = at("os_", [128, 2, 128], at_w1 + 1536)
        h_hi = at("h_hi", [128, KD, T], at_h, F32R)
        h_lo = at("h_lo", [128, KD, T], at_con + NLIVE, F32R)
        assert NLIVE + KD * T <= NCONST
        E = [at_e + 2 * D * q for q in range(4)]
        P = [at_w1 + 2 * D * q for q in range(2)]
        w_hi = [at(f"w_hi{q}", [128, D], where, F32R) for q, where in enumerate(E + P)]
        w_lo = [at(f"w_lo{q}", [128, D], where + D, F32R) for q, where in enumerate(E + P)]
        keys = at("keys", [128, 16, 128], at_a)
        sT = at("sT", [128, 3, 16, 128], at_a + 2048)
        assert at_a + 2048 + 6144 <= at_e
        r0 = at_e + 8 * D
        qT = at("qT", [128, 4, T], r0)
        r1 = r0 + 4 * T
        step = at("step", [128, 8 * TOPK, TOPK], r1, BF16)
        prod = at("prod", [128, 8 * TOPK, TOPK], r1 + 1024, BF16)
        dlt = at("dlt", [128, 8, 2, TOPK], r1 + 2048, BF16)
        rowlen = at("rowlen", [128, TOPK], r1 + 2176, BF16)
        val = at("val", [128, 3, 8, 2, TOPK], r1 + 2192)
        idx = at("idx", [128, 3, 8, 2, TOPK], r1 + 2960, U32)
        r2 = r1 + 3728
        idf = at("idf", [128, 8, 2, TOPK], r2)
        cand = at("cand", [128, 8, NCAND], r2 + 256)
        topv = at("topv", [128, 8, TOPK], r2 + 656)
        pos = at("pos", [128, 8, TOPK], r2 + 784, U32)
        posf = at("posf", [128, 8 * TOPK], r2 + 912)
        rowo = at("rowo", [128, 8 * TOPK], r2 + 1040)
        ssum = at("ssum", [128, 3, 8], r2 + 1168)
        pick = at("pick", [128, 3, 3, 8 * TOPK], r2 + 1200)
        gates = at("gates", [128, NE, T], at_a)
        u_out = at("u_out", [128, 2, T], at_x)
        slotT = at("slotT", [128, 3, T], at_x + 2 * T)
        one_a = at("one_a", [128, 2, 2, 128], at_x + 5 * T)
        one_b = [at("one_b0", [128, 2, 128], at_x + 5 * T + 512), at("one_b1", [128, 2, 128], rest)]
        assert at_x + 5 * T + 768 <= at_h
        y_hi = at("y_hi", [128, 2, T], at_x, F32R)
        y_lo = at("y_lo", [128, 2, T], at_x + 2 * T, F32R)
        a_in = at("a_in", [128, 4, T], at_x + 4 * T)
        assert at_x + 8 * T <= at_h
        yT = at("yT", [128, KD, T], at_e)
        a_dram = nc.dram_tensor("activations", [NE, 128, T], F32, kind="Internal").ap()

        ps = ctx.enter_context(nc.psum_tensor("ps", [128, 8, 512], F32))

        def k(name, rows=128):
            a, n = CONST[name]
            return con[0:rows, a:a + n]

        def sem(name):
            return ctx.enter_context(nc.semaphore(name))

        con_in, small_in, pt_in, cmp_in, nsk_in, win_in, keys_in = map(
            sem, ("con_in", "small_in", "pt_in", "cmp_in", "nsk_in", "win_in", "keys_in"))
        x_in = [sem(f"x_in{q}") for q in range(4)]
        kv_in = [sem(f"kv_in{q}") for q in range(4)]
        x_h, x_l, o_h, o_l = map(sem, ("x_h", "x_l", "o_h", "o_l"))
        full = [sem(f"ring_full{r}") for r in range(4)]
        gate_mm, z_sb, v_mm, v_sb, q_ready, cmp_ready, zero_done = map(sem, (
            "gate_mm", "z_sb", "v_mm", "v_sb", "q_ready", "cmp_ready", "zero_done"))
        pe_zero, ch_mm, ch_sb, ckv_mm, ckv_sb = map(sem, ("pe_zero", "ch_mm", "ch_sb", "ckv_mm", "ckv_sb"))
        sb_qk, sb_zc, sb_ln, sb_sp, sb_tri, sb_arg, sb_w, sb_pv, sb_o = map(sem, (
            "sb_qk", "sb_zc", "sb_ln", "sb_sp", "sb_tri", "sb_arg", "sb_w", "sb_pv", "sb_o"))
        ss_half, ss_qk, ss_ln, ss_sp, ss_tri, ss_arg, ss_w, ss_pv, ss_o = map(sem, (
            "ss_half", "ss_qk", "ss_ln", "ss_sp", "ss_tri", "ss_arg", "ss_w", "ss_pv", "ss_o"))
        nc_qk, nc_s, nc_e, nc_p, nc_t, nc_pt = map(sem, ("nc_qk", "nc_s", "nc_e", "nc_p", "nc_t", "nc_pt"))
        np_qk, np_s, np_e, np_p, np_t, np_pt, np_pv, np_o = map(sem, (
            "np_qk", "np_s", "np_e", "np_p", "np_t", "np_pt", "np_pv", "np_o"))
        ns_qk, ns_b, ns_r, ns_t, ns_s, ns_e, ns_p, ns_tb, ns_pt, ns_pv, ns_o = map(sem, (
            "ns_qk", "ns_b", "ns_r", "ns_t", "ns_s", "ns_e", "ns_p", "ns_tb", "ns_pt", "ns_pv", "ns_o"))
        rm_sq, rm_mm, rm_sd, rm_on = map(sem, ("rm_sq", "rm_mm", "rm_sd", "rm_on"))
        m_pre = sem("m_pre")
        ln_mm, ln_c, ln_sq, ln_v, ln_sd, ln_g, ln_h = map(sem, (
            "ln_mm", "ln_c", "ln_sq", "ln_v", "ln_sd", "ln_g", "ln_h"))
        h_h, h_l, q_sb, s_mm, s_sb = map(sem, ("h_h", "h_l", "q_sb", "s_mm", "s_sb"))
        part_hi, w_mm = map(sem, ("part_hi", "w_mm"))
        part_lo = [sem(f"part_lo{r}") for r in range(4)]
        rt_exp_in, rt_exp, rt_pick, rt_t, rt_slot = map(sem, ("rt_exp_in", "rt_exp", "rt_pick", "rt_t", "rt_slot"))
        u_act, one_ready, g_mm, g_sb = map(sem, ("u_act", "one_ready", "g_mm", "g_sb"))
        spill = [sem(f"spill{r}") for r in range(2)]
        a_full = [sem(f"a_full{r}") for r in range(4)]
        y_mul, y_h, y_l, h_sum = map(sem, ("y_mul", "y_h", "y_l", "h_sum"))
        dve_link, act_link = map(sem, ("dve_link", "act_link"))
        out_y, out_kv, out_win = map(sem, ("out_y", "out_kv", "out_win"))

        N_IN, N_OUT, N_Q = GT, KD, 16
        AT_OUT, AT_Q = N_IN, N_IN + N_OUT
        AT_U = AT_Q + N_Q
        AT_V = AT_U + NE

        def filled(n):
            return n % 4, 16 * (n // 4 + 1)

        U_ALONE = NE - T // 8

        def place(n):
            return n % 4 if n < AT_U + U_ALONE else 4 + n % 2

        block = ctx.enter_context(nc.Block())

        @block.sync
        def _(sp):
            def load(n, src):
                if n >= 4:
                    sp.wait_ge(part_lo[n % 4], 2 * (n // 4))
                sp.dma_start(ring[:, n % 4, :], src).then_inc(full[n % 4], 16)

            load(0, w_in[0])
            for q in range(4):
                sp.dma_start(xTs[:, 2 * q:2 * q + 2, :], xT[:, 2 * q:2 * q + 2, :]).then_inc(x_in[q], 16)
            for n in range(1, N_IN):
                load(n, w_in[n])
                if n == 6:
                    sp.dma_start(con[:, :], consts).then_inc(con_in, 16)
            sp.wait_ge(ss_w, 1)
            for n in range(N_OUT):
                load(AT_OUT + n, w_out[n])
            for n in range(N_Q):
                load(AT_Q + n, w_q[n])

            tile = lambda t, i, r: t[bass.ds(4 * i + r, 1)].rearrange("a p c -> (a p) c")

            def store(r, act_done, dst):
                sp.wait_ge(u_act, act_done)
                sp.dma_start(dst, u_out[:, r % 2, :]).then_inc(spill[r % 2], 16)

            for n in range(8):
                load(AT_U + n, uT[n])
                if n >= 6:
                    store(n, 4 + n - 5, a_dram[n - 6])
            with sp.Fori(2, NE // 4) as i:
                for r in range(4):
                    sp.wait_ge(part_lo[(AT_U + r) % 4], 2 * i + 2 * ((AT_U + r) // 4))
                    sp.dma_start(ring[:, (AT_U + r) % 4, :], tile(uT, i, r)).then_inc(full[(AT_U + r) % 4], 16)
                    store(r, 4 * i + r - 1, tile(a_dram, i - 2 + r // 2, (r + 2) % 4))
            for n in range(NE, NE + 6):
                if n < NE + 4:
                    load(AT_U + n, v[n - NE])
                if n == NE + 5:
                    for r in range(2):
                        sp.wait_ge(spill[r], 16 * 2)
                    sp.wait_ge(g_mm, 2 + T // 2)
                    for r in range(4):
                        sp.dma_start(a_in[:, r, :], a_dram[r]).then_inc(a_full[r], 16)
                store(n, 4 + n - 5, a_dram[n - 6])
            for r in range(2):
                sp.wait_ge(spill[r], 16 * NE // 2)
            with sp.Fori(1, NE // 4) as i:
                for r in range(4):
                    sp.wait_ge(part_lo[(AT_V + r) % 4], 2 * i + 2 * ((AT_V + r) // 4))
                    sp.dma_start(ring[:, (AT_V + r) % 4, :], tile(v, i, r)).then_inc(full[(AT_V + r) % 4], 16)
                    sp.wait_ge(y_l, 4 * i + r - 3)
                    sp.dma_start(a_in[:, r, :], tile(a_dram, i, r)).then_inc(a_full[r], 16)
            for c in range(0, KD, 2):
                sp.wait_ge(ln_h, c + 2)
                sp.dma_start(y_out[:, c:c + 2, :], sqb[:, c:c + 2, :]).then_inc(out_y, 16)
            sp.wait_ge(out_y, 16 * KD // 2)
            sp.wait_ge(out_kv, 32)
            sp.wait_ge(out_win, 48)

        @block.gpsimd
        def _(pool):
            pool.dma_start(pt[:, :], page_table).then_inc(pt_in, 16)
            pool.wait_ge(full[2], 16)
            pool.dma_start(w1s[:, :, :, :], w1).then_inc(small_in, 16)
            nc.gpsimd.memset(pes, 0.0).then_inc(pe_zero, 1)
            pool.wait_ge(pe_zero, 1)
            pool.dma_start(pes[:, :, 0:16], pe_cmp).then_inc(cmp_in, 16)
            pool.dma_start(w2s[:, :, :], w2).then_inc(small_in, 16)
            pool.dma_start(vec[:, :, :], vecs).then_inc(small_in, 16)
            pool.dma_start(wg[:, :, :], w_gate).then_inc(small_in, 16)
            nc.gpsimd.memset(qbd_a[:, :, :, :], 0.0)
            nc.gpsimd.memset(qbd_b[:, :, :], 0.0).then_inc(zero_done, 1)
            pool.wait_ge(pt_in, 16)
            src = lambda t, n: t[bass.ds(nc.gpsimd.value_load(pt[0:1, n:n + 1], min_val=0,
                                                              max_val=cache_sb.shape[0] - 1), 1)]
            for n in range(PAGES):
                b, p = n // 2, n % 2
                pool.dma_start(cmpT[:, 2 + 2 * b:4 + 2 * b, :, 64 * p:64 * p + 64].rearrange("p g k n -> p (g k) n"),
                               src(cache_cmp, n).rearrange("a p g k n -> (a p) (g k) n")).then_inc(cmp_in, 16)
            pool.wait_ge(w_mm, 2 * N_IN)
            for n in range(PAGES):
                pool.dma_start(kvs[:, n, :], src(cache_sb, n).rearrange("a p c -> (a p) c")).then_inc(kv_in[n // 4], 16)
            for n in range(PAGES):
                pool.dma_start(nsk[:, n, :], src(cache_nsa, n).rearrange("a p c -> (a p) c")).then_inc(nsk_in, 16)
            pool.dma_start(win_out[:, 0:PAST - TS, :], win_rows[:, TS:PAST, :]).then_inc(out_win, 16)
            pool.wait_ge(z_sb, 4 + ZT)
            pool.dma_start(kv_out[:, 0:8, :], zT[:, KA:KA + 8, :]).then_inc(out_kv, 16)
            pool.dma_start(kv_out[:, 8:14, :], zT[:, CK:CK + 6, :]).then_inc(out_kv, 16)
            pool.wait_ge(v_sb, 3)
            pool.dma_start(win_out[:, PAST - TS:PAST, 0:128], knat[:, :]).then_inc(out_win, 16)
            pool.dma_start(win_out[:, PAST - TS:PAST, 128:256], vnat[0:32, 2, 5, :]).then_inc(out_win, 16)
            pool.wait_ge(ss_half, 1)
            pool.dma_start(winkv, win_kv).then_inc(win_in, 16)
            for n in range(AT_OUT, AT_OUT + 4):
                slot = n % 4
                pool.wait_ge(part_hi, 2 * (n + 1))
                nc.gpsimd.tensor_tensor(w_lo[slot][:, :], ring[:, slot, :], w_hi[slot][:, :].bitcast(F32),
                                        ALU.subtract).then_inc(part_lo[slot], 2)
            pool.wait_ge(ln_v, 1)
            pool.dma_start(keys[:, :, :], keysT).then_inc(keys_in, 16)
        @block.tensor
        def _(pe):
            mm = nc.tensor.matmul
            ident = k("ident")

            pe.sem_inc(g_mm, 2)
            def parts(slot, hi_, lo_, c, bank, start, stop):
                block_ = slice(c * 128, (c + 1) * 128)
                hi, lo = w_hi[slot][:, block_], w_lo[slot][:, block_]
                mm(ps[:, bank, 0:T], hi, hi_, start=start, stop=False)
                mm(ps[:, bank, 0:T], hi, lo_, start=False, stop=False)
                return mm(ps[:, bank, 0:T], lo, hi_, start=False, stop=stop)

            def project(slot, x, bank, lows, between=lambda kd: None, kds=range(KD), x_low=None):
                for kd in kds:
                    if x_low is not None:
                        pe.wait_ge(x_low, kd + 1)
                    if kd % 4 == 0:
                        pe.wait_ge(lows[0], lows[1 + kd // 4])
                    ins = parts(slot, x[0][:, kd, :], x[1][:, kd, :], kd, bank, kd == 0, kd == KD - 1)
                    if kd % 4 == 3:
                        ins.then_inc(w_mm, 1)
                    between(kd)

            def halves(i, n):
                return part_lo[n % 4], 2 * i + (2 * (n // 4) + 1), 2 * i + (2 * (n // 4) + 2)

            x_parts, o_parts, h_parts = (x_hi, x_lo), (o_hi, o_lo), (h_hi, h_lo)
            with pe.Fori(0, 5) as i:
                for r in range(4):
                    pe.wait_ge(z_sb, 4 * i + r + 1)
                    project(r, x_parts, r, halves(i, r), x_low=None if r else x_l)
            for c in range(20, N_IN):
                pe.wait_ge(z_sb, c + 1)
                project(c % 4, x_parts, c % 4, halves(0, c))
            pe.wait_ge(small_in, 16 * 4)
            pe.wait_ge(z_sb, GT + 1)
            for kd in range(KD):
                ins = mm(ps[0:24, 2, 0:T], wg[:, kd, :], xTs[:, kd, :], start=kd == 0, stop=kd == KD - 1)
            ins.then_inc(gate_mm, 1)

            pe.wait_ge(con_in, 16)
            pe.wait_ge(z_sb, 4 + ZT)
            for tt, (t0, n) in enumerate(TOK):
                a, b = (4, 6, 0)[tt], (5, 7, 1)[tt]
                tok = slice(t0, t0 + n)
                for j in range(4):
                    nc.tensor.transpose(ps[0:n, a, j * 128:(j + 1) * 128], zT[:, VA + j, tok], ident)
                nc.tensor.transpose(ps[0:n, b, 0:128], zT[:, SV, tok], ident)
                nc.tensor.transpose(ps[0:n, b, 128:256], zT[:, WV, tok], ident)
                if tt == 2:
                    nc.tensor.transpose(ps[0:n, b, 256:384], zT[:, WK, tok], ident)
                nc.tensor.transpose(ps[0:n, b, 384:408], zT[0:24, GT, tok], ident[0:24, 0:24]).then_inc(v_mm, 1)

            pe.wait_ge(q_ready, 1)
            pe.wait_ge(v_sb, 3)

            def sb_scores(h):
                if h >= 2:
                    pe.wait_ge(sb_zc, h - 1)
                hp, half = h // 2, slice((h % 2) * HD, (h % 2 + 1) * HD)
                b = 1 + h % 2
                mm(ps[:, b, 0:256], zT[half, KA + hp, 0:128], zT[half, hp, 0:256], start=True, stop=True)
                mm(ps[:, b, 256:384], zT[half, KA + hp, 128:256], zT[half, hp, 128:256],
                   start=True, stop=True).then_inc(sb_qk, 1)

            def sb_sums(h):
                pe.wait_ge(sb_sp, h + 1)
                if h >= 2:
                    pe.wait_ge(sb_arg, h - 1)
                b, x = 3 + h % 2, (h % 2) * 384
                mm(ps[:, b, 0:256], k("negtri"), sp_[:, x:x + 256], start=True, stop=False)
                mm(ps[:, b, 128:256], k("negones"), sp_[:, x + 256:x + 384], start=False, stop=False)
                mm(ps[:, b, 0:128], ident, k("block"), start=False, stop=True)
                mm(ps[:, b, 256:384], k("negtri"), sp_[:, x + 256:x + 384], start=True, stop=False)
                mm(ps[:, b, 256:384], ident, k("block"), start=False, stop=True).then_inc(sb_tri, 1)

            def sb_values(h):
                pe.wait_ge(sb_w, h + 1)
                hp, x = h // 2, (h % 2) * 384
                if h % 2 == 0 and hp >= 2:
                    pe.wait_ge(sb_o, hp - 1)
                half = slice((h % 2) * HD, (h % 2 + 1) * HD)
                b = 5 + hp % 2
                mm(ps[half, b, 0:256], vnat[:, 0, hp, half], wb[:, x:x + 256], start=True, stop=False)
                mm(ps[half, b, 128:256], vnat[:, 1, hp, half], wb[:, x + 256:x + 384],
                   start=False, stop=True).then_inc(sb_pv, 1)

            sb_scores(0)
            sb_scores(1)

            pe.wait_ge(cmp_ready, 1)
            pe.wait_ge(cmp_in, 16 * (PAGES + 1))
            for j in range(2):
                for m in range(16):
                    blocks = cmpT[:, :, j, m:m + 8 * (NC_ - 1) + 1:8]
                    ins = mm(ps[:, 5 + j, 0:(2 * NSEQ + 1) * NC_], w1s[:, j, m, :], blocks, start=m == 0, stop=m == 15)
                ins.then_inc(ch_mm, 1)
                if j == 0:
                    sb_sums(0)
            pe.wait_ge(ch_sb, 1)
            hd = hdn[:, :, :].rearrange("p j (s g n) -> p j s g n", g=2, n=NC_)
            for g in range(2):
                ins = mm(ps[g * HD:(g + 1) * HD, 7, 0:NSEQ * NC_], w2s[:, 0, :], hd[:, 0, :, g, :],
                         start=True, stop=True)
            ins.then_inc(ckv_mm, 1)
            pe.wait_ge(ch_sb, 2)
            for s in range(NSEQ):
                for g in range(2):
                    c = (s % 4) * 128 + g * HD
                    ins = mm(ps[0:NC_, (0, 5, 6)[s // 4], c:c + HD], hd[:, 1, s, g, :], w2s[:, 1, :],
                             start=True, stop=True)
            ins.then_inc(ckv_mm, 1)
            for h in range(8):
                if h + 2 < 8:
                    sb_scores(h + 2)
                if h == 0:
                    pe.wait_ge(ckv_sb, 2)
                pe.wait_ge(kv_in[h // 2], 64)
                for p in range(2):
                    for hp in range(4):
                        c = p * 256 + hp * 64 + h * 8
                        ins = mm(ps[:, 0, c:c + 8], kvs[:, 2 * h + p, hp * 128:(hp + 1) * 128], qbd_a[:, hp, h, :],
                           start=True, stop=True)
                if h == 3:
                    ins.then_inc(ss_half, 1)
                if h + 1 < 8:
                    sb_sums(h + 1)
                sb_values(h)
            for hp in range(4):
                ins = mm(ps[0:32, 7, hp * 64:(hp + 1) * 64], zT[:, KA + hp, TP:T],
                         qbd_a[:, hp, :, :], start=True, stop=True)
            ins.then_inc(ss_qk, 1)

            pe.wait_ge(sb_o, 4)
            for h in range(8):
                r, g = h % 4, slice((h // 4) * HD, (h // 4 + 1) * HD)
                for tt in range(2):
                    c = (2 * r + tt) * 16
                    ins = mm(ps[:, 5 + h // 4, c:c + NC_], zT[g, QB + r, tt * 128:(tt + 1) * 128], ckT[g, 0, :],
                             start=True, stop=True)
            ins.then_inc(nc_qk, 1)

            NS = ((1, 2), (0, 7))

            def ns_scores(br, keys_of):
                for b in range(NB):
                    rows = slice(b % 4 * 32, b % 4 * 32 + 32)
                    out = ps[rows, NS[br][b // 4], 0:PAST]
                    mm(out, qbd_b[:, b, :], keys_of(b), start=True, stop=True)
                for w in range(2):
                    ins = mm(ps[:, NS[br][w], PAST:PAST + 32], qbd_b[:, 4 * w:4 * w + 4, :],
                             zT[:, (SK, WK)[br], TP:T], start=True, stop=True)
                return ins

            pe.wait_ge(sb_zc, 8)
            pe.wait_ge(nsk_in, 16 * PAGES)
            ns_scores(0, lambda b: nsk[:, 2 * b:2 * b + 2, 0:128])
            for b in range(NB):
                mm(ps[b % 4 * 32:b % 4 * 32 + 32, 1, 288 + b // 4 * 16:288 + b // 4 * 16 + NC_], qbd_b[:, b, :],
                   ckT[:, 1 + b, :], start=True, stop=True)
            for w in range(2):
                mm(ps[:, 1, 320 + w * 24:344 + w * 24], k("selrow", 32)[:, w * 128:(w + 1) * 128], gnat[0:32, 2, :],
                   start=True, stop=True)
            pe.wait_ge(ss_sp, 1)
            pe.wait_ge(sb_arg, 8)
            mm(ps[:, 3, 0:512], k("negtri"), sp_[:, 0:512], start=True, stop=False)
            mm(ps[:, 3, 0:256], k("negones"), sp_[:, 256:512], start=False, stop=False)
            mm(ps[:, 3, 0:256], k("negones", 32), sp_[0:32, 512:768], start=False, stop=False)
            mm(ps[:, 3, 256:512], k("negones", 32), sp_[0:32, 512:768], start=False, stop=True)
            mm(ps[0:32, 4, 0:256], k("negtri", 32)[:, 0:32], sp_[0:32, 512:768], start=True, stop=False)
            mm(ps[0:32, 4, 0:256], ident[0:32, 0:32], k("blockn", 32), start=False, stop=True).then_inc(ss_tri, 1)
            pe.wait_ge(win_in, 16)
            ns_scores(1, lambda b: winkv[:, b, 0:PAST]).then_inc(ns_qk, 1)

            pe.wait_ge(nc_p, 1)
            pe.wait_ge(ss_arg, 1)
            for h in range(8):
                for tt in range(2):
                    ins = nc.tensor.transpose(ps[0:NC_, 3 + h // 2, (h % 2) * 256 + tt * 128:(h % 2) * 256 + (tt + 1) * 128],
                                              sc_[:, 2 * h + tt, :], ident)
            ins.then_inc(nc_t, 1)

            HEADS = [(n // 2, n % 2) for n in range(8)]

            def np_scores(n):
                r, g = HEADS[n]
                half = slice(g * HD, (g + 1) * HD)
                if n >= 2:
                    pe.wait_ge(np_s, n - 1)
                elif n == 0:
                    pe.wait_ge(ns_s, 1)
                    pe.wait_ge(nc_pt, 1)
                for br, kt in enumerate((SK, WK)):
                    b = 2 * (n % 2) + br
                    mm(ps[:, b, 0:128], zT[half, QB + r, 0:128], zT[half, kt, 0:128], start=True, stop=True)
                    ins = mm(ps[:, b, 128:384], zT[half, QB + r, 128:256], zT[half, kt, 0:256],
                             start=True, stop=True)
                ins.then_inc(np_qk, 1)

            def np_turn(n):
                pe.wait_ge(np_p, n + 1)
                if n >= 1:
                    pe.wait_ge(np_pt, n)
                for br in range(2):
                    for c in range(3):
                        ins = nc.tensor.transpose(ps[:, 4 + br, c * 128:(c + 1) * 128],
                                                  pb[:, n % 2, br, c * 128:(c + 1) * 128], ident)
                ins.then_inc(np_t, 1)

            def np_values(n):
                r, g = HEADS[n]
                half = slice(g * HD, (g + 1) * HD)
                h = g * 4 + r
                b = 6
                pe.wait_ge(np_pt, n + 1)
                if g == 0 and r >= 1:
                    pe.wait_ge(np_o, r)
                mm(ps[half, b, 0:256], cv[:, 0, half], ptc[:, h, :], start=True, stop=False)
                for br in range(2):
                    mm(ps[half, b, 0:256], vnat[:, 0, 4 + br, half], ptb[:, n % 2, br, 0:256], start=False, stop=False)
                    ins = mm(ps[half, b, 128:256], vnat[:, 1, 4 + br, half], ptb[:, n % 2, br, 256:384],
                             start=False, stop=br == 1)
                ins.then_inc(np_pv, 1)

            def ss_values(n):
                hp = n // 2
                if n % 2 == 0:
                    mm(ps[:, 7, hp * 64:(hp + 1) * 64], vnat[0:32, 2, hp, :], wb[0:32, 512 + hp * 64:576 + hp * 64],
                       start=True, stop=False)
                for b in range(n % 2 * 4, n % 2 * 4 + 4):
                    for p in range(2):
                        c = hp * 64 + b * 8
                        ins = mm(ps[:, 7, c:c + 8], kvs[:, 2 * b + p, 512 + hp * 128:640 + hp * 128],
                                 wb[:, p * 256 + c:p * 256 + c + 8], start=False, stop=(b == NB - 1 and p == 1))
                if n == 7:
                    ins.then_inc(ss_pv, 1)

            pe.wait_ge(ss_w, 1)
            pe.wait_ge(ns_b, 1)
            ss_values(0)
            np_scores(0)
            np_scores(1)
            ss_values(1)
            for n in range(9):
                if n < 8:
                    np_turn(n)
                if n + 2 < 8:
                    np_scores(n + 2)
                if n + 2 < 8:
                    ss_values(n + 2)
                if n >= 1:
                    np_values(n - 1)

            pe.wait_ge(ns_p, 1)
            pe.wait_ge(np_s, 8)
            for w in range(2):
                for br in range(2):
                    for p in range(2):
                        nc.tensor.transpose(ps[:, 2 + br, p * 256 + w * 128:p * 256 + (w + 1) * 128],
                                            spb[:, br, w, p * 128:(p + 1) * 128], ident)
                    nc.tensor.transpose(ps[0:32, 0, br * 256 + w * 128:br * 256 + (w + 1) * 128],
                                        spb[:, br, w, 256:288], ident)
                ins = nc.tensor.transpose(ps[0:NC_, 1, w * 128:(w + 1) * 128], ssc[:, w, :], ident)
            ins.then_inc(ns_tb, 1)
            def rms_sums(m):
                for j in range(4):
                    pe.wait_ge(rm_sq, 4 * m + j + 1)
                    ins = mm(ps[:, (7, 3)[m], 0:T], k("ones"), sqb[:, 4 * m + j, :], start=j == 0, stop=j == 3)
                ins.then_inc(rm_mm, 1)

            rms_sums(0)
            pe.wait_ge(ns_pt, 1)
            pe.wait_ge(np_pt, 8)
            for w in range(2):
                for br in range(2):
                    mm(ps[:, 4 + w, 0:128], ptns[:, br, w * 128:(w + 1) * 128], vnat[0:32, 2, 4 + br, :],
                       start=br == 0, stop=False)
                for b in range(4 * w, 4 * w + 4):
                    out = ps[b % 4 * 32:b % 4 * 32 + 32, 4 + w, 0:128]
                    for p in range(2):
                        c = slice(p * 256 + b * 32, p * 256 + (b + 1) * 32)
                        mm(out, ptss[:, 0, c], nsk[:, 2 * b + p, 128:256], start=False, stop=False)
                        mm(out, ptss[:, 1, c], winkv[:, b, 256 + p * 128:384 + p * 128], start=False, stop=False)
                    ins = mm(out, ptcs[:, b * 32:(b + 1) * 32], cv[:, 1 + b, :], start=False, stop=True)
            ins.then_inc(ns_pv, 1)

            pe.wait_ge(ns_r, 1)
            for w in range(2):
                ins = nc.tensor.transpose(ps[:, 6, w * 128:(w + 1) * 128], os_[:, w, :], ident)
            ins.then_inc(ns_t, 1)
            def first_tiles(tiles, kds):
                for c in tiles:
                    project(place(AT_OUT + c), o_parts, 4 + c, halves(0, AT_OUT + c), kds=kds, x_low=o_l)

            rms_sums(1)
            pe.wait_ge(ns_o, 1)
            first_tiles(range(4), range(4))
            first_tiles(range(4), range(4, KD))
            for c in range(4, KD):
                pe.wait_ge(m_pre, c - 3)
                project(place(AT_OUT + c), o_parts, c, halves(0, AT_OUT + c))

            def norm_sums(n, x):
                for c in range(KD):
                    pe.wait_ge(m_pre, KD * n + c + 1)
                    ins = mm(ps[:, 0, 0:T], k("ones"), x[:, c, :], start=c == 0, stop=c == KD - 1)
                ins.then_inc(ln_mm, 1)
                for c in range(KD):
                    pe.wait_ge(ln_sq, KD * n + c + 1)
                    ins = mm(ps[:, 1, 0:T], k("ones"), sqb[:, c, :], start=c == 0, stop=c == KD - 1)
                ins.then_inc(ln_v, 1)

            norm_sums(0, xTs)

            def scores(slot, key_tile, copied, free):
                pe.wait_ge(q_sb, copied)
                pe.wait_ge(s_sb, free)
                for tt, (t0, n) in enumerate(TOK):
                    ins = mm(ps[0:n, 4 + slot, tt * 128:(tt + 1) * 128], qT[:, slot, t0:t0 + n], key_tile,
                             start=True, stop=True)
                ins.then_inc(s_mm, 1)

            for c in range(2):
                project((AT_Q + c) % 4, h_parts, c, halves(0, AT_Q + c), x_low=h_l)
            pe.wait_ge(keys_in, 16)
            with pe.Fori(0, 3) as i:
                for r in range(4):
                    scores(r, keys[:, bass.ds(4 * i + r, 1), :], 4 * i + (4 + r + 1), 4 * i + r + 1)
                    pe.wait_ge(q_sb, 4 * i + r + 3)
                    project((AT_Q + r + 2) % 4, h_parts, (r + 2) % 4, halves(i, AT_Q + r + 2))
            for c in (12, 13):
                scores(c % 4, keys[:, c, :], 4 + c + 1, c + 1)
                project((AT_Q + c + 2) % 4, h_parts, (c + 2) % 4, halves(0, AT_Q + c + 2))
            for r in range(4):
                if r < 2:
                    scores(2 + r, keys[:, 14 + r, :], 4 + 15 + r, 15 + r)
                pe.wait_ge(q_sb, 4 + 12 + r + 1)
                pe.wait_ge(u_act, r + 1)
                project((AT_U + r) % 4, h_parts, r, halves(0, AT_U + r))

            def experts_up(first, last):
                with pe.Fori(first, last) as i:
                    for r in range(4):
                        pe.wait_ge(u_act, 4 * i + r + 1)
                        project((AT_U + r) % 4, h_parts, r, halves(i, AT_U + r))

            experts_up(1, U_ALONE // 4 - 1)
            pe.wait_ge(rt_pick, 3)
            pe.wait_ge(s_sb, 4 + 16)
            for c in range(3):
                for tt, (t0, n) in enumerate(TOK):
                    ins = nc.tensor.transpose(ps[:, 4 + c, t0:t0 + n], pick[0:n, tt, c, :], ident[0:n, 0:n])
                ins.then_inc(rt_t, 1)
            experts_up(U_ALONE // 4 - 1, U_ALONE // 4)

            pe.wait_ge(rt_slot, 3)
            with pe.Fori(0, T // 32) as i:
                for r in range(4):
                    def pair(kd):
                        if kd % 2 == 0:
                            return
                        q = kd // 2
                        pe.wait_ge(one_ready, 16 * i + (4 * r + q + 1))
                        if q % 2 == 0:
                            pe.wait_ge(g_sb, 8 * i + (2 * r + q // 2 + 1))
                        for t in range(2):
                            c = (q % 2) * 256 + t * 128
                            ins = mm(ps[:, 4 + (2 * r + q // 2) % 4, c:c + 128], one_a[:, q % 2, t, :],
                                     one_b[q % 2][:, t, :], start=True, stop=True)
                        ins.then_inc(g_mm, 1)

                    pe.wait_ge(u_act, 4 * i + (U_ALONE + r + 1))
                    project(4 + r % 2, h_parts, r, halves(i, AT_U + U_ALONE + r), pair)

            pe.wait_ge(g_sb, 4 + T // 4)
            pe.wait_ge(u_act, 4 + NE)

            def experts_down(r, lows, ready, start, stop):
                pe.wait_ge(y_l, ready)
                for c in range(KD):
                    if c % 4 == 0:
                        pe.wait_ge(lows[0], lows[1 + c // 4])
                    ins = parts(4 + r % 2, y_hi[:, r % 2, :], y_lo[:, r % 2, :], c, c, start, stop)
                    if c % 4 == 3:
                        ins.then_inc(w_mm, 1)

            for r in range(4):
                experts_down(r, halves(0, AT_V + r), r + 1, r == 0, False)
            with pe.Fori(1, NE // 4 - 1) as i:
                for r in range(4):
                    experts_down(r, halves(i, AT_V + r), 4 * i + r + 1, False, False)
            for r in range(4):
                experts_down(r, halves(0, AT_V + NE - 4 + r), NE - 3 + r, False, r == 3)
            norm_sums(1, yT)

        @block.scalar
        def _(act):
            A = nc.scalar.activation
            done = [0]

            def link(ins):
                done[0] += 1
                ins.then_inc(act_link, 1)
                act.wait_ge(act_link, done[0])

            def high(ring_slot, arrived, slot, half=None, used=None):
                act.wait_ge(full[ring_slot], arrived)
                if used is not None:
                    act.wait_ge(w_mm, used)
                x = slice(0, D) if half is None else slice(half * D // 2, (half + 1) * D // 2)
                nc.scalar.copy(w_hi[slot][:, x], ring[:, ring_slot, x]).then_inc(part_hi, 2 if half is None else 1)

            def high_of(n, used=None):
                high(*filled(n), place(n), used=used)

            act.sem_inc(z_sb, 4)
            high_of(0)
            for c in range(KD):
                act.wait_ge(x_in[c // 2], 16)
                nc.scalar.copy(x_hi[:, c, :], xTs[:, c, :]).then_inc(x_h, 1)
            for n in range(1, 4):
                high_of(n)
            with act.Fori(0, 4) as i:
                for r in range(4):
                    act.wait_ge(w_mm, 8 * i + 2 * (r + 1))
                    nc.scalar.copy(zT[:, bass.ds(4 * i + r, 1), :], ps[:, r:r + 1, 0:T]).then_inc(z_sb, 1)
                    high(r, 16 * i + 32, r)
            for c in range(16, N_IN):
                act.wait_ge(w_mm, 2 * (c + 1))
                nc.scalar.copy(zT[:, c, :], ps[:, c % 4, 0:T]).then_inc(z_sb, 1)
                if c + 4 < N_IN:
                    high_of(c + 4)
            act.wait_ge(gate_mm, 1)
            nc.scalar.copy(zT[0:24, GT, :], ps[0:24, 2, 0:T]).then_inc(z_sb, 1)

            for tt, (t0, n) in enumerate(TOK):
                a, b = (4, 6, 0)[tt], (5, 7, 1)[tt]
                act.wait_ge(v_mm, tt + 1)
                nc.scalar.copy(vnat[0:n, tt, 0:4, :], ps[0:n, a, :].rearrange("p (a b) -> p a b", b=128))
                nc.scalar.copy(vnat[0:n, tt, 4:6, :], ps[0:n, b, 0:256].rearrange("p (a b) -> p a b", b=128))
                if tt == 2:
                    nc.scalar.copy(knat[:, :], ps[0:n, b, 256:384])
                A(gnat[0:n, tt, :], ps[0:n, b, 384:408], ACT.Exp, scale=-1.0).then_inc(v_sb, 1)

            def sb_soft(h):
                x = slice((h % 2) * 384, (h % 2) * 384 + 384)
                act.wait_ge(sb_qk, h + 1)
                if h >= 2:
                    act.wait_ge(sb_arg, h - 1)
                nc.scalar.copy(zb[:, x], ps[:, 1 + h % 2, 0:384])
                ins = A(lb[:, x], ps[:, 1 + h % 2, 0:384], ACT.Abs)
                ins.then_inc(sb_zc, 1)
                act.wait_ge(sb_zc, h + 1)
                link(A(lb[:, x], lb[:, x], ACT.Exp, scale=-1.0))
                A(lb[:, x], lb[:, x], ACT.Ln, bias=1.0).then_inc(sb_ln, 1)

            def sb_exp(h):
                x = slice((h % 2) * 384, (h % 2) * 384 + 384)
                act.wait_ge(sb_arg, h + 1)
                if h >= 2:
                    act.wait_ge(sb_pv, h - 1)
                A(wb[:, x], ab[:, x], ACT.Exp).then_inc(sb_w, 1)

            def hidden(j):
                act.wait_ge(ch_mm, j + 1)
                link(nc.scalar.copy(cb[:, j:j + 1], ps[:, 5 + j, 2 * NSEQ * NC_:2 * NSEQ * NC_ + 1]))
                A(hdn[:, j, :], ps[:, 5 + j, 0:2 * NSEQ * NC_], ACT.Gelu_apprx_tanh,
                  bias=cb[:, j:j + 1]).then_inc(ch_sb, 1)

            sb_soft(0)
            sb_soft(1)
            hidden(0)
            hidden(1)
            act.wait_ge(ckv_mm, 1)
            nc.scalar.copy(ckT[:, :, :], ps[:, 7, 0:NSEQ * NC_].rearrange("p (s n) -> p s n", n=NC_)).then_inc(ckv_sb, 1)
            act.wait_ge(ckv_mm, 2)
            for m in range(3):
                w = min(4, NSEQ - 4 * m)
                ins = nc.scalar.copy(cv[:, 4 * m:4 * m + w, :],
                                     ps[0:NC_, (0, 5, 6)[m], 0:w * 128].rearrange("p (s n) -> p s n", n=128))
            ins.then_inc(ckv_sb, 1)
            sb_exp(0)
            for h in range(1, 8):
                if h + 1 < 8:
                    sb_soft(h + 1)
                sb_exp(h)

            act.wait_ge(ss_qk, 1)
            act.wait_ge(sb_arg, 8)
            parts = ((slice(0, 128), slice(0, 512), 0), (slice(0, 32), slice(512, 768), 7))
            for rows, c, b in parts:
                w = c.stop - c.start
                nc.scalar.copy(zb[rows, c], ps[rows, b, 0:w])
                link(A(lb[rows, c], ps[rows, b, 0:w], ACT.Abs))
            for rows, c, b in parts:
                link(A(lb[rows, c], lb[rows, c], ACT.Exp, scale=-1.0))
            for rows, c, b in parts:
                ins = A(lb[rows, c], lb[rows, c], ACT.Ln, bias=1.0)
            ins.then_inc(ss_ln, 1)
            act.wait_ge(nc_s, 1)
            A(sc_[:, :, :], sc_[:, :, :], ACT.Exp).then_inc(nc_e, 1)
            act.wait_ge(ss_arg, 1)
            act.wait_ge(sb_pv, 8)
            for rows, c, b in parts:
                ins = A(wb[rows, c], ab[rows, c], ACT.Exp)
            ins.then_inc(ss_w, 1)
            act.wait_ge(nc_t, 1)
            for m in range(4):
                ins = nc.scalar.copy(ptc[:, 2 * m:2 * m + 2, :], ps[0:NC_, 3 + m, :].rearrange("p (h t) -> p h t", t=256))
            ins.then_inc(nc_pt, 1)

            def np_exp(n):
                act.wait_ge(np_s, n + 1)
                x = (n % 2) * 16
                for br in range(2):
                    for tt, c in enumerate((slice(0, 128), slice(128, 384))):
                        y = x + 2 * br + tt
                        ins = A(pb[:, n % 2, br, c], pb[:, n % 2, br, c], ACT.Exp, bias=sm[:, y:y + 1],
                                accum_out=sm[:, y + 4:y + 5])
                ins.then_inc(np_e, 1)

            np_exp(0)
            for n in range(8):
                if n + 1 < 8:
                    np_exp(n + 1)
                if n == 1:
                    act.wait_ge(ns_s, 1)
                    for w in range(2):
                        for br in range(2):
                            y = 64 + 2 * br + w
                            A(spb[:, br, w, :], spb[:, br, w, :], ACT.Exp, bias=sm[:, y:y + 1], accum_out=sm[:, y + 8:y + 9])
                        y = 64 + 4 + w
                        ins = A(ssc[:, w, :], ssc[:, w, :], ACT.Exp, bias=sm[:, y:y + 1], accum_out=sm[:, y + 8:y + 9])
                    ins.then_inc(ns_e, 1)
                act.wait_ge(np_t, n + 1)
                if n >= 2:
                    act.wait_ge(np_pv, n - 1)
                nc.scalar.copy(ptb[:, n % 2, :, :], ps[:, 4:6, 0:384]).then_inc(np_pt, 1)

            act.wait_ge(ss_o, 1)
            for c in range(4):
                A(sqb[:, c, :], oT[:, c, :], ACT.Square).then_inc(rm_sq, 1)
            act.wait_ge(ns_tb, 1)
            nc.scalar.copy(ptss[:, :, :], ps[:, 2:4, :])
            nc.scalar.copy(ptns[:, :, :], ps[0:32, 0, :].rearrange("p (a b) -> p a b", b=256))
            nc.scalar.copy(ptcs[:, :], ps[0:NC_, 1, 0:256]).then_inc(ns_pt, 1)
            high_of(AT_OUT)
            act.wait_ge(rm_sd, 1)
            A(srow[:, :], srow[:, :], ACT.Sqrt).then_inc(rm_sd, 1)
            high_of(AT_OUT + 1)
            act.wait_ge(ns_pv, 1)
            nc.scalar.copy(os_[:, :, :], ps[:, 4:6, 0:128]).then_inc(ns_r, 1)
            act.wait_ge(ns_o, 1)
            act.wait_ge(np_o, 4)
            for c in range(4, KD):
                A(sqb[:, c, :], oT[:, c, :], ACT.Square).then_inc(rm_sq, 1)
            for c in range(4):
                act.wait_ge(rm_on, c + 1)
                nc.scalar.copy(o_hi[:, c, :], oT[:, c, :]).then_inc(o_h, 1)
            high_of(AT_OUT + 2)
            act.wait_ge(rm_sd, 3)
            A(rrow[:, :], rrow[:, :], ACT.Sqrt).then_inc(rm_sd, 1)
            high_of(AT_OUT + 3)
            for c in range(4, KD):
                act.wait_ge(rm_on, c + 1)
                nc.scalar.copy(o_hi[:, c, :], oT[:, c, :]).then_inc(o_h, 1)
            for n in range(AT_OUT, AT_Q):
                high_of(n + 4, 2 * AT_OUT + 4 + n - AT_OUT + 1 if n < AT_OUT + 4 else 2 * (n + 1))

            def norm_act(n, x, b, out, done):
                for c in range(KD):
                    act.wait_ge(ln_c, KD * n + c + 1)
                    A(sqb[:, c, :], x[:, c, :], ACT.Square).then_inc(ln_sq, 1)
                act.wait_ge(ln_sd, 2 * n + 1)
                A(srow[:, :], srow[:, :], ACT.Sqrt).then_inc(ln_sd, 1)
                for c in range(KD):
                    act.wait_ge(ln_g, KD * n + c + 1)
                    A(out[:, c, :], x[:, c, :], ACT.Identity, bias=vec[:, b, c:c + 1]).then_inc(done, 1)

            act.wait_ge(out_win, 48)
            act.wait_ge(out_kv, 32)
            norm_act(0, xTs, 2, h_hi, h_h)

            act.sem_inc(q_sb, 4)
            act.sem_inc(s_sb, 4)

            def scores_out(c):
                act.wait_ge(s_mm, c + 1)
                nc.scalar.copy(sT[:, 0:2, c, :], ps[:, 4 + c % 4, 0:256].rearrange("p (t k) -> p t k", k=128))
                nc.scalar.copy(sT[0:32, 2, c, :], ps[0:32, 4 + c % 4, 256:384]).then_inc(s_sb, 1)

            for m in range(N_Q):
                act.wait_ge(w_mm, 2 * (AT_Q + m + 1))
                if m >= 4:
                    act.wait_ge(s_mm, m - 3)
                nc.scalar.copy(qT[:, m % 4, :], ps[:, m % 4, 0:T]).then_inc(q_sb, 1)
                high_of(AT_Q + m + 4)
                if m >= 2:
                    scores_out(m - 2)

            act.sem_inc(u_act, 4)
            act.sem_inc(g_sb, 4)

            def gelu(i, r, first=0):
                act.wait_ge(w_mm, 8 * i + 2 * (AT_U + first + r + 1))
                if first + r >= 2:
                    act.wait_ge(spill[r % 2], 32 * i + 16 * ((first + r) // 2))
                A(u_out[:, r % 2, :], ps[:, r, 0:T], ACT.Gelu_apprx_tanh).then_inc(u_act, 1)

            def gelu_then_high(i, r, first=0):
                gelu(i, r, first)
                n = AT_U + first + r + 4
                slot, value = filled(n)
                high(slot, 16 * i + value, place(n))

            for r in range(4):
                if r < 2:
                    scores_out(14 + r)
                gelu_then_high(0, r)
            with act.Fori(0, U_ALONE // 4 - 3) as i:
                for r in range(4):
                    gelu_then_high(i, r, 4)
            act.wait_ge(rt_exp_in, 3)
            for tt, (t0, n) in enumerate(TOK):
                A(pick[0:n, tt, 2, :], pick[0:n, tt, 2, :], ACT.Exp).then_inc(rt_exp, 1)
            for r in range(8):
                if r == 4:
                    for c in range(3):
                        act.wait_ge(rt_t, c + 1)
                        nc.scalar.copy(slotT[:, c, :], ps[:, 4 + c, 0:T]).then_inc(rt_slot, 1)
                if r < 6:
                    gelu_then_high(0, r % 4, U_ALONE - 8 + r // 4 * 4)
                else:
                    gelu(0, r - 4, U_ALONE - 4)

            with act.Fori(0, T // 32) as i:
                for r in range(4):
                    slot, value = filled(AT_U + U_ALONE + r + 2)
                    for half in range(2):
                        if half:
                            gelu(i, r, U_ALONE)
                        high(slot, 16 * i + value, 4 + r % 2, half, 8 * i + (2 * (AT_U + U_ALONE + r) + half + 1))
                        act.wait_ge(g_mm, 16 * i + (2 + 4 * r + 2 * half + 2))
                        nc.scalar.copy(gates[:, :, bass.ds(32 * i + (8 * r + 4 * half), 4)],
                                       ps[:, 4 + (2 * r + half) % 4, :].rearrange("p (t j) -> p j t", j=128)
                                       ).then_inc(g_sb, 1)

            def high_y(r, ready, used=None):
                act.wait_ge(y_mul, ready)
                if used is not None:
                    act.wait_ge(w_mm, used)
                nc.scalar.copy(y_hi[:, r % 2, :], a_in[:, r % 4, :]).then_inc(y_h, 1)

            def highs_down(i, j):
                slot, value = filled(AT_V + j)
                used = 8 * i + 2 * (AT_V + j - 2)
                high(slot, 16 * i + value, 4 + j % 2, 0, used + 1)
                high_y(j, 4 * i + j + 1, used + 2)
                high(slot, 16 * i + value, 4 + j % 2, 1, used + 2)

            for j in range(2):
                act.wait_ge(spill[j], 16 * NE // 2)
                high_y(j, j + 1)
            for j in range(2, 4):
                highs_down(0, j)
            with act.Fori(0, NE // 4 - 1) as i:
                for j in range(4, 8):
                    highs_down(i, j)
            norm_act(1, yT, 4, sqb, ln_h)

        @block.vector
        def _(dve):
            V = nc.vector
            done = [0]

            def link(ins):
                done[0] += 1
                ins.then_inc(dve_link, 1)
                dve.wait_ge(dve_link, done[0])

            def low(highs, ring_slot, slot, half=None):
                dve.wait_ge(part_hi, highs)
                x = slice(0, D) if half is None else slice(half * D // 2, (half + 1) * D // 2)
                V.tensor_tensor(w_lo[slot][:, x], ring[:, ring_slot, x], w_hi[slot][:, x].bitcast(F32),
                                ALU.subtract).then_inc(part_lo[ring_slot], 2 if half is None else 1)

            lows, routed = [0], []

            def low_next():
                n = lows[0]
                if n == AT_U + U_ALONE - 4 and not routed:
                    return
                low(2 * (n + 1), n % 4, place(n))
                lows[0] = n + 1

            low_next()
            for c in range(KD):
                dve.wait_ge(x_h, c + 1)
                V.tensor_tensor(x_lo[:, c, :], xTs[:, c, :], x_hi[:, c, :].bitcast(F32), ALU.subtract).then_inc(x_l, 1)
            while lows[0] < N_IN:
                low_next()

            dve.wait_ge(z_sb, 4 + ZT)
            link(V.tensor_scalar(zT[:, 0:4, :], zT[:, 0:4, :], SCALE, None, ALU.mult))
            link(V.tensor_scalar(zT[:, QB:QB + 4, :], zT[:, QB:QB + 4, :], SCALE, None, ALU.mult))
            dve.wait_ge(zero_done, 1)
            for g in range(2):
                half = slice(g * HD, (g + 1) * HD)
                V.tensor_copy(qbd_a[half, :, :, g * 4:(g + 1) * 4],
                              zT[half, 0:4, TP:T].rearrange("p h (b t) -> p h b t", t=TS))
                ins = V.tensor_copy(qbd_b[half, :, g * 16:(g + 1) * 16].rearrange("p b (r t) -> p b r t", t=TS),
                                    zT[half, QB:QB + 4, TP:T].rearrange("p r (b t) -> p b r t", t=TS))
            ins.then_inc(q_ready, 1)
            for g in range(2):
                for par in range(2):
                    for j in range(2):
                        ins = V.tensor_copy(cmpT[par * HD:(par + 1) * HD, g, j, :],
                                            zT[g * HD:(g + 1) * HD, CK + j, par:TP:2])
            ins.then_inc(cmp_ready, 1)
            dve.wait_ge(v_sb, 3)
            for rows, tt in ((slice(0, 128), slice(0, 2)), (slice(0, 32), slice(2, 3))):
                link(V.tensor_scalar(gnat[rows, tt, :], gnat[rows, tt, :], 1.0, None, ALU.add))
                link(V.reciprocal(gnat[rows, tt, :], gnat[rows, tt, :]))

            def sb_plus(h):
                x = (h % 2) * 384
                dve.wait_ge(sb_ln, h + 1)
                if h >= 2:
                    dve.wait_ge(sb_tri, h - 1)
                link(V.scalar_tensor_tensor(sp_[:, x:x + 384], zb[:, x:x + 384], 0.0, lb[:, x:x + 384],
                                            ALU.max, ALU.add))
                V.tensor_tensor(sp_[:, x:x + 128], sp_[:, x:x + 128], k("keep"), ALU.mult)
                V.tensor_tensor(sp_[:, x + 256:x + 384], sp_[:, x + 256:x + 384], k("keep"),
                                ALU.mult).then_inc(sb_sp, 1)

            def sb_out(hp):
                dve.wait_ge(sb_pv, 2 * hp + 2)
                V.tensor_copy(oT[:, hp, 0:256], ps[:, 5 + hp % 2, 0:256]).then_inc(sb_o, 1)

            sb_plus(0)
            for h in range(8):
                if h + 1 < 8:
                    sb_plus(h + 1)
                x = (h % 2) * 384
                dve.wait_ge(sb_tri, h + 1)
                if h >= 2:
                    dve.wait_ge(sb_w, h - 1)
                V.tensor_tensor(ab[:, x:x + 384], zb[:, x:x + 384], ps[:, 3 + h % 2, 0:384],
                                ALU.add).then_inc(sb_arg, 1)
                if h in (3, 5, 7):
                    sb_out((h - 3) // 2)
            sb_out(3)

            dve.wait_ge(ss_ln, 1)
            dve.wait_ge(sb_tri, 8)
            V.scalar_tensor_tensor(sp_[:, 0:512], zb[:, 0:512], 0.0, lb[:, 0:512], ALU.max, ALU.add)
            link(V.scalar_tensor_tensor(sp_[0:32, 512:768], zb[0:32, 512:768], 0.0, lb[0:32, 512:768],
                                        ALU.max, ALU.add))
            V.tensor_tensor(sp_[0:32, 512:768], sp_[0:32, 512:768], k("keepn", 32), ALU.mult).then_inc(ss_sp, 1)
            dve.wait_ge(nc_qk, 1)
            for g in range(2):
                ins = V.tensor_tensor(sc_[:, 8 * g:8 * g + 8, :],
                                      ps[:, 5 + g, 0:128].rearrange("p (a b) -> p a b", b=16)[:, :, 0:NC_],
                                      k("cbias").rearrange("p (a b) -> p a b", b=NC_)[:, 8 * g:8 * g + 8, :], ALU.add)
            link(ins)
            mx, tot = sm[:, 96:112], sm[:, 112:128]
            wide = lambda a: a.unsqueeze(2).to_broadcast([128, 16, NC_])
            link(V.tensor_reduce(mx, sc_[:, :, :], AX, ALU.max))
            V.tensor_tensor(sc_[:, :, :], sc_[:, :, :], wide(mx), ALU.subtract).then_inc(nc_s, 1)
            dve.wait_ge(ss_tri, 1)
            dve.wait_ge(sb_w, 8)
            V.tensor_tensor(ab[:, 0:512], zb[:, 0:512], ps[:, 3, 0:512], ALU.add)
            V.tensor_tensor(ab[0:32, 512:768], zb[0:32, 512:768], ps[0:32, 4, 0:256], ALU.add).then_inc(ss_arg, 1)
            dve.wait_ge(nc_e, 1)
            v4 = sc_[:, :, :].rearrange("p (h w) n -> p h w n", w=2)
            cm = k("cmask").rearrange("p (w n) -> p w n", n=NC_).unsqueeze(1).to_broadcast([128, 8, 2, NC_])
            link(V.tensor_tensor(v4, v4, cm, ALU.mult))
            link(V.tensor_reduce(tot, sc_[:, :, :], AX, ALU.add))
            link(V.tensor_scalar(tot, tot, 1.0, None, ALU.max))
            link(V.reciprocal(tot, tot))
            gate = gnat[:, 0:2, :].rearrange("p w (h b) -> p h w b", b=3)
            link(V.tensor_tensor(mx.rearrange("p (h w) -> p h w", w=2), tot.rearrange("p (h w) -> p h w", w=2),
                                 gate[:, :, :, 0], ALU.mult))
            V.tensor_tensor(sc_[:, :, :], sc_[:, :, :], wide(mx), ALU.mult).then_inc(nc_p, 1)

            dve.wait_ge(ns_qk, 1)
            dve.wait_ge(out_kv, 32)
            tab = k("stab").rearrange("p (w s) -> p w s", w=2)
            V.tensor_tensor(spb[:, 0, :, :], ps[:, 1:3, 0:PAST + 32], tab, ALU.add)
            for w in range(2):
                ins = V.tensor_tensor(spb[:, 1, w, :], ps[:, (0, 7)[w], 0:PAST + 32], tab[:, w, :], ALU.add)
            ins.then_inc(ns_b, 1)
            V.tensor_tensor(ssc[:, :, :], ps[:, 1, 288:320].rearrange("p (w n) -> p w n", n=16)[:, :, 0:NC_],
                            k("sctab").unsqueeze(1).to_broadcast([128, 2, NC_]), ALU.add)
            g3 = gtmp[:, :, :].rearrange("p w (h b) -> p w h b", b=3)
            link(V.tensor_tensor(g3, ps[:, 1, 320:368].rearrange("p (w h b) -> p w h b", h=8, b=3),
                                 k("rowhead").unsqueeze(1).unsqueeze(3).to_broadcast([128, 2, 8, 3]), ALU.mult))
            V.tensor_reduce(sm[:, 64:68].rearrange("p (b w) -> p b w", w=2), spb[:, :, :, :], AX, ALU.max, negate=True)
            V.tensor_reduce(grow[:, :, :], gtmp[:, :, :].rearrange("p w (h b) -> p w b h", b=3), AX, ALU.add)
            link(V.tensor_reduce(sm[:, 68:70], ssc[:, :, :], AX, ALU.max, negate=True))
            V.tensor_copy(sm[:, 88:90], sm[:, 68:70]).then_inc(ns_s, 1)
            HEADS = [(n // 2, n % 2) for n in range(8)]

            def np_bias(n):
                r, g = HEADS[n]
                dve.wait_ge(np_qk, n + 1)
                if n >= 2:
                    dve.wait_ge(np_t, n - 1)
                else:
                    dve.wait_ge(ckv_sb, 2)
                b = 2 * (n % 2)
                x = (n % 2) * 16
                link(V.scalar_tensor_tensor(pb[:, n % 2, :, :], k("dist").unsqueeze(1).to_broadcast([128, 2, 384]),
                                            SLOPES[g * 4 + r], ps[:, b:b + 2, 0:384], ALU.mult, ALU.add))
                m = sm[:, x:x + 4].rearrange("p (b w) -> p b w", w=2)
                V.tensor_reduce(m[:, :, 0:1], pb[:, n % 2, :, 0:128], AX, ALU.max, negate=True)
                V.tensor_reduce(m[:, :, 1:2], pb[:, n % 2, :, 128:384], AX, ALU.max, negate=True).then_inc(np_s, 1)

            def np_scale(n):
                r, g = HEADS[n]
                h = g * 4 + r
                x = (n % 2) * 16
                dve.wait_ge(np_e, n + 1)
                link(V.reciprocal(sm[:, x + 4:x + 8], sm[:, x + 4:x + 8]))
                link(V.tensor_tensor(sm[:, x + 8:x + 12].rearrange("p (b w) -> p b w", w=2),
                                     sm[:, x + 4:x + 8].rearrange("p (b w) -> p b w", w=2),
                                     gnat[:, 0:2, 3 * h + 1:3 * h + 3].rearrange("p w b -> p b w"), ALU.mult))
                for br in range(2):
                    for tt, c in enumerate((slice(0, 128), slice(128, 384))):
                        y = x + 8 + 2 * br + tt
                        ins = V.tensor_scalar(pb[:, n % 2, br, c], pb[:, n % 2, br, c], sm[:, y:y + 1], None, ALU.mult)
                ins.then_inc(np_p, 1)

            def np_out(r):
                dve.wait_ge(np_pv, 2 * r + 2)
                V.tensor_copy(oT[:, 4 + r, 0:256], ps[:, 6, 0:256]).then_inc(np_o, 1)

            def ns_scale():
                dve.wait_ge(ns_e, 1)
                link(V.reciprocal(sm[:, 72:78], sm[:, 72:78]))
                V.tensor_tensor(sm[:, 80:84].rearrange("p (b w) -> p b w", w=2),
                                sm[:, 72:76].rearrange("p (b w) -> p b w", w=2),
                                grow[:, :, 1:3].rearrange("p w b -> p b w"), ALU.mult)
                link(V.tensor_tensor(sm[:, 84:86], sm[:, 76:78], grow[:, :, 0], ALU.mult))
                for w in range(2):
                    for br in range(2):
                        y = 80 + 2 * br + w
                        V.tensor_scalar(spb[:, br, w, :], spb[:, br, w, :], sm[:, y:y + 1], None, ALU.mult)
                    ins = V.tensor_scalar(ssc[:, w, :], ssc[:, w, :], sm[:, 84 + w:85 + w], None, ALU.mult)
                ins.then_inc(ns_p, 1)

            np_bias(0)
            for n in range(8):
                if n + 1 < 8:
                    np_bias(n + 1)
                np_scale(n)
                if n == 1:
                    ns_scale()
                if n in (3, 5, 7):
                    np_out((n - 3) // 2)
            np_out(3)

            dve.wait_ge(ss_pv, 1)
            for g in range(2):
                half = slice(g * HD, (g + 1) * HD)
                ins = V.tensor_copy(oT[half, 0:4, TP:T].rearrange("p h (b t) -> p h b t", t=TS),
                                    ps[half, 7, 0:256].rearrange("p (h b g t) -> p h b g t", h=4, b=NB, g=2)[:, :, :, g, :])
            ins.then_inc(ss_o, 1)
            def scaled(c):
                V.scalar_tensor_tensor(oT[:, c, :], oT[:, c, :], vec[:, 0, c:c + 1], (srow, rrow)[c // 4][:, :],
                                       ALU.mult, ALU.mult).then_inc(rm_on, 1)

            def o_low(c):
                dve.wait_ge(o_h, c + 1)
                V.tensor_tensor(o_lo[:, c, :], oT[:, c, :], o_hi[:, c, :].bitcast(F32), ALU.subtract).then_inc(o_l, 1)

            dve.wait_ge(small_in, 16 * 4)
            dve.wait_ge(rm_mm, 1)
            V.tensor_scalar(srow[:, :], ps[:, 7, 0:T], 1.0 / 512, EPS, ALU.mult, ALU.add).then_inc(rm_sd, 1)
            dve.wait_ge(rm_sd, 2)
            link(V.reciprocal(srow[:, :], srow[:, :]))
            dve.wait_ge(ns_t, 1)
            for g in range(2):
                half = slice(g * HD, (g + 1) * HD)
                ins = V.tensor_copy(oT[half, 4:8, TP:T].rearrange("p r (b t) -> p b r t", t=TS),
                                    ps[half, 6, 0:256].rearrange("p (b g r t) -> p b g r t", g=2, r=4, t=TS)[:, :, g, :, :])
            ins.then_inc(ns_o, 1)

            for c in range(4):
                scaled(c)
                if c >= 2:
                    o_low(c - 2)
            o_low(2)
            o_low(3)
            dve.wait_ge(rm_mm, 2)
            V.tensor_scalar(rrow[:, :], ps[:, 3, 0:T], 1.0 / 512, EPS, ALU.mult, ALU.add).then_inc(rm_sd, 1)
            dve.wait_ge(rm_sd, 4)
            link(V.reciprocal(rrow[:, :], rrow[:, :]))
            for c in range(4, KD):
                scaled(c)
                if c >= 6:
                    o_low(c - 2)
            o_low(6)
            o_low(7)

            def norm(n, x, g, after=lambda c: None):
                dve.wait_ge(ln_mm, n + 1)
                link(V.tensor_scalar(srow[:, :], ps[:, 0, 0:T], 1.0 / D, None, ALU.mult))
                for c in range(KD):
                    V.tensor_tensor(x[:, c, :], x[:, c, :], srow[:, :], ALU.subtract).then_inc(ln_c, 1)
                dve.wait_ge(ln_v, n + 1)
                V.tensor_scalar(srow[:, :], ps[:, 1, 0:T], 1.0 / D, EPS, ALU.mult, ALU.add).then_inc(ln_sd, 1)
                dve.wait_ge(ln_sd, 2 * n + 2)
                link(V.reciprocal(rrow[:, :], srow[:, :]))
                for c in range(KD):
                    V.scalar_tensor_tensor(x[:, c, :], x[:, c, :], vec[:, g, c:c + 1], rrow[:, :],
                                           ALU.mult, ALU.mult).then_inc(ln_g, 1)
                    after(c)

            lows[0] += 4
            for c in range(KD):
                dve.wait_ge(w_mm, 2 * AT_OUT + (4 + c + 1 if c < 4 else 2 * (c + 1)))
                V.scalar_tensor_tensor(xTs[:, c, :], xTs[:, c, :], ALPHA, ps[:, 4 + c % 4, 0:T],
                                       ALU.mult, ALU.add).then_inc(m_pre, 1)
                if c < KD - 1:
                    low_next()
            def h_low(c):
                dve.wait_ge(h_h, c + 1)
                V.scalar_tensor_tensor(h_lo[:, c, :], xTs[:, c, :], vec[:, 2, c:c + 1], h_hi[:, c, :].bitcast(F32),
                                       ALU.add, ALU.subtract).then_inc(h_l, 1)

            norm(0, xTs, 1, lambda c: h_low(c - 2) if c >= 2 else None)
            h_low(KD - 2)
            h_low(KD - 1)
            while lows[0] < AT_Q + 4:
                low_next()

            owed = [1.0]

            def pace(work, per_tile=PACE):
                owed[0] += work / per_tile
                while owed[0] >= 1:
                    low_next()
                    owed[0] -= 1

            link(V.tensor_copy(rowlen[:, :], k("rowlen")))
            def top16(lists):
                marks = [0] * len(lists)

                def turn(step, marked=True, after=True):
                    for q, (values, out, where) in enumerate(lists):
                        if after and marks[q]:
                            dve.wait_ge(dve_link, marks[q])
                        ins = step(values, out, where)
                        if marked:
                            done[0] += 1
                            marks[q] = done[0]
                            ins.then_inc(dve_link, 1)

                turn(lambda v, o, w: V.max(o[:, 0:8], v))
                turn(lambda v, o, w: V.max_index(w[:, 0:8], o[:, 0:8], v), marked=False)
                turn(lambda v, o, w: V.match_replace(v, o[:, 0:8], v, -3.0e38))
                turn(lambda v, o, w: V.max(o[:, 8:16], v))
                turn(lambda v, o, w: V.max_index(w[:, 8:16], o[:, 8:16], v))
                dve.wait_ge(dve_link, done[0])

            pace(0)
            for c in range(16):
                dve.wait_ge(s_sb, 4 + c + 1)
                top16([(sT[0:n, tt, c, :], val[0:n, tt, c // 2, c % 2, :], idx[0:n, tt, c // 2, c % 2, :])
                       for tt, (t0, n) in enumerate(TOK)])
                pace(3, PACE_Q if c < 10 else PACE)
            for tt, (t0, n) in enumerate(TOK):
                R = slice(0, n)
                link(V.tensor_copy(idf[R, :, :, :], idx[R, tt, :, :, :]))
                s1, s2 = val[R, tt, :, 0, :], val[R, tt, :, 1, :]
                for i in range(5):
                    w = ROWLEN[i]
                    V.tensor_tensor(cand[R, :, ROWOFF[i]:ROWOFF[i] + w], s2[:, :, 0:w],
                                    s1[:, :, i:i + 1].to_broadcast([n, 8, w]), ALU.add)
                V.tensor_tensor(cand[R, :, ROWOFF[5]:ROWOFF[8]].rearrange("p h (i j) -> p h i j", j=2),
                                s1[:, :, 5:8].unsqueeze(3).to_broadcast([n, 8, 3, 2]),
                                s2[:, :, 0:2].unsqueeze(2).to_broadcast([n, 8, 3, 2]), ALU.add)
                link(V.tensor_tensor(cand[R, :, ROWOFF[8]:NCAND], s1[:, :, 8:16],
                                     s2[:, :, 0:1].to_broadcast([n, 8, 8]), ALU.add))
                for h in range(0, 8, 2):
                    top16([(cand[R, g, :], topv[R, g, :], pos[R, g, :]) for g in (h, h + 1)])
                    pace(2)
                V.tensor_tensor(pick[R, tt, 2, :].rearrange("p (h k) -> p h k", k=TOPK), topv[R, :, :],
                                topv[R, :, 0:1].to_broadcast([n, 8, TOPK]), ALU.subtract).then_inc(rt_exp_in, 1)
                link(V.tensor_copy(posf[R, :], pos[R, :, :].rearrange("p h k -> p (h k)")))
                V.tensor_copy(dlt[R, :, :, 0:1], idf[R, :, :, 0:1])
                link(V.tensor_tensor(dlt[R, :, :, 1:TOPK], idf[R, :, :, 1:TOPK], idf[R, :, :, 0:TOPK - 1], ALU.subtract))
                many = [n, 8 * TOPK, TOPK]
                link(V.tensor_tensor(step[R, :, :], posf[R, :].unsqueeze(2).to_broadcast(many),
                                     k("rowoff")[R, :].unsqueeze(1).to_broadcast(many), ALU.is_ge))
                pace(3)

                def pick_from(out, steps):
                    link(V.tensor_tensor(prod[R, :, :].rearrange("p (h k) i -> p h k i", k=TOPK),
                                         step[R, :, :].rearrange("p (h k) i -> p h k i", k=TOPK), steps, ALU.mult))
                    pace(1)
                    link(V.tensor_reduce(out, prod[R, :, :], AX, ALU.add))
                    pace(2)

                four = [n, 8, TOPK, TOPK]
                pick_from(pick[R, tt, 0, :], dlt[R, :, 0, :].unsqueeze(2).to_broadcast(four))
                pick_from(rowo[R, :], rowlen[R, :].unsqueeze(1).unsqueeze(1).to_broadcast(four))
                link(V.tensor_tensor(posf[R, :], posf[R, :], rowo[R, :], ALU.subtract))
                link(V.tensor_tensor(step[R, :, :], posf[R, :].unsqueeze(2).to_broadcast(many),
                                     k("iota")[R, 0:TOPK].unsqueeze(1).to_broadcast(many), ALU.is_ge))
                pace(2)
                pick_from(pick[R, tt, 1, :], dlt[R, :, 1, :].unsqueeze(2).to_broadcast(four))
            while lows[0] < AT_U + U_ALONE - 4:
                low_next()
            routed.append(True)
            for tt, (t0, n) in enumerate(TOK):
                R = slice(0, n)
                e = pick[R, tt, 2, :].rearrange("p (h k) -> p h k", k=TOPK)
                dve.wait_ge(rt_exp, tt + 1)
                link(V.tensor_reduce(ssum[R, tt, :], e, AX, ALU.add))
                link(V.reciprocal(ssum[R, tt, :], ssum[R, tt, :]))
                V.tensor_tensor(e, e, ssum[R, tt, :].unsqueeze(2).to_broadcast([n, 8, TOPK]), ALU.mult).then_inc(rt_pick, 1)
            while lows[0] < AT_U + U_ALONE:
                low_next()

            def low_half(i, n, half):
                low(8 * i + (2 * n + half + 1), n % 4, 4 + n % 2, half)

            m0 = AT_U + U_ALONE
            low_half(0, m0, 0)
            low_half(0, m0, 1)
            low_half(0, m0 + 1, 0)
            dve.wait_ge(rt_slot, 3)
            with dve.Fori(0, T // 32) as i:
                for r in range(4):
                    for q in range(4):
                        t0 = 8 * r + 2 * q
                        dve.wait_ge(g_mm, 16 * i + (4 * r + q + 1))
                        for t in range(2):
                            at_t = bass.ds(32 * i + (t0 + t), 1)
                            V.tensor_scalar(one_a[:, q % 2, t, :], k("iota"), slotT[:, 0, at_t], slotT[:, 2, at_t],
                                            ALU.is_equal, ALU.mult)
                        V.tensor_tensor(one_b[q % 2][:, :, :], k("iota").unsqueeze(1).to_broadcast([128, 2, 128]),
                                        slotT[:, 1, bass.ds(32 * i + t0, 2)].unsqueeze(2).to_broadcast([128, 2, 128]),
                                        ALU.is_equal).then_inc(one_ready, 1)
                        if q == 1:
                            low_half(i, m0 + r + 1, 1)
                        if q == 3:
                            low_half(i, m0 + r + 2, 0)

            def weigh(r, j, arrived):
                dve.wait_ge(a_full[r], arrived)
                V.tensor_tensor(a_in[:, r, :].unsqueeze(1), a_in[:, r, :].unsqueeze(1), gates[:, j, :],
                                ALU.mult).then_inc(y_mul, 1)

            def low_y(r, ready):
                dve.wait_ge(y_h, ready)
                V.tensor_tensor(y_lo[:, r % 2, :], a_in[:, r % 4, :], y_hi[:, r % 2, :].bitcast(F32),
                                ALU.subtract).then_inc(y_l, 1)

            def lows_down(i, j, weigh_next=True):
                low_half(i, AT_V + j, 0)
                if weigh_next:
                    weigh((j + 1) % 4, bass.ds(4 * i + j + 1, 1), 16 * i + 16 * ((j + 1) // 4 + 1))
                low_y(j, 4 * i + j + 1)
                low_half(i, AT_V + j, 1)

            dve.wait_ge(g_sb, 4 + T // 4)
            for j in range(2):
                weigh(j, slice(j, j + 1), 16)
            low_half(0, AT_V + 1, 1)
            low_y(0, 1)
            low_y(1, 2)
            weigh(2, slice(2, 3), 16)
            lows_down(0, 2)
            lows_down(0, 3)
            with dve.Fori(1, NE // 4 - 1) as i:
                for r in range(4):
                    lows_down(i, r)
            for r in range(4):
                lows_down(0, NE - 4 + r, r < 3)
                c = slice(2 * r, 2 * r + 2)
                V.tensor_tensor(yT[:, c, :], h_hi[:, c, :].bitcast(F32), h_lo[:, c, :].bitcast(F32), ALU.add
                                ).then_inc(h_sum, 1)

            dve.wait_ge(h_sum, 4)
            for c in range(KD):
                dve.wait_ge(w_mm, 2 * (AT_V + NE) - 1 + c // 4)
                V.scalar_tensor_tensor(yT[:, c, :], yT[:, c, :], ALPHA, ps[:, c, 0:T],
                                       ALU.mult, ALU.add).then_inc(m_pre, 1)
            norm(1, yT, 3)




def lay_out(x_prompt, x_sample, cache_sb_kv, cache_nsa_kv, cache_win_kv, page_table, w_in, cmp_pe, cmp_w1,
            cmp_w2, mix_norm_g, w_out, ln1_g, ln1_b, peer_w_q, peer_sub_keys, peer_u, peer_v, ln2_g, ln2_b):
    f = np.ascontiguousarray
    np_ = lambda a: np.asarray(a)
    x = np.concatenate([np_(x_prompt).reshape(-1, D), np_(x_sample).reshape(-1, D)])
    feat = lambda a: a.reshape(a.shape[0], KD, 128).transpose(2, 1, 0)

    def tiles(w):
        return w.reshape(KD, 128, -1, 128).transpose(2, 1, 0, 3).reshape(w.shape[1] // 128, 128, D)

    swap = lambda a, ax: a.reshape(a.shape[:ax] + (2, 4, HD) + a.shape[ax + 1:]).swapaxes(ax, ax + 1).reshape(a.shape)
    w = np_(w_in)[0]
    qb, kb = QB * 128, CK * 128
    w = np.concatenate([w[:, :qb], swap(w[:, qb:kb], 1), w[:, kb:]], 1)
    wo = np_(w_out)[0]
    wo = np.concatenate([wo[:512], swap(wo[512:], 0)])
    mg = np_(mix_norm_g)[0]
    mg = np.concatenate([mg[:512], swap(mg[512:], 0)])
    vecs = np.stack([a.reshape(KD, 128).T for a in (mg, np_(ln1_g)[0], np_(ln1_b)[0], np_(ln2_g)[0], np_(ln2_b)[0])], 1)
    sb = np_(cache_sb_kv)[0]
    pages = sb.shape[0]
    kT = sb[:, :, 0].reshape(pages, 128, 4, 128).transpose(0, 3, 2, 1).reshape(pages, 128, 512)
    cache_sb = np.concatenate([kT, sb[:, :, 1].reshape(pages, 128, 512)], 2)
    ns = np_(cache_nsa_kv)[0]
    cache_nsa = np.concatenate([ns[:, :, 2].reshape(pages, 128, 128).transpose(0, 2, 1),
                                ns[:, :, 3].reshape(pages, 128, 128)], 2)
    cache_cmp = ns[:, :, 0:2].reshape(pages, 64, 2, 2, 2, HD).transpose(0, 2, 5, 4, 3, 1).reshape(pages, 128, 2, 2, 64)
    win = np_(cache_win_kv)[0].reshape(NB, PAST, 2, 128)
    win_kT = win[:, :, 0].transpose(2, 0, 1)
    win_v = win[:, :, 1].reshape(NB, 2, 128, 128).transpose(2, 0, 1, 3).reshape(128, NB, 256)
    return {
        "xT": f(feat(x)), "w_in": f(tiles(w[:, :GT * 128])),
        "w_gate": f(w[:, GT * 128:].reshape(KD, 128, 24).transpose(1, 0, 2)),
        "w_out": f(tiles(wo)), "w_q": f(tiles(np_(peer_w_q)[0])),
        "keysT": f(np_(peer_sub_keys)[0].reshape(16, 128, 128).transpose(2, 0, 1)),
        "uT": f(np_(peer_u)[0].reshape(128, 128, KD, 128).transpose(1, 3, 2, 0).reshape(128, 128, D)),
        "v": f(np_(peer_v)[0].reshape(128, 128, D).transpose(1, 0, 2)),
        "w1": f(np_(cmp_w1)[0].reshape(2, 16, 128, 128).transpose(2, 0, 1, 3)),
        "pe_cmp": f(np_(cmp_pe)[0].reshape(2, 16, 128).transpose(2, 0, 1)),
        "w2": f(np_(cmp_w2)[0].transpose(1, 0, 2)),
        "vecs": f(vecs), "cache_sb": f(cache_sb), "cache_nsa": f(cache_nsa), "cache_cmp": f(cache_cmp),
        "win_kv": f(np.concatenate([win_kT, win_v], 2)),
        "win_rows": f(win.reshape(NB, PAST, 256)), "page_table": f(np_(page_table).reshape(1, PAGES)),
        "consts": CONST_ARRAY,
    }


OUTPUTS = [((128, KD, T), "float32"), ((128, 14, T), "float32"), ((NB, PAST, 256), "float32")]


def take_out(y, kv, win):
    rows = lambda a: a.transpose(2, 1, 0).reshape(T, -1)
    y, kv = rows(y), rows(kv)
    sb, nsa, wn = kv[:, :1024], kv[:, 1024:1536], kv[:, 1536:]
    c = np.ascontiguousarray
    return (c(y[:TP].reshape(1, TP, D)), c(y[TP:].reshape(NB, TS, D)),
            c(sb[:TP].reshape(1, 1, TP, 2, 8, HD)), c(nsa[:TP].reshape(1, 1, TP, 4, 2, HD)),
            c(wn[:TP].reshape(1, 1, TP, 2, 2, HD)),
            c(sb[TP:].reshape(1, NB, TS, 2, 8, HD)), c(nsa[TP:].reshape(1, NB, TS, 4, 2, HD)),
            c(win.reshape(1, NB, PAST, 2, 2, HD)))


def kernel(**inputs):
    import concourse.bacc as bacc
    from concourse.bass_utils import run_bass_kernel_spmd

    arrays = lay_out(**inputs)
    nc = bacc.Bacc("TRN2", target_bir_lowering=False, num_devices=1)
    args = [nc.dram_tensor(f"in_{n}_dram", a.shape, mybir.dt.from_np(a.dtype), kind="ExternalInput").ap()
            for n, a in arrays.items()]
    outs = [nc.dram_tensor(f"out_{i}_dram", s, mybir.dt.from_np(np.dtype(d)), kind="ExternalOutput").ap()
            for i, (s, d) in enumerate(OUTPUTS)]
    trunk(nc, *args, *outs)
    got = run_bass_kernel_spmd(nc, [{f"in_{n}_dram": a for n, a in arrays.items()}], core_ids=[0]).results[0]
    return take_out(*(np.asarray(got[f"out_{i}_dram"]) for i in range(len(OUTPUTS))))
```
